# Optimizing a Trainium2 kernel written in Bass

```python
import jax, jax.numpy as jnp
from jax import lax
import numpy as np

D_MODEL = 1024
BATCH = 1
SEQ = 256
DEPTH = 2

A_HEADS = 4
A_HEAD_DIM = 128
D_A = A_HEADS * A_HEAD_DIM
CHUNK = 128
B_GROUPS = 4
D_B = D_MODEL - D_A
B_CONV = 3
D_IN_AB = 2 * D_A + 3 * D_B
D_RNN = D_MODEL
LRU_HEADS = 8
LRU_HEAD_DIM = D_RNN // LRU_HEADS
C_CONV = 4
LRU_C = 8.0
N_GROUPS = 4
EXPERTS_PER_GROUP = 8
N_EXPERTS = N_GROUPS * EXPERTS_PER_GROUP
TOP_K = 2
D_EXPERT = 512
MOE_BLOCK = 128
N_EVEN = (DEPTH + 1) // 2
N_ODD = DEPTH // 2
EPS = 1e-6


def rms_norm(x, g):
    xf = x.astype(jnp.float32)
    y = xf * lax.rsqrt(jnp.mean(jnp.square(xf), axis=-1, keepdims=True) + EPS)
    return y.astype(x.dtype) * g

def layer_norm(x, g):
    xf = x.astype(jnp.float32)
    mu = jnp.mean(xf, axis=-1, keepdims=True)
    var = jnp.mean(jnp.square(xf - mu), axis=-1, keepdims=True)
    return ((xf - mu) * lax.rsqrt(var + EPS)).astype(x.dtype) * g

def causal_conv(x, w):
    k_width = w.shape[0]
    t_len = x.shape[1]
    xp = jnp.pad(x, ((0, 0), (k_width - 1, 0), (0, 0)))
    y = xp[:, 0:t_len] * w[0]
    for k in range(1, k_width):
        y = y + xp[:, k:k + t_len] * w[k]
    return y

def mixer_ab(h, w_in, a_ln_g, a_ws, a_ws_b, b_conv_w, w_out):
    bsz, t_len, _ = h.shape
    z = h @ w_in
    u, v, gate_b, gate_c, xb = jnp.split(
        z, [D_A, 2 * D_A, 2 * D_A + D_B, 2 * D_A + 2 * D_B], axis=-1)
    u = jax.nn.gelu(u)
    v = layer_norm(jax.nn.gelu(v), a_ln_g)
    vc = v.reshape(bsz, t_len // CHUNK, CHUNK, A_HEADS, A_HEAD_DIM)
    causal = jnp.tril(jnp.ones((CHUNK, CHUNK), dtype=bool))
    ws = jnp.where(causal, a_ws, 0.0)
    mixed = jnp.einsum('hts,bcshd->bcthd', ws, vc) + a_ws_b.T[:, :, None]
    y_a = u * mixed.reshape(bsz, t_len, D_A)
    y_b = gate_b * causal_conv(gate_c * xb, b_conv_w)
    return jnp.concatenate([y_a, y_b], axis=-1) @ w_out

def mixer_rglru(h, w_in, conv_w, conv_b, w_a, b_a, w_x, b_x, lam, w_out):
    bsz, t_len, _ = h.shape
    gate, xr = jnp.split(h @ w_in, [D_RNN], axis=-1)
    gate = jax.nn.gelu(gate)
    xr = causal_conv(xr, conv_w) + conv_b
    xh = xr.reshape(bsz, t_len, LRU_HEADS, LRU_HEAD_DIM)
    r = jax.nn.sigmoid(jnp.einsum('bthi,hij->bthj', xh, w_a).reshape(bsz, t_len, D_RNN) + b_a)
    i = jax.nn.sigmoid(jnp.einsum('bthi,hij->bthj', xh, w_x).reshape(bsz, t_len, D_RNN) + b_x)
    log_a = (LRU_C * r.astype(jnp.float32)) * jax.nn.log_sigmoid(lam.astype(jnp.float32))
    a = jnp.exp(log_a)
    b = jnp.sqrt(-jnp.expm1(2.0 * log_a)) * (i * xr).astype(jnp.float32)

    def combine(left, right):
        a_l, b_l = left
        a_r, b_r = right
        return a_l * a_r, a_r * b_l + b_r

    _, hseq = lax.associative_scan(combine, (a, b), axis=1)
    return (gate * hseq.astype(h.dtype)) @ w_out

def hierarchical_moe(h, w_rg, b_rg, w_re, b_re, w_gate, w_up, w_down):
    bsz, t_len, d = h.shape
    n_tok = bsz * t_len
    xt = h.reshape(n_tok, d)
    g_logits = (xt @ w_rg + b_rg).astype(jnp.float32)
    g_idx = jnp.argmax(g_logits, axis=-1)
    g_prob = jnp.take_along_axis(jax.nn.softmax(g_logits, axis=-1), g_idx[:, None], axis=-1)
    e_logits = (xt @ w_re + b_re).astype(jnp.float32).reshape(n_tok, N_GROUPS, EXPERTS_PER_GROUP)
    e_sel = jnp.take_along_axis(e_logits, g_idx[:, None, None], axis=1)[:, 0]
    top_val, top_idx = lax.top_k(e_sel, TOP_K)
    gates = g_prob * jax.nn.softmax(top_val, axis=-1)
    expert_ids = g_idx[:, None].astype(jnp.int32) * EXPERTS_PER_GROUP + top_idx.astype(jnp.int32)

    n_slots = n_tok * TOP_K
    n_blocks = -(-n_slots // MOE_BLOCK) + N_EXPERTS
    flat_e = expert_ids.reshape(n_slots)
    flat_tok = jnp.repeat(jnp.arange(n_tok, dtype=jnp.int32), TOP_K)
    flat_g = gates.reshape(n_slots)
    order = jnp.argsort(flat_e)
    sorted_e = flat_e[order]
    counts = jnp.bincount(flat_e, length=N_EXPERTS)
    starts = jnp.cumsum(counts) - counts
    padded = (counts + MOE_BLOCK - 1) // MOE_BLOCK * MOE_BLOCK
    pad_ends = jnp.cumsum(padded)
    pad_starts = pad_ends - padded
    dest = pad_starts[sorted_e] + (jnp.arange(n_slots, dtype=jnp.int32) - starts[sorted_e])
    slot_tok = jnp.full((n_blocks * MOE_BLOCK,), n_tok, jnp.int32).at[dest].set(flat_tok[order])
    slot_g = jnp.zeros((n_blocks * MOE_BLOCK,), jnp.float32).at[dest].set(flat_g[order])
    block_e = jnp.minimum(
        jnp.searchsorted(pad_ends, jnp.arange(n_blocks, dtype=jnp.int32) * MOE_BLOCK, side='right'),
        N_EXPERTS - 1)
    x_pad = jnp.concatenate([xt, jnp.zeros((1, d), xt.dtype)], axis=0)

    def expert_block(args):
        tok_b, g_b, e = args
        xb = x_pad[tok_b]
        hid = jax.nn.silu(xb @ w_gate[e]) * (xb @ w_up[e])
        return (hid @ w_down[e]) * g_b[:, None].astype(xb.dtype)

    y = lax.map(expert_block, (slot_tok.reshape(n_blocks, MOE_BLOCK),
                               slot_g.reshape(n_blocks, MOE_BLOCK), block_e))
    out = jax.ops.segment_sum(y.reshape(-1, d), slot_tok, num_segments=n_tok + 1)[:n_tok]
    return out.reshape(bsz, t_len, d)

def first_inputs(seed: int = 0) -> dict:
    key = jax.random.key(seed)
    ks = jax.random.split(key, 26)

    def nrm(k, shape, scale):
        return jax.random.normal(k, shape, jnp.float32) * scale

    a8 = jax.random.uniform(ks[17], (N_ODD, D_RNN), jnp.float32, 0.9, 0.999)
    a_base = a8 ** (1.0 / LRU_C)
    c_lambda = jnp.log(a_base) - jnp.log1p(-a_base)
    return {
        "x": nrm(ks[0], (BATCH, SEQ, D_MODEL), 1.0),
        "norm_mix_g": 1.0 + nrm(ks[1], (DEPTH, D_MODEL), 0.05),
        "norm_ffn_g": 1.0 + nrm(ks[2], (DEPTH, D_MODEL), 0.05),
        "norm_final_g": 1.0 + nrm(ks[3], (D_MODEL,), 0.05),
        "ab_w_in": nrm(ks[4], (N_EVEN, D_MODEL, D_IN_AB), D_MODEL ** -0.5),
        "a_ln_g": 1.0 + nrm(ks[5], (N_EVEN, D_A), 0.05),
        "a_ws": nrm(ks[6], (N_EVEN, A_HEADS, CHUNK, CHUNK), CHUNK ** -0.5),
        "a_ws_b": 1.0 + nrm(ks[7], (N_EVEN, A_HEADS, CHUNK), 0.1),
        "b_conv_w": nrm(ks[8], (N_EVEN, B_CONV, D_B), B_CONV ** -0.5),
        "ab_w_out": nrm(ks[9], (N_EVEN, D_A + D_B, D_MODEL), (D_A + D_B) ** -0.5),
        "c_w_in": nrm(ks[10], (N_ODD, D_MODEL, 2 * D_RNN), D_MODEL ** -0.5),
        "c_conv_w": nrm(ks[11], (N_ODD, C_CONV, D_RNN), C_CONV ** -0.5),
        "c_conv_b": nrm(ks[12], (N_ODD, D_RNN), 0.01),
        "c_w_a": nrm(ks[13], (N_ODD, LRU_HEADS, LRU_HEAD_DIM, LRU_HEAD_DIM), LRU_HEAD_DIM ** -0.5),
        "c_b_a": nrm(ks[14], (N_ODD, D_RNN), 0.01),
        "c_w_x": nrm(ks[15], (N_ODD, LRU_HEADS, LRU_HEAD_DIM, LRU_HEAD_DIM), LRU_HEAD_DIM ** -0.5),
        "c_b_x": nrm(ks[16], (N_ODD, D_RNN), 0.01),
        "c_lambda": c_lambda,
        "c_w_out": nrm(ks[18], (N_ODD, D_RNN, D_MODEL), D_RNN ** -0.5),
        "moe_w_rg": nrm(ks[19], (DEPTH, D_MODEL, N_GROUPS), D_MODEL ** -0.5),
        "moe_b_rg": nrm(ks[20], (DEPTH, N_GROUPS), 0.01),
        "moe_w_re": nrm(ks[21], (DEPTH, D_MODEL, N_EXPERTS), D_MODEL ** -0.5),
        "moe_b_re": nrm(ks[22], (DEPTH, N_EXPERTS), 0.01),
        "moe_w_gate": nrm(ks[23], (DEPTH, N_EXPERTS, D_MODEL, D_EXPERT), D_MODEL ** -0.5),
        "moe_w_up": nrm(ks[24], (DEPTH, N_EXPERTS, D_MODEL, D_EXPERT), D_MODEL ** -0.5),
        "moe_w_down": nrm(ks[25], (DEPTH, N_EXPERTS, D_EXPERT, D_MODEL), D_EXPERT ** -0.5),
    }

def first_block(x, norm_mix_g, norm_ffn_g, norm_final_g,
              ab_w_in, a_ln_g, a_ws, a_ws_b, b_conv_w, ab_w_out,
              c_w_in, c_conv_w, c_conv_b, c_w_a, c_b_a, c_w_x, c_b_x, c_lambda, c_w_out,
              moe_w_rg, moe_b_rg, moe_w_re, moe_b_re, moe_w_gate, moe_w_up, moe_w_down):
    for layer in range(DEPTH):
        idx = layer // 2
        h = rms_norm(x, norm_mix_g[layer])
        if layer % 2 == 0:
            x = x + mixer_ab(h, ab_w_in[idx], a_ln_g[idx], a_ws[idx], a_ws_b[idx],
                             b_conv_w[idx], ab_w_out[idx])
        else:
            x = x + mixer_rglru(h, c_w_in[idx], c_conv_w[idx], c_conv_b[idx], c_w_a[idx],
                                c_b_a[idx], c_w_x[idx], c_b_x[idx], c_lambda[idx], c_w_out[idx])
        h = rms_norm(x, norm_ffn_g[layer])
        x = x + hierarchical_moe(h, moe_w_rg[layer], moe_b_rg[layer], moe_w_re[layer],
                                 moe_b_re[layer], moe_w_gate[layer], moe_w_up[layer],
                                 moe_w_down[layer])
    return rms_norm(x, norm_final_g)


POOL_WINDOWS = (2, 4, 8, 16)
POOL_GROUPS = len(POOL_WINDOWS)
POOL_GROUP_DIM = D_MODEL // 8
POOL_DIM = POOL_GROUPS * POOL_GROUP_DIM
POOL_WMAX = max(POOL_WINDOWS)
HEAD_DIM = 64
N_Q_HEADS = D_MODEL // 128
N_KV_HEADS = 2
GQA_GROUP = N_Q_HEADS // N_KV_HEADS
ATTN_DIM = N_Q_HEADS * HEAD_DIM
KV_DIM = N_KV_HEADS * HEAD_DIM
WINDOW = 128
BLOCK = 128
ROPE_THETA = 500000.0
ROT_DIM = HEAD_DIM // 4
N_BRANCHES = 2
IN_DIM = POOL_DIM + ATTN_DIM + 2 * KV_DIM + N_BRANCHES * D_MODEL
D_FF = 2816


def rmsnorm(x, g):
    xf = x.astype(jnp.float32)
    y = xf * lax.rsqrt(jnp.mean(xf * xf, axis=-1, keepdims=True) + EPS)
    return (y * g.astype(jnp.float32)).astype(x.dtype)

def swiglu(h, w_gu, w_down):
    g, u = jnp.split(h @ w_gu, 2, axis=-1)
    return (jax.nn.silu(g) * u) @ w_down

def pool_mixer(u, w_grp, scale):
    B, S, _ = u.shape
    uf = u.astype(jnp.float32)
    c = jnp.cumsum(uf, axis=1)
    c_pad = jnp.pad(c, ((0, 0), (POOL_WMAX, 0), (0, 0)))
    t = jnp.arange(S)
    outs = []
    for g, w in enumerate(POOL_WINDOWS):
        lo, hi = g * POOL_GROUP_DIM, (g + 1) * POOL_GROUP_DIM
        win_sum = c[:, :, lo:hi] - c_pad[:, POOL_WMAX - w:POOL_WMAX - w + S, lo:hi]
        count = jnp.minimum(t + 1, w).astype(jnp.float32)[None, :, None]
        outs.append(win_sum / count - uf[:, :, lo:hi])
    d = jnp.stack(outs, axis=2).astype(u.dtype)
    y = jnp.einsum('bsgc,gcd->bsgd', d, w_grp).reshape(B, S, POOL_DIM)
    return y * scale

def partial_rope(x, cos, sin):
    half = ROT_DIM // 2
    x1 = x[..., :half].astype(jnp.float32)
    x2 = x[..., half:ROT_DIM].astype(jnp.float32)
    c = cos[None, :, None, :]
    s = sin[None, :, None, :]
    rot = jnp.concatenate([x1 * c - x2 * s, x2 * c + x1 * s], axis=-1).astype(x.dtype)
    return jnp.concatenate([rot, x[..., ROT_DIM:]], axis=-1)

def swa_sink_attention(q, k, v, sinks):
    B, S = q.shape[0], q.shape[1]
    nb = S // BLOCK
    qb = q.reshape(B, nb, BLOCK, N_KV_HEADS, GQA_GROUP, HEAD_DIM)

    def with_prev(t):
        tb = t.reshape(B, nb, BLOCK, N_KV_HEADS, HEAD_DIM)
        prev = jnp.pad(tb[:, :-1], ((0, 0), (1, 0), (0, 0), (0, 0), (0, 0)))
        return jnp.concatenate([prev, tb], axis=2)

    kb, vb = with_prev(k), with_prev(v)
    s = jnp.einsum('bnqhgd,bnkhd->bnhgqk', qb, kb).astype(jnp.float32) * (HEAD_DIM ** -0.5)
    qi = jnp.arange(BLOCK)[:, None]
    ki = jnp.arange(2 * BLOCK)[None, :]
    diff = qi + BLOCK - ki
    band = (diff >= 0) & (diff < WINDOW)
    valid = (jnp.arange(nb)[:, None, None] > 0) | (ki[None] >= BLOCK)
    mask = band[None] & valid
    s = jnp.where(mask[None, :, None, None], s, -jnp.inf)
    sink = sinks.astype(jnp.float32).reshape(1, 1, N_KV_HEADS, GQA_GROUP, 1, 1)
    m = jnp.maximum(jnp.max(s, axis=-1, keepdims=True), sink)
    p = jnp.exp(s - m)
    denom = jnp.sum(p, axis=-1, keepdims=True) + jnp.exp(sink - m)
    p = (p / denom).astype(v.dtype)
    o = jnp.einsum('bnhgqk,bnkhd->bnqhgd', p, vb)
    return o.reshape(B, S, ATTN_DIM)

def second_inputs(seed: int = 0) -> dict:
    key = jax.random.key(seed)
    ks = jax.random.split(key, 17)
    f32 = jnp.float32

    def w(k, shape, fan_in):
        return jax.random.normal(k, shape, f32) * (fan_in ** -0.5)

    def gain(k, shape):
        return 1.0 + 0.05 * jax.random.normal(k, shape, f32)

    L = DEPTH
    return {
        "x": jax.random.normal(ks[0], (BATCH, SEQ, D_MODEL), f32),
        "ln_ffn1": gain(ks[1], (L, D_MODEL)),
        "w_ffn1_gu": w(ks[2], (L, D_MODEL, 2 * D_FF), D_MODEL),
        "w_ffn1_down": w(ks[3], (L, D_FF, D_MODEL), D_FF),
        "ln_mix": gain(ks[4], (L, D_MODEL)),
        "w_in": w(ks[5], (L, D_MODEL, IN_DIM), D_MODEL),
        "pool_w": w(ks[6], (L, POOL_GROUPS, POOL_GROUP_DIM, POOL_GROUP_DIM), POOL_GROUP_DIM),
        "pool_scale": 1.0 + 0.1 * jax.random.normal(ks[7], (L, POOL_DIM), f32),
        "w_pool_branch": w(ks[8], (L, POOL_DIM, D_MODEL), POOL_DIM),
        "q_norm": gain(ks[9], (L, HEAD_DIM)),
        "k_norm": gain(ks[10], (L, HEAD_DIM)),
        "sinks": 0.5 * jax.random.normal(ks[11], (L, N_Q_HEADS), f32),
        "w_attn_branch": w(ks[12], (L, ATTN_DIM, D_MODEL), ATTN_DIM),
        "w_out": w(ks[13], (L, D_MODEL, D_MODEL), D_MODEL),
        "ln_ffn2": gain(ks[14], (L, D_MODEL)),
        "w_ffn2_gu": w(ks[15], (L, D_MODEL, 2 * D_FF), D_MODEL),
        "w_ffn2_down": w(ks[16], (L, D_FF, D_MODEL), D_FF),
    }

def second_block(x, ln_ffn1, w_ffn1_gu, w_ffn1_down, ln_mix, w_in, pool_w, pool_scale,
              w_pool_branch, q_norm, k_norm, sinks, w_attn_branch, w_out,
              ln_ffn2, w_ffn2_gu, w_ffn2_down):
    B, S, _ = x.shape
    pos = jnp.arange(S, dtype=jnp.float32)
    inv_freq = ROPE_THETA ** (-jnp.arange(0, ROT_DIM, 2, dtype=jnp.float32) / ROT_DIM)
    ang = pos[:, None] * inv_freq[None, :]
    cos, sin = jnp.cos(ang), jnp.sin(ang)
    splits = [POOL_DIM, POOL_DIM + ATTN_DIM, POOL_DIM + ATTN_DIM + KV_DIM,
              POOL_DIM + ATTN_DIM + 2 * KV_DIM]

    for l in range(DEPTH):
        x = x + 0.5 * swiglu(rmsnorm(x, ln_ffn1[l]), w_ffn1_gu[l], w_ffn1_down[l])

        h = rmsnorm(x, ln_mix[l])
        z = h @ w_in[l]
        u_pool, q, k, v, gate_logits = jnp.split(z, splits, axis=-1)

        a = pool_mixer(u_pool, pool_w[l], pool_scale[l]) @ w_pool_branch[l]

        q = rmsnorm(q.reshape(B, S, N_Q_HEADS, HEAD_DIM), q_norm[l])
        k = rmsnorm(k.reshape(B, S, N_KV_HEADS, HEAD_DIM), k_norm[l])
        v = v.reshape(B, S, N_KV_HEADS, HEAD_DIM)
        q = partial_rope(q, cos, sin)
        k = partial_rope(k, cos, sin)
        b = swa_sink_attention(q, k, v, sinks[l]) @ w_attn_branch[l]

        g_pool, g_attn = jnp.split(jax.nn.sigmoid(gate_logits), N_BRANCHES, axis=-1)
        x = x + (g_pool * a + g_attn * b) @ w_out[l]

        x = x + 0.5 * swiglu(rmsnorm(x, ln_ffn2[l]), w_ffn2_gu[l], w_ffn2_down[l])
    return x


def setup_inputs(seed=0):
    out = dict(first_inputs(seed))
    for name, value in second_inputs(seed + 1).items():
        if name != "x":
            out[name + "_2"] = value
    return out


def reference(
    x, norm_mix_g, norm_ffn_g, norm_final_g, ab_w_in, a_ln_g, a_ws, a_ws_b, b_conv_w, ab_w_out,
    c_w_in, c_conv_w, c_conv_b, c_w_a, c_b_a, c_w_x, c_b_x, c_lambda, c_w_out, moe_w_rg,
    moe_b_rg, moe_w_re, moe_b_re, moe_w_gate, moe_w_up, moe_w_down, ln_ffn1_2, w_ffn1_gu_2,
    w_ffn1_down_2, ln_mix_2, w_in_2, pool_w_2, pool_scale_2, w_pool_branch_2, q_norm_2,
    k_norm_2, sinks_2, w_attn_branch_2, w_out_2, ln_ffn2_2, w_ffn2_gu_2, w_ffn2_down_2,
):
    x = first_block(
        x, norm_mix_g, norm_ffn_g, norm_final_g, ab_w_in, a_ln_g, a_ws, a_ws_b, b_conv_w,
        ab_w_out, c_w_in, c_conv_w, c_conv_b, c_w_a, c_b_a, c_w_x, c_b_x, c_lambda, c_w_out,
        moe_w_rg, moe_b_rg, moe_w_re, moe_b_re, moe_w_gate, moe_w_up, moe_w_down,
    )
    return second_block(
        x, ln_ffn1_2, w_ffn1_gu_2, w_ffn1_down_2, ln_mix_2, w_in_2, pool_w_2, pool_scale_2,
        w_pool_branch_2, q_norm_2, k_norm_2, sinks_2, w_attn_branch_2, w_out_2, ln_ffn2_2,
        w_ffn2_gu_2, w_ffn2_down_2,
    )


_drawn_inputs = setup_inputs


def setup_inputs(seed=0):
    import zlib

    import numpy as np

    out = dict(_drawn_inputs(seed))
    spreads = {}
    factors = {'c_b_a': 8.0,
     'c_b_x': 5.849,
     'moe_b_rg': 4.089,
     'q_norm_2': 8.0,
     'k_norm_2': 8.0,
     'sinks_2': 46.118}
    for name, (base, spread) in spreads.items():
        noise = np.random.default_rng([zlib.crc32(name.encode()), seed]).standard_normal(out[name].shape)
        drawn = base * np.exp(spread * noise) if base else spread * noise
        out[name] = __import__('jax').numpy.asarray(drawn.astype(out[name].dtype))
    for name, factor in factors.items():
        out[name] = (out[name] * factor).astype(out[name].dtype)
    return out
```

```python
from contextlib import ExitStack, contextmanager

import numpy as np
import concourse.bass as bass
from concourse import mybir
from concourse.alu_op_type import AluOpType as ALU

F32 = mybir.dt.float32
I32 = mybir.dt.int32
BF16 = mybir.dt.bfloat16
ACTF = mybir.ActivationFunctionType
X = mybir.AxisListType.X

P = 128
D = 1024
KD = D // P
T = 256
TT = T // P
EPS = 1e-6

D_A = 512
NA = D_A // P
N_GROUPS, PER_GROUP = 4, 8
N_EXP = N_GROUPS * PER_GROUP
D_EXP = 512
FE = D_EXP // P
CAP = 32
QUAD = P // CAP
QUADS = N_EXP // QUAD

D_FF = 2816
GF = 2
N_GRP = D_FF // P // GF
HD = 64
N_Q, N_KV = 8, 2
N_HEADS = N_Q + N_KV
WINDOWS = (2, 4, 8, 16)
EDGE = max(WINDOWS)
ROT = HD // 4
NEG = -1e30

RING = 6
CHUNK = 256
RING_F = KD * CHUNK
EXP_F = KD * D_EXP
WORK_F = 8320


def constant_table():
    i = np.arange(P)
    parts = [("ident", np.eye(P)), ("ones", np.ones((P, P)))]
    parts.append(("causal", (i[None, :] <= i[:, None]) * 1.0))
    parts.append(("before", (i[:, None] < i[None, :]) * 1.0))
    parts.append(("iota", np.tile(np.arange(CAP, dtype=np.float64), (P, 1))))
    parts.append(("rank_g", np.tile(N_GROUPS - np.arange(N_GROUPS), (P, 1))))
    parts.append(("rank_e", np.tile(N_EXP - np.arange(N_EXP), (P, 1))))
    pos = np.arange(T, dtype=np.float32)
    freq = np.float32(500000.0) ** (-np.arange(0, ROT, 2, dtype=np.float32) / np.float32(ROT))
    ang = (pos[:, None] * freq[None, :].astype(np.float32)).astype(np.float32)
    half = ROT // 2
    for name, v in (("cos", np.cos(ang)), ("sin", np.sin(ang))):
        parts.append((name, v.reshape(TT, P, half).transpose(1, 0, 2).reshape(P, TT * half)))
    cnt = np.stack([1.0 / np.minimum(np.arange(EDGE) + 1, w) for w in WINDOWS])
    parts.append(("rcount", np.tile(cnt.reshape(1, -1), (P, 1))))
    q, k = i[:, None], np.arange(2 * P)[None, :]
    diff = q + P - k
    parts.append(("band", np.where((diff >= 0) & (diff < P), 0.0, NEG)))
    where, at = {}, 0
    for name, v in parts:
        where[name] = (at, v.shape[1])
        at += v.shape[1]
    return where, np.concatenate([v for _, v in parts], axis=1).astype(np.float32)


def small_layout():
    cols = [("norm_mix_g", 2 * KD), ("norm_ffn_g", 2 * KD), ("norm_final_g", KD),
            ("b_conv_w", 3 * NA), ("c_conv_w", 4 * KD), ("c_conv_b", KD), ("c_b_a", KD),
            ("c_b_x", KD), ("c_lambda", KD), ("ln_ffn1_2", 2 * KD), ("ln_mix_2", 2 * KD),
            ("ln_ffn2_2", 2 * KD), ("pool_scale_2", 2 * 4),
            ("a_ln_g", D_A), ("a_ws_b", NA * P), ("moe_b", 2 * (N_GROUPS + N_EXP)),
            ("q_norm_2", 2 * HD), ("k_norm_2", 2 * HD), ("sinks_2", 2 * N_Q)]
    where, at = {}, 0
    for name, n in cols:
        where[name] = (at, n)
        at += n
    return where, at


class Counter:

    def __init__(self, name, sem, step):
        self.name, self.sem, self.step, self.const = name, sem, step, 0


class Ticket:

    def __init__(self, counter, const, loops):
        self.counter, self.const, self.loops = counter, const, loops


class Loop:
    def __init__(self, prog, name, n):
        self.prog, self.name, self.n, self.open = prog, name, n, True
        self.entry = {}

    def rate(self, counter):
        return self.prog.rates.get((self.name, counter.name), 0)

    def mark(self, name, ticket):
        self.prog.new_marks[(self.name, name)] = ticket.const - self.entry.get(ticket.counter.name, 0)
        assert ticket.loops[-1] is self

    def last_time(self, name, counter):
        off = self.prog.marks.get((self.name, name), 0)
        c = self.entry.get(counter.name, 0) + off - self.rate(counter)
        return Ticket(counter, c, tuple(self.prog.loops))


class Program:
    def __init__(self, nc, rates, marks):
        self.nc, self.rates, self.marks = nc, rates, marks
        self.new_rates, self.new_marks = {}, {}
        self.loops, self.counters, self.engines = [], [], []
        self.turns = nc.alloc_semaphore("turns")

    def counter(self, name, step=1):
        c = Counter(name, self.nc.alloc_semaphore(name), step)
        self.counters.append(c)
        return c

    def now(self, counter):
        return Ticket(counter, counter.const, tuple(self.loops))

    @contextmanager
    def loop(self, name, n):
        lp = Loop(self, name, n)
        lp.entry = {c.name: c.const for c in self.counters}
        with self.nc.Fori(0, n) as i:
            lp.i = i
            self.loops.append(lp)
            yield lp
            self.loops.pop()
            for e in self.engines:
                e.seen = {k: v for k, v in e.seen.items() if lp not in k[1]}
        lp.open = False
        for c in self.counters:
            per = c.const - lp.entry.get(c.name, 0)
            self.new_rates[(name, c.name)] = per
            c.const += (n - 1) * per


class Engine:
    def __init__(self, prog, e, name):
        self.prog, self.e, self.name, self.seen = prog, e, name, {}
        self.count = prog.counter(name)
        prog.engines.append(self)

    def wait(self, *tickets):
        for t in tickets:
            if t is None:
                continue
            if isinstance(t, (list, tuple)):
                self.wait(*t)
                continue
            const, live = t.const, []
            for lp in t.loops:
                if lp.open:
                    live.append(lp)
                else:
                    const += (lp.n - 1) * lp.rate(t.counter)
            if const <= 0 and not live:
                continue
            key = (t.counter, tuple(live))
            if self.seen.get(key, -1) >= const:
                continue
            self.seen[key] = const
            value = const
            for lp in live:
                if lp.rate(t.counter):
                    value = value + lp.i * lp.rate(t.counter)
            self.e.wait_ge(t.counter.sem, value)

    def done(self, instruction):
        instruction.then_inc(self.count.sem, 1)
        self.count.const += 1
        return self.prog.now(self.count)

    def then(self, instruction):
        t = self.done(instruction)
        self.wait(t)
        return t

    def last(self):
        return self.prog.now(self.count)

    def step(self):
        self.e.sem_inc(self.prog.turns, 1)


class Buffer:

    def __init__(self, ap=None):
        self.ap, self.ready, self.free = ap, None, None


def build(nc, a, out, rates=None, marks=None, upto=None):
    pr = Program(nc, rates or {}, marks or {})
    PE, ACT, DVE, POOL, SP = (Engine(pr, e, n) for e, n in (
        (nc.tensor, "pe_done"), (nc.scalar, "act_done"), (nc.vector, "dve_done"),
        (nc.gpsimd, "pool_done"), (nc.sync, "sp_done")))
    compute = (PE, ACT, DVE)
    mm = nc.tensor.matmul

    def sb(name, cols, dt=F32):
        return nc.alloc_sbuf_tensor(name, [P, cols], dt)

    cw, _ = constant_table()
    n_const = sum(n for _, n in cw.values())
    sw, n_small = small_layout()
    consts, small = sb("consts", n_const), sb("small", n_small)

    def C(name):
        return consts[:, cw[name][0]:cw[name][0] + cw[name][1]]

    def S(name, at=0, n=None):
        c0, width = sw[name]
        return small[:, c0 + at:c0 + at + (width - at if n is None else n)]

    xT = sb("xT", KD * T)[:, :].rearrange("p (k t) -> p k t", k=KD)
    hT = sb("hT", KD * T)[:, :].rearrange("p (k t) -> p k t", k=KD)
    work = sb("work", WORK_F)
    rinv = sb("rinv", T)
    most_tokens = sb("most_tokens", 2, I32)
    zeros = sb("zeros", 512, BF16)
    dense_ring = [sb(f"dense_ring{s}", RING_F) for s in range(RING)]
    expert_mem = sb("expert_ring", RING * EXP_F)
    expert_ring = [expert_mem[:, s * EXP_F:(s + 1) * EXP_F] for s in range(RING)]
    ps = nc.alloc_psum_tensor("ps", [P, 8, 512], F32)
    bank = [Buffer(ps[:, b, :]) for b in range(8)]
    x_state, h_state, work_state = Buffer(xT), Buffer(hT), Buffer()

    once = {}

    def load(name, dst, src, eng=SP):
        c = once.get(name) or pr.counter("ld_" + name, 16)
        once[name] = c
        eng.e.dma_start(dst, src).then_inc(c.sem, 16)
        c.const += 16
        return pr.now(c)

    x_tok = work[:, 0:TT * D].rearrange("p (a d) -> p a d", a=TT)
    x_loaded = load("x", x_tok, a["x"].rearrange("(a p) d -> p a d", p=P))
    consts_loaded = load("consts", consts[:, :], a["consts"])
    small_loaded = load("small", small[:, :], a["small"])

    slot_count = [pr.counter(f"dense{s}_loaded", 16) for s in range(RING)]
    slot_queue = [[] for _ in range(RING)]

    def dense_load(s, pieces):
        for dst, src in pieces(dense_ring[s]):
            nc.sync.dma_start(dst, src).then_inc(slot_count[s].sem, 16)
            slot_count[s].const += 16

    def queue_stage(chunks):
        for j, c in enumerate(chunks):
            slot_queue[j % RING].append(c)

    def dense_release(s, ticket):
        if slot_queue[s]:
            SP.wait(ticket)
            dense_load(s, slot_queue[s].pop(0))

    def dense_ready(engine, s):
        engine.wait(pr.now(slot_count[s]))

    def cols(w, c0, n=CHUNK, k=KD):
        def pieces(buf):
            return [(buf[:, 0:k * n].rearrange("p (k n) -> p k n", k=k),
                     w[:, c0:c0 + n].rearrange("(k p) n -> p k n", p=P))]
        return pieces

    def rows(w, r):
        def pieces(buf):
            src = w[bass.ds(r * GF * P, GF * P), :]
            return [(buf[:, 0:GF * D].rearrange("p (f n) -> p f n", f=GF),
                     src.rearrange("(f p) n -> p f n", p=P))]
        return pieces

    def cols_at(w, g, base):
        def pieces(buf):
            src = w[:, bass.ds(g * CHUNK + base, CHUNK)]
            return [(buf[:, :].rearrange("p (k n) -> p k n", k=KD),
                     src.rearrange("(k p) n -> p k n", p=P))]
        return pieces

    exp_count = [pr.counter(f"expert{s}_loaded", 16) for s in range(RING)]

    def expert_piece(layer, pair, s):
        e, m = pair * 2 + s % 2, s // 2
        w = a[("moe_w_gate", "moe_w_up", "moe_w_down")[m]]
        src = w[bass.ds(e + layer * N_EXP, 1), :, :].rearrange("o (k p) n -> p (o k) n", p=P)
        return expert_ring[s].rearrange("p (k n) -> p k n", k=KD if m < 2 else FE), src

    def expert_load(layer, pair, s, counts=None):
        c = (counts or exp_count)[s]
        nc.sync.dma_start(*expert_piece(layer, pair, s)).then_inc(c.sem, 16)
        c.const += 16

    ffn_w = [(a["w_ffn1_gu_2"], a["w_ffn1_down_2"]), (a["w_ffn2_gu_2"], a["w_ffn2_down_2"])]

    def ffn_chunks(layer, which):
        gu, dn = (w[layer] for w in ffn_w[which])
        first = []
        for g in range(2):
            first += [cols_at(gu, g, 0), cols_at(gu, g, D_FF), rows(dn, g)]
        return first

    def mixer2_chunks(layer):
        w_in = a["w_in_2"][layer]
        wa = a["w_attn_branch_2"][layer]
        order = [2, 3, 4, 0, 1] + list(range(5, 13))
        chunks = [cols(w_in, c * CHUNK) for c in order]

        def pool_w(buf):
            return [(buf[:, 0:4 * P].rearrange("p (g d) -> p g d", g=4),
                     a["pool_w_2"][layer].rearrange("g c d -> c g d"))]

        def attn_rows(c0):
            def pieces(buf):
                v = buf[:, :].rearrange("p (j n) -> p j n", j=4)
                return [(v[g * HD:(g + 1) * HD, :, :],
                         wa[g * 4 * HD:(g + 1) * 4 * HD, c0:c0 + 512].rearrange("(j c) n -> c j n", c=HD))
                        for g in range(2)]
            return pieces

        chunks.append(pool_w)
        wp = a["w_pool_branch_2"][layer]
        chunks += [cols(wp, 0, 512, 4), cols(wp, 512, 512, 4), attn_rows(0), attn_rows(512)]
        chunks += [cols(a["w_out_2"][layer], c * CHUNK) for c in range(4)]
        return chunks

    queue_stage([cols(a["ab_w_in"], c * CHUNK) for c in (2, 3, 6, 7, 8, 9, 4, 5, 0, 1)])
    queue_stage([cols(a["ab_w_out"], c * CHUNK) for c in range(4)])
    queue_stage([cols(a["c_w_in"], c * CHUNK) for c in (4, 5, 6, 7, 0, 1, 2, 3)])

    def lru_w(w):
        return lambda buf: [(buf[:, 0:KD * P].rearrange("p (h d) -> p h d", h=KD),
                             w.rearrange("h c d -> c h d"))]

    queue_stage([lru_w(a["c_w_a"]), lru_w(a["c_w_x"])]
                + [cols(a["c_w_out"], c * CHUNK) for c in range(4)])
    for layer in range(2):
        queue_stage(ffn_chunks(layer, 0))
        slot_queue[2].append(rows(a["w_ffn1_down_2"][layer], N_GRP - 1))
        queue_stage(mixer2_chunks(layer))
        queue_stage(ffn_chunks(layer, 1))
        slot_queue[2].append(rows(a["w_ffn2_down_2"][layer], N_GRP - 1))

    for s in range(RING):
        dense_load(s, slot_queue[s].pop(0))
    ws_rows = work[:, 6144:6144 + NA * P].rearrange("p (h s) -> p h s", h=NA)
    ws_loaded = load("ws", ws_rows, a["a_ws"].rearrange("h t s -> t h s"))
    for s in range(RING):
        expert_load(0, 0, s)

    PE.wait(consts_loaded)
    DVE.wait(consts_loaded, small_loaded)
    ACT.wait(consts_loaded, small_loaded)
    z_ready = DVE.done(nc.vector.memset(zeros[:, :], 0.0))
    PE.wait(z_ready)

    def copy_out(engine, dst, src):
        return engine.done(nc.scalar.copy(dst, src) if engine is ACT else nc.vector.tensor_copy(dst, src))

    def transpose_block(src_of, dst, n, bank0, width=P, engines=(ACT, DVE)):
        tickets = []
        for b in range((n + 3) // 4):
            m = min(4, n - 4 * b)
            buf = bank[(bank0 + b) % 8]
            PE.wait(buf.free)
            for j in range(m):
                ins = nc.tensor.transpose(buf.ap[:, j * P:(j + 1) * P], src_of(4 * b + j), C("ident"))
            t = PE.done(ins)
            e = engines[b % len(engines)]
            e.wait(t)
            buf.free = copy_out(e, dst[:, 4 * b * P:(4 * b + m) * P], buf.ap[:, 0:m * P])
            tickets.append(buf.free)
        return tickets

    def flat(ap):
        return ap.rearrange("p k t -> p (k t)")

    def rms_norm(gain):
        ACT.wait(x_state.ready, h_state.free)
        DVE.wait(h_state.free)
        PE.wait(bank[0].free)
        for q in range(4):
            t = ACT.done(nc.scalar.activation(hT[:, 2 * q:2 * q + 2, :], xT[:, 2 * q:2 * q + 2, :], ACTF.Square))
            PE.wait(t)
            for k in (2 * q, 2 * q + 1):
                ins = mm(bank[0].ap[:, 0:T], C("ones"), hT[:, k, :], start=k == 0, stop=k == KD - 1)
        DVE.wait(PE.done(ins))
        t = DVE.done(nc.vector.tensor_scalar(rinv[:, :], bank[0].ap[:, 0:T], 1.0 / D, EPS, ALU.mult, ALU.add))
        bank[0].free = t
        ACT.wait(t)
        t = ACT.done(nc.scalar.activation(rinv[:, :], rinv[:, :], ACTF.Sqrt))
        DVE.wait(t)
        DVE.then(nc.vector.reciprocal(rinv[:, :], rinv[:, :]))
        h_state.ready = []
        for k in range(KD):
            h_state.ready.append(DVE.done(nc.vector.scalar_tensor_tensor(
                hT[:, k, :], xT[:, k, :], gain[:, k:k + 1], rinv[:, :], ALU.mult, ALU.mult)))

    def project(n_chunks, rhs, nk, evacuate, bank_of, tiles=2, rhs_ready=None):
        for j in range(n_chunks):
            s = j % RING
            dense_ready(PE, s)
            w = dense_ring[s][:, 0:nk * tiles * P].rearrange("p (k n) -> p k n", k=nk)
            bufs = [bank[b] for b in bank_of(j)]
            for f in range(tiles):
                buf = bufs[f // 2]
                PE.wait(buf.free)
                for k in range(nk):
                    if rhs_ready and f == 0:
                        PE.wait(rhs_ready[k])
                    ins = mm(buf.ap[:, (f % 2) * T:(f % 2 + 1) * T], w[:, k, f * P:(f + 1) * P], rhs(k),
                             start=k == 0, stop=k == nk - 1)
            t = PE.done(ins)
            dense_release(s, t)
            evacuate(j, bufs, t)

    def add_to_x(scale=None):
        def evacuate(j, bufs, t):
            DVE.wait(t)
            xs = flat(xT)[:, j * 2 * T:(j + 1) * 2 * T]
            if scale is None:
                ins = nc.vector.tensor_tensor(xs, bufs[0].ap, xs, ALU.add)
            else:
                ins = nc.vector.scalar_tensor_tensor(xs, bufs[0].ap, scale, xs, ALU.mult, ALU.add)
            bufs[0].free = x_state.ready = DVE.done(ins)
        return evacuate

    PE.wait(x_loaded)
    tk = []
    for tt in range(TT):
        for kq in range(2):
            buf = bank[tt * 2 + kq]
            for j in range(4):
                ins = nc.tensor.transpose(buf.ap[:, j * P:(j + 1) * P],
                                          x_tok[:, tt, (kq * 4 + j) * P:(kq * 4 + j + 1) * P], C("ident"))
            t = PE.done(ins)
            e = (ACT, DVE)[kq]
            e.wait(t)
            buf.free = copy_out(e, xT[:, kq * 4:kq * 4 + 4, tt * P:(tt + 1) * P],
                                buf.ap.rearrange("p (j t) -> p j t", j=4))
            tk.append(buf.free)
    x_state.ready = tk
    work_state.free = [PE.last()] + tk
    DVE.wait(tk)

    def mixer_ab():
        def tile(at, n, w=T):
            return work[:, at:at + n * w].rearrange("p (k t) -> p k t", k=n)
        yT = tile(0, KD)
        v_tok = tile(2048, TT, D_A)
        PAD = 2
        gx = tile(3072, NA, T + PAD)
        acc = tile(3072 + NA * (T + PAD), NA)
        wsT = work[:, 5632:5632 + NA * P].rearrange("p (h t) -> p h t", h=NA)
        stat = work[:, 6656:6656 + 16]
        for e in (ACT, DVE):
            e.wait(work_state.free)
        DVE.then(nc.vector.memset(gx[:, :, 0:PAD], 0.0))
        DVE.wait(ws_loaded)
        for h in range(NA):
            t = DVE.done(nc.vector.tensor_tensor(ws_rows[:, h, :], ws_rows[:, h, :], C("causal"), ALU.mult))
        PE.wait(t)
        ws_done = transpose_block(lambda h: ws_rows[:, h, :], flat(wsT), NA, 7, engines=(ACT,))

        v_done = []
        for j in range(2):
            dense_ready(PE, j)
            w = dense_ring[j][:, :].rearrange("p (k n) -> p k n", k=KD)
            buf = bank[1 + j]
            PE.wait(buf.free)
            for tt in range(TT):
                for k in range(KD):
                    PE.wait(h_state.ready[k])
                    ins = mm(buf.ap[:, tt * CHUNK:(tt + 1) * CHUNK], hT[:, k, tt * P:(tt + 1) * P], w[:, k, :],
                             start=k == 0, stop=k == KD - 1)
            t = PE.done(ins)
            dense_release(j, t)
            ACT.wait(t)
            buf.free = ACT.done(nc.scalar.activation(
                v_tok[:, :, j * CHUNK:(j + 1) * CHUNK], buf.ap.rearrange("p (a n) -> p a n", a=TT),
                ACTF.Gelu_apprx_tanh))
            v_done.append(buf.free)

        def layer_norm():
            DVE.wait(v_done)
            cen = tile(0, TT, D_A)
            for tt in range(TT):
                s = stat[:, 4 * tt:4 * tt + 4]
                DVE.then(nc.vector.tensor_reduce(s[:, 0:1], v_tok[:, tt, :], X, ALU.add))
                DVE.then(nc.vector.tensor_scalar(s[:, 0:1], s[:, 0:1], 1.0 / D_A, None, ALU.mult))
                DVE.then(nc.vector.tensor_scalar(v_tok[:, tt, :], v_tok[:, tt, :], s[:, 0:1], None, ALU.subtract))
                DVE.then(nc.vector.tensor_tensor(cen[:, tt, :], v_tok[:, tt, :], v_tok[:, tt, :], ALU.mult))
                DVE.then(nc.vector.tensor_reduce(s[:, 1:2], cen[:, tt, :], X, ALU.add))
                t = DVE.done(nc.vector.tensor_scalar(s[:, 1:2], s[:, 1:2], 1.0 / D_A, EPS, ALU.mult, ALU.add))
                ACT.wait(t)
                t = ACT.done(nc.scalar.activation(s[:, 2:3], s[:, 1:2], ACTF.Sqrt))
                DVE.wait(t)
                DVE.then(nc.vector.reciprocal(s[:, 3:4], s[:, 2:3]))
                t = DVE.then(nc.vector.scalar_tensor_tensor(v_tok[:, tt, :], v_tok[:, tt, :], s[:, 3:4],
                                                            S("a_ln_g"), ALU.mult, ALU.mult))
            return t
        state = {}

        def evacuate(j, bufs, t):
            jj, src = j % 2, bufs[0].ap
            src2 = src.rearrange("p (f t) -> p f t", f=2)
            part = slice(2 * jj, 2 * jj + 2)
            kind = j // 2
            if kind == 0:
                ACT.wait(t)
                bufs[0].free = ACT.done(nc.scalar.copy(acc[:, part, :], src2))
                state["gc", jj] = bufs[0].free
            elif kind == 1:
                DVE.wait(t, state["gc", jj])
                bufs[0].free = DVE.then(nc.vector.tensor_tensor(gx[:, part, PAD:], src2, acc[:, part, :], ALU.mult))
                for c in (2 * jj, 2 * jj + 1):
                    DVE.then(nc.vector.tensor_scalar(acc[:, c, :], gx[:, c, 0:T], S("b_conv_w", c, 1), None, ALU.mult))
                    for tap in (1, 2):
                        DVE.then(nc.vector.scalar_tensor_tensor(
                            acc[:, c, :], gx[:, c, tap:tap + T], S("b_conv_w", tap * NA + c, 1),
                            acc[:, c, :], ALU.mult, ALU.add))
            elif kind == 2:
                if jj == 0:
                    state["ln"] = layer_norm()
                DVE.wait(t)
                bufs[0].free = DVE.done(nc.vector.tensor_tensor(
                    yT[:, NA + 2 * jj:NA + 2 * jj + 2, :], src2, acc[:, part, :], ALU.mult))
                state["yb"] = bufs[0].free
            else:
                ACT.wait(t, state["ln"])
                bufs[0].free = ACT.done(nc.scalar.activation(yT[:, part, :], src2, ACTF.Gelu_apprx_tanh))
                state["u"] = bufs[0].free

        def seq(n):
            return [3 + n % 4]
        for j in range(8):
            s = (j + 2) % RING
            dense_ready(PE, s)
            w = dense_ring[s][:, :].rearrange("p (k n) -> p k n", k=KD)
            buf = bank[seq(j)[0]]
            PE.wait(buf.free)
            for f in range(2):
                for k in range(KD):
                    ins = mm(buf.ap[:, f * T:(f + 1) * T], w[:, k, f * P:(f + 1) * P], hT[:, k, :],
                             start=k == 0, stop=k == KD - 1)
            t = PE.done(ins)
            dense_release(s, t)
            evacuate(j, [buf], t)
        h_state.free = PE.last()
        PE.wait(state["ln"], ws_done, bank[0].free, bank[1].free)
        for h in range(NA):
            for c in range(TT):
                ins = mm(bank[h // 2].ap[:, (h % 2) * T + c * P:(h % 2) * T + (c + 1) * P],
                         v_tok[:, c, h * P:(h + 1) * P], wsT[:, h, :], start=True, stop=True)
        t = PE.done(ins)
        DVE.wait(t, state["u"], DVE.last())
        y_ready = []
        for h in range(NA):
            m = bank[h // 2].ap[:, (h % 2) * T:(h % 2 + 1) * T].rearrange("p (c t) -> p c t", c=TT)
            bias = S("a_ws_b", h * P, P).unsqueeze(1).to_broadcast([P, TT, P])
            tmp = acc[:, h, :].rearrange("p (c t) -> p c t", c=TT)
            DVE.then(nc.vector.tensor_tensor(tmp, m, bias, ALU.add))
            y_ready.append(DVE.done(nc.vector.tensor_tensor(yT[:, h, :], acc[:, h, :], yT[:, h, :], ALU.mult)))
        bank[0].free = bank[1].free = y_ready[-1]
        y_ready += [state["yb"]] * NA
        project(4, lambda k: yT[:, k, :], KD, add_to_x(), lambda j: [2 + j % 4], rhs_ready=y_ready)
        work_state.free = [PE.last(), DVE.last(), ACT.last()]

    def mixer_rglru():
        def tile(at, n=KD, w=T):
            return work[:, at:at + n * w].rearrange("p (k t) -> p k t", k=n)
        PAD = 3
        gate = tile(0)
        pad = tile(2048, KD, T + PAD)
        bx = tile(2048)
        xr = tile(2048 + KD * (T + PAD))
        ra = tile(2048 + KD * (T + PAD) + KD * T)
        cst = work[:, 8256:8256 + 6 * KD].rearrange("p (n k) -> p n k", k=KD)
        for e in compute:
            e.wait(work_state.free)
        DVE.then(nc.vector.memset(pad[:, :, 0:PAD], 0.0))
        lam = S("c_lambda")
        y, s, s2, pol = (cst[:, n, :] for n in range(1, 5))
        DVE.then(nc.vector.tensor_scalar(s, lam, -1.0, None, ALU.mult))
        t = DVE.then(nc.vector.tensor_tensor(s, s, lam, ALU.min))
        ACT.wait(t)
        t = ACT.done(nc.scalar.activation(y, s, ACTF.Exp))
        DVE.wait(t)
        DVE.then(nc.vector.tensor_scalar(s, y, 2.0, None, ALU.add))
        DVE.then(nc.vector.reciprocal(s, s))
        DVE.then(nc.vector.tensor_tensor(s, s, y, ALU.mult))
        DVE.then(nc.vector.tensor_tensor(s2, s, s, ALU.mult))
        terms = 9
        DVE.then(nc.vector.tensor_scalar(pol, s2, 1.0 / (2 * terms + 1), 1.0 / (2 * terms - 1), ALU.mult, ALU.add))
        for n in range(terms - 2, -1, -1):
            DVE.then(nc.vector.tensor_tensor(pol, pol, s2, ALU.mult))
            DVE.then(nc.vector.tensor_scalar(pol, pol, 1.0 / (2 * n + 1), None, ALU.add))
        DVE.then(nc.vector.tensor_tensor(pol, pol, s, ALU.mult))
        DVE.then(nc.vector.tensor_scalar(s, lam, 0.0, None, ALU.min))
        DVE.then(nc.vector.scalar_tensor_tensor(pol, pol, -2.0, s, ALU.mult, ALU.add))
        DVE.then(nc.vector.tensor_scalar(cst[:, 0, :], pol, 8.0, None, ALU.mult))
        DVE.then(nc.vector.tensor_scalar(cst[:, 4, :], S("c_b_a"), 0.5, None, ALU.mult))
        half_b = DVE.then(nc.vector.tensor_scalar(cst[:, 5, :], S("c_b_x"), 0.5, None, ALU.mult))

        xr_ready = {}

        def evacuate(j, bufs, t):
            part, src = slice(2 * (j % 4), 2 * (j % 4) + 2), bufs[0].ap.rearrange("p (f t) -> p f t", f=2)
            ACT.wait(t)
            if j >= 4:
                bufs[0].free = ACT.done(nc.scalar.activation(gate[:, part, :], src, ACTF.Gelu_apprx_tanh))
                return
            bufs[0].free = ACT.done(nc.scalar.copy(pad[:, part, PAD:], src))
            DVE.wait(bufs[0].free)
            for c in (2 * j, 2 * j + 1):
                DVE.then(nc.vector.tensor_scalar(xr[:, c, :], pad[:, c, 0:T], S("c_conv_w", c, 1),
                                                 S("c_conv_b", c, 1), ALU.mult, ALU.add))
                for tap in (1, 2, 3):
                    xr_ready[c] = DVE.then(nc.vector.scalar_tensor_tensor(
                        xr[:, c, :], pad[:, c, tap:tap + T], S("c_conv_w", tap * KD + c, 1),
                        xr[:, c, :], ALU.mult, ALU.add))
        project(8, lambda k: hT[:, k, :], KD, evacuate, lambda j: [1 + j % 6], rhs_ready=h_state.ready)
        h_state.free = PE.last()
        gate_ready = ACT.last()
        ACT.wait(half_b, DVE.last())
        for m in range(2):
            dense_ready(PE, m)
            w = dense_ring[m][:, 0:KD * P].rearrange("p (h d) -> p h d", h=KD)
            for h in range(KD):
                buf = bank[h]
                PE.wait(xr_ready[h], buf.free)
                ins = mm(buf.ap[:, 0:T], w[:, h, :], xr[:, h, :], start=True, stop=True)
                t = PE.done(ins)
                ACT.wait(t)
                dst = (ra, bx)[m]
                buf.free = tt_ = ACT.done(nc.scalar.activation(
                    dst[:, h, :], buf.ap[:, 0:T], ACTF.Tanh, bias=cst[:, 4 + m, h:h + 1], scale=0.5))
            dense_release(m, t)
        DVE.wait(tt_)
        DVE.then(nc.vector.tensor_scalar(flat(ra), flat(ra), 0.5, 0.5, ALU.mult, ALU.add))
        for h in range(KD):
            t = DVE.done(nc.vector.tensor_scalar(ra[:, h, :], ra[:, h, :], cst[:, 0, h:h + 1], None, ALU.mult))
        DVE.wait(t)
        ACT.wait(t, h_state.free)
        hf = flat(hT)
        t1 = ACT.done(nc.scalar.activation(hf, flat(ra), ACTF.Tanh, scale=-1.0))
        t2 = ACT.done(nc.scalar.activation(flat(ra), flat(ra), ACTF.Exp))
        DVE.then(nc.vector.tensor_scalar(flat(bx), flat(bx), 0.5, 0.5, ALU.mult, ALU.add))
        DVE.then(nc.vector.tensor_tensor(flat(bx), flat(bx), flat(xr), ALU.mult))
        DVE.wait(t1, t2)
        DVE.then(nc.vector.tensor_tensor(flat(xr), flat(ra), flat(ra), ALU.mult))
        DVE.then(nc.vector.scalar_tensor_tensor(flat(xr), flat(xr), 1.0, hf, ALU.add, ALU.mult))
        t = DVE.last()
        ACT.wait(t)
        t = ACT.done(nc.scalar.activation(flat(xr), flat(xr), ACTF.Sqrt))
        DVE.wait(t, gate_ready)
        DVE.then(nc.vector.tensor_tensor(flat(bx), flat(bx), flat(xr), ALU.mult))
        y_ready = []
        for h in range(KD):
            DVE.then(nc.vector.tensor_tensor_scan(xr[:, h, :], ra[:, h, :], bx[:, h, :], 0.0, ALU.mult, ALU.add))
            y_ready.append(DVE.done(nc.vector.tensor_tensor(gate[:, h, :], gate[:, h, :], xr[:, h, :], ALU.mult)))
        for j in range(4):
            s = 2 + j
            dense_ready(PE, s)
            w = dense_ring[s][:, :].rearrange("p (k n) -> p k n", k=KD)
            buf = bank[j]
            PE.wait(buf.free)
            for f in range(2):
                for k in range(KD):
                    PE.wait(y_ready[k])
                    ins = mm(buf.ap[:, f * T:(f + 1) * T], w[:, k, f * P:(f + 1) * P], gate[:, k, :],
                             start=k == 0, stop=k == KD - 1)
            t = PE.done(ins)
            dense_release(s, t)
            add_to_x()(j, [buf], t)
        work_state.free = [PE.last(), DVE.last(), ACT.last()]
        h_state.free = [PE.last(), DVE.last()]

    def moe(layer):
        NG, NE = N_GROUPS, N_EXP
        at = [0]

        def wk(n):
            at[0] += n
            assert at[0] <= WORK_F
            return work[:, at[0] - n:at[0]]
        h_tok = wk(TT * D)
        xs = wk(KD * P).rearrange("p (k c) -> p k c", k=KD)
        y_slots = wk(D)
        silu_g = [wk(2 * P) for _ in range(2)]
        hid = [wk(2 * P) for _ in range(2)]
        hidT = [wk(2 * P) for _ in range(2)]
        pick = wk(TT * P)
        pick_g = wk(TT * P)
        spread = wk(T)
        w_route = wk(KD * (NG + NE))
        lg = wk(TT * (NG + NE)).rearrange("p (a n) -> p a n", a=TT)
        posm, gates, chosen, tmp_e, one1 = (wk(TT * NE).rearrange("p (a n) -> p a n", a=TT) for _ in range(5))
        gmx = wk(TT * 8).rearrange("p (a n) -> p a n", a=TT)
        goh = wk(TT * NG).rearrange("p (a n) -> p a n", a=TT)
        flag = most_tokens[:, layer:layer + 1]
        for e in compute:
            e.wait(work_state.free)
        SP.wait(work_state.free)
        wr = w_route.rearrange("p (k n) -> p k n", k=KD)
        load("route", wr[:, :, 0:NG], a["moe_w_rg"][layer].rearrange("(k p) n -> p k n", p=P))
        w_loaded = load("route", wr[:, :, NG:], a["moe_w_re"][layer].rearrange("(k p) n -> p k n", p=P))

        rms_norm(S("norm_ffn_g", layer * KD, KD))
        PE.wait(h_state.ready)
        h_done = transpose_block(lambda i: hT[:, i % KD, (i // KD) * P:(i // KD + 1) * P], h_tok, TT * KD, 1)
        PE.wait(w_loaded, bank[6].free)
        n = NG + NE
        for tt in range(TT):
            for k in range(KD):
                ins = mm(bank[6].ap[:, tt * n:(tt + 1) * n], hT[:, k, tt * P:(tt + 1) * P], wr[:, k, :],
                         start=k == 0, stop=k == KD - 1)
        t = PE.done(ins)
        h_state.free = t
        DVE.wait(t)
        V = nc.vector
        bias = S("moe_b", layer * n, n).unsqueeze(1).to_broadcast([P, TT, n])
        bank[6].free = DVE.then(V.tensor_tensor(lg, bank[6].ap[:, 0:TT * n].rearrange("p (a n) -> p a n", a=TT), bias, ALU.add))

        def bc(ap, m):
            return ap.to_broadcast([P, TT, m])

        def first_max(dst, values, rank, m, mx, mi):
            DVE.then(V.tensor_reduce(mx, values, X, ALU.max))
            DVE.then(V.tensor_tensor(dst, values, bc(mx, m), ALU.is_equal))
            DVE.then(V.tensor_tensor(dst, dst, rank.unsqueeze(1).to_broadcast([P, TT, m]), ALU.mult))
            DVE.then(V.tensor_reduce(mi, dst, X, ALU.max))
            DVE.then(V.tensor_tensor(dst, dst, bc(mi, m), ALU.is_equal))

        g = lg[:, :, 0:NG]
        col = [gmx[:, :, i:i + 1] for i in range(8)]
        first_max(goh, g, C("rank_g"), NG, col[0], col[1])
        t = DVE.then(V.tensor_tensor(g, g, bc(col[0], NG), ALU.subtract))
        ACT.wait(t)
        t = ACT.done(nc.scalar.activation(g, g, ACTF.Exp))
        DVE.wait(t)
        DVE.then(V.tensor_reduce(col[2], g, X, ALU.add))
        DVE.then(V.reciprocal(col[2], col[2]))
        e4 = lg[:, :, NG:].rearrange("p a (g j) -> p a g j", g=NG)
        in_g = goh.unsqueeze(3).to_broadcast([P, TT, NG, PER_GROUP])
        DVE.then(V.tensor_scalar(tmp_e.rearrange("p a (g j) -> p a g j", g=NG), in_g, -1.0, -NEG, ALU.add, ALU.mult))
        for tt in range(TT):
            t = DVE.done(V.tensor_tensor(e4[:, tt], e4[:, tt], in_g[:, tt], ALU.mult))
        DVE.wait(t)
        ev = lg[:, :, NG:]
        DVE.then(V.tensor_tensor(ev, ev, tmp_e, ALU.add))
        first_max(one1, ev, C("rank_e"), NE, col[3], col[1])
        DVE.then(V.tensor_scalar(tmp_e, one1, 2 * NEG, None, ALU.mult))
        DVE.then(V.tensor_tensor(ev, ev, tmp_e, ALU.add))
        first_max(tmp_e, ev, C("rank_e"), NE, col[4], col[1])
        t = DVE.then(V.tensor_tensor(col[4], col[4], col[3], ALU.subtract))
        ACT.wait(t)
        t = ACT.done(nc.scalar.activation(col[4], col[4], ACTF.Exp))
        DVE.wait(t)
        DVE.then(V.tensor_scalar(col[5], col[4], 1.0, None, ALU.add))
        DVE.then(V.reciprocal(col[5], col[5]))
        DVE.then(V.tensor_tensor(col[5], col[5], col[2], ALU.mult))
        DVE.then(V.tensor_tensor(col[4], col[4], col[5], ALU.mult))
        DVE.then(V.tensor_tensor(chosen, one1, tmp_e, ALU.add))
        DVE.then(V.tensor_tensor(gates, one1, bc(col[5], NE), ALU.mult))
        DVE.then(V.tensor_tensor(tmp_e, tmp_e, bc(col[4], NE), ALU.mult))
        t = DVE.then(V.tensor_tensor(gates, gates, tmp_e, ALU.add))
        PE.wait(t, bank[7].free)
        B7 = bank[7].ap
        mm(B7[:, 0:NE], C("before"), chosen[:, 0, :], start=True, stop=True)
        mm(B7[:, NE:2 * NE], C("ones"), chosen[:, 0, :], start=True, stop=False)
        mm(B7[:, NE:2 * NE], C("before"), chosen[:, 1, :], start=False, stop=True)
        mm(B7[:, 2 * NE:3 * NE], C("ones"), chosen[:, 0, :], start=True, stop=False)
        t = PE.done(mm(B7[:, 2 * NE:3 * NE], C("ones"), chosen[:, 1, :], start=False, stop=True))
        DVE.wait(t)
        r2 = B7[:, 0:TT * NE].rearrange("p (a n) -> p a n", a=TT)
        DVE.then(V.scalar_tensor_tensor(posm, r2, 1.0, chosen, ALU.add, ALU.mult))
        DVE.then(V.tensor_scalar(posm, posm, -1.0, None, ALU.add))
        DVE.then(V.tensor_reduce(col[6][:, 0], B7[:, 2 * NE:3 * NE], X, ALU.max))
        flag_ready = DVE.then(V.tensor_copy(flag[:, 0:1], col[6][:, 0]))
        bank[7].free = flag_ready

        DVE.wait(h_done)
        ACT.wait(h_done)
        PE.wait(h_done)
        for b in bank:
            PE.wait(b.free)
            b.free = None
        start = [DVE.last(), ACT.last(), PE.last()]
        for e in compute:
            e.wait(start)
        iota = C("iota").unsqueeze(1).to_broadcast([P, QUAD, CAP])
        ends = {}

        def quad_body(quad, counts, release, before):
            DVE.wait(before("pick", PE), before("pick_dve", DVE))
            es = bass.ds(quad * QUAD, QUAD)
            for tt in range(TT):
                slot_of = posm[:, tt, es].unsqueeze(2).to_broadcast([P, QUAD, CAP])
                gate_of = gates[:, tt, es].unsqueeze(2).to_broadcast([P, QUAD, CAP])
                d = pick[:, tt * P:(tt + 1) * P].rearrange("p (e c) -> p e c", e=QUAD)
                dg = pick_g[:, tt * P:(tt + 1) * P].rearrange("p (e c) -> p e c", e=QUAD)
                DVE.then(V.tensor_tensor(d, slot_of, iota, ALU.is_equal))
                picked = DVE.done(V.tensor_tensor(dg, d, gate_of, ALU.mult))
            ends["pick_dve"] = picked
            PE.wait(picked)
            xs_ready = []
            for k in range(KD):
                b = k // 4
                if k % 4 == 0:
                    PE.wait(before(f"bank{b}", DVE))
                for tt in range(TT):
                    ins = mm(bank[b].ap[:, (k % 4) * P:(k % 4 + 1) * P],
                             h_tok[:, tt * D + k * P:tt * D + (k + 1) * P],
                             pick[:, tt * P:(tt + 1) * P], start=tt == 0, stop=tt == TT - 1)
                if k % 4 == 3:
                    t = PE.done(ins)
                    e = (ACT, DVE)[b]
                    e.wait(t, before("xs", PE))
                    xs_ready.append(copy_out(e, xs.rearrange("p k c -> p (k c)")[:, (k - 3) * P:(k + 1) * P], bank[b].ap))
            PE.wait(before("bank5", DVE))
            for tt in range(TT):
                ins = nc.tensor.transpose(bank[5].ap[:, tt * P:(tt + 1) * P], pick_g[:, tt * P:(tt + 1) * P], C("ident"))
            t = ends["pick"] = PE.done(ins)
            ACT.wait(t, before("spread", PE))
            spread_ready = copy_out(ACT, spread, bank[5].ap[:, 0:T])
            PE.wait(xs_ready)
            for pair in range(2):
                b = bank[2 + pair]
                PE.wait(before(f"bank{2 + pair}", DVE))
                half = D_EXP // 2
                for m in range(2):
                    for x in range(2):
                        PE.wait(pr.now(counts[2 * m + x]))
                    for k in range(KD):
                        for x in range(2):
                            w = expert_ring[2 * m + x].rearrange("p (k n) -> p k n", k=KD)
                            slots = xs[:, k, (2 * pair + x) * CAP:(2 * pair + x + 1) * CAP]
                            for hf in range(2):
                                c = (2 * x + hf) * CAP
                                ins = mm(b.ap[c:c + CAP, m * half:(m + 1) * half], slots,
                                         w[:, k, hf * half:(hf + 1) * half], start=k == 0, stop=k == KD - 1)
                    t = PE.done(ins)
                    for x in range(2):
                        release(quad * 2 + pair, 2 * m + x, t)
                if pair == 1:
                    ends["xs"] = t
                ACT.wait(t, before(f"silu{pair}", DVE))
                silu_ready = ACT.done(nc.scalar.activation(silu_g[pair], b.ap[:, 0:half], ACTF.Silu))
                DVE.wait(silu_ready, before(f"hid{pair}", PE))
                t = DVE.done(V.tensor_tensor(hid[pair], silu_g[pair], b.ap[:, half:], ALU.mult))
                ends[f"bank{2 + pair}"] = ends[f"silu{pair}"] = t
                PE.wait(t, before("bank4", DVE) if pair == 0 else hidT_ready)
                for q in range(2):
                    ins = nc.tensor.transpose(bank[4].ap[:, q * P:(q + 1) * P], hid[pair][:, q * P:(q + 1) * P], C("ident"))
                t = ends[f"hid{pair}"] = PE.done(ins)
                DVE.wait(t, before(f"hidT{pair}", PE))
                hidT_ready = copy_out(DVE, hidT[pair], bank[4].ap[:, 0:2 * P])
                PE.wait(hidT_ready, before("y_bank", ACT), before("y_bank_dve", DVE))
                for x in range(2):
                    PE.wait(pr.now(counts[4 + x]))
                for n in range(2):
                    for f in range(FE):
                        for x in range(2):
                            w = expert_ring[4 + x].rearrange("p (k n) -> p k n", k=FE)
                            c = (f % 2) * P + x * 2 * CAP + (f // 2) * CAP
                            r0 = (2 * pair + x) * CAP
                            ins = mm(bank[6 + n].ap[r0:r0 + CAP, :], hidT[pair][:, c:c + CAP],
                                     w[:, f, n * 512:(n + 1) * 512], start=f == 0, stop=f == FE - 1)
                t = ends[f"hidT{pair}"] = PE.done(ins)
                for x in range(2):
                    release(quad * 2 + pair, 4 + x, t)
            ACT.wait(t, before("y", PE))
            y_ready = [copy_out(ACT, y_slots[:, 0:512], bank[6].ap)]
            ends["y_bank"] = y_ready[0]
            DVE.wait(t, before("y", PE))
            y_ready.append(copy_out(DVE, y_slots[:, 512:1024], bank[7].ap))
            ends["y_bank_dve"] = y_ready[1]
            PE.wait(y_ready, spread_ready)
            for q, bn in enumerate((5, 0, 1, 4)):
                b = bank[bn]
                for j in range(2):
                    ins = mm(b.ap[:, j * T:(j + 1) * T], y_slots[:, (2 * q + j) * P:(2 * q + j + 1) * P], spread,
                             start=True, stop=True)
                t = PE.done(ins)
                DVE.wait(t, before("x_dve", DVE) if q == 0 else None)
                xsl = flat(xT)[:, q * 2 * T:(q + 1) * 2 * T]
                ends[f"bank{bn}"] = ends["x_dve"] = DVE.done(V.tensor_tensor(xsl, b.ap, xsl, ALU.add))
            ends["y"] = ends["spread"] = t

        def close(lp):
            for name, t in ends.items():
                lp.mark(name, t)

        DVE.wait(x_state.ready)
        with pr.loop(f"quads{layer}", QUADS - 1) as lp:
            def load_next(pair, s, t):
                SP.wait(t)
                expert_load(layer, pair + 1, s)
            quad_body(lp.i, exp_count, load_next, lambda name, e: lp.last_time(name, e.count))
            close(lp)
        closed = dict(ends)

        def load_last(pair, s, t):
            if pair == 2 * QUADS - 2:
                load_next(pair, s, t)
        quad_body(QUADS - 1, exp_count, load_last, lambda name, e: closed[name])

        def more(tag, above, passes):
            for e in pr.engines:
                e.wait(flag_ready, PE.last(), ACT.last(), DVE.last())
            most = nc.values_load(flag[0:1, 0:1], min_val=0, max_val=T)
            keep = [(e, e.count, dict(e.seen)) for e in pr.engines]
            with nc.If(most > above):
                for e in pr.engines:
                    e.count = pr.counter(f"{e.name}_{tag}{layer}")
                counts = [pr.counter(f"expert{s}_{tag}{layer}", 16) for s in range(RING)]

                def one_pass():
                    DVE.then(V.tensor_scalar(posm, posm, -float(CAP), None, ALU.add))
                    DVE.step()
                    with pr.loop(f"quads_{tag}{layer}", QUADS) as lq:
                        for s in range(RING):
                            expert_load(layer, lq.i * 2, s, counts)

                        def load_second(pair, s, t):
                            if len(seconds) < RING:
                                seconds.append(s)
                                SP.wait(t)
                                expert_load(layer, pair + 1, s, counts)
                        seconds = []
                        quad_body(lq.i, counts, load_second, lambda name, e: None)
                        turn = [PE.last(), ACT.last(), DVE.last()]
                        for e in (PE, ACT, DVE, SP):
                            e.wait(turn)
                            e.step()
                if passes == 1:
                    one_pass()
                else:
                    with pr.loop(f"passes_{tag}{layer}", passes):
                        one_pass()
            for e, c, seen in keep:
                e.count, e.seen = c, seen
        more("more", CAP, 1)
        more("rest", 2 * CAP, T // CAP - 2)
        x_state.ready = DVE.last()
        if layer == 0:
            for s in range(RING):
                expert_load(1, 0, s)
        for b in bank:
            b.free = DVE.last()
        for e in compute:
            e.wait(DVE.last(), ACT.last(), PE.last())
        work_state.free = [PE.last(), DVE.last(), ACT.last()]

    hid_f = [work[:, i * 512:(i + 1) * 512] for i in range(2)]
    silu_f = [work[:, (2 + i) * 512:(3 + i) * 512] for i in range(2)]

    def ffn(layer, which, gain):
        tag = f"ffn{layer}{which}"
        gu, dn = (w[layer] for w in ffn_w[which])
        rms_norm(gain)
        for e in compute:
            e.wait(work_state.free)
        acc = [bank[4 + q] for q in range(4)]
        for b in acc:
            PE.wait(b.free)
            mm(b.ap, zeros[:, 0:P], zeros[:, :], start=True, stop=False, skip_group_check=True)
        now = {}

        def gate_up(par, before, release):
            for m in range(2):
                s, b = 3 * par + m, bank[2 * par + m]
                dense_ready(PE, s)
                PE.wait(before(f"bank{par}", DVE))
                w = dense_ring[s][:, :].rearrange("p (k n) -> p k n", k=KD)
                for f in range(GF):
                    for k in range(KD):
                        PE.wait(h_state.ready[k])
                        ins = mm(b.ap[:, f * T:(f + 1) * T], w[:, k, f * P:(f + 1) * P], hT[:, k, :],
                                 start=k == 0, stop=k == KD - 1)
                t = PE.done(ins)
                release(s, t)
                if m == 0:
                    ACT.wait(t, before(f"bank{par}", DVE))
                    gt = ACT.done(nc.scalar.activation(silu_f[par], b.ap, ACTF.Silu))
            DVE.wait(t, gt, before(f"hid{par}", PE))
            now[f"bank{par}"] = now[f"ready{par}"] = DVE.done(
                nc.vector.tensor_tensor(hid_f[par], silu_f[par], bank[2 * par + 1].ap, ALU.mult))

        def down(par, ready, release):
            s = 3 * par + 2
            dense_ready(PE, s)
            PE.wait(ready)
            w = dense_ring[s][:, 0:GF * D].rearrange("p (f n) -> p f n", f=GF)
            for k in range(KD):
                for f in range(GF):
                    ins = mm(acc[k // 2].ap[:, (k % 2) * T:(k % 2 + 1) * T], w[:, f, k * P:(k + 1) * P],
                             hid_f[par][:, f * T:(f + 1) * T], start=False, stop=False, skip_group_check=True)
            t = PE.done(ins)
            now[f"hid{par}"] = t
            release(s, t)

        for b in range(4):
            PE.wait(bank[b].free)
        none = lambda name, e: None

        def first_release(s, t):
            SP.wait(t)
            dense_load(s, cols_at(gu, 2, 0 if s % 3 == 0 else D_FF))

        gate_up(0, none, first_release)
        loop_turns = (N_GRP - 1) // 2 - 1
        with pr.loop(tag, loop_turns) as lp:
            before = lambda name, e: lp.last_time(name, e.count)

            def release(ahead):
                def go(s, t):
                    SP.wait(t)
                    m = s % 3
                    g = lp.i * 2 + ahead
                    dense_load(s, rows(dn, g) if m == 2 else cols_at(gu, g, 0 if m == 0 else D_FF))
                return go
            gate_up(1, before, release(3))
            down(0, before("ready0", DVE), release(2))
            gate_up(0, before, release(4))
            down(1, now["ready1"], release(3))
            for name, t in now.items():
                lp.mark(name, t)
        closed = dict(now)
        after = lambda name, e: closed[name]
        gate_up(1, after, dense_release)
        down(0, closed["ready0"], dense_release)
        gate_up(0, after, dense_release)
        down(1, now["ready1"], dense_release)
        down(0, now["ready0"], dense_release)
        t = PE.last()
        DVE.wait(t)
        for q in range(4):
            xsl = flat(xT)[:, q * 2 * T:(q + 1) * 2 * T]
            acc[q].free = x_state.ready = DVE.done(nc.vector.scalar_tensor_tensor(
                xsl, acc[q].ap, 0.5, xsl, ALU.mult, ALU.add))
        for b in range(4):
            bank[b].free = now[f"bank{b // 2}"]
        h_state.free = PE.last()
        work_state.free = [PE.last(), DVE.last(), ACT.last()]

    def mixer2(layer):
        V = nc.vector
        rms_norm(S("ln_mix_2", layer * KD, KD))
        for e in compute:
            e.wait(work_state.free)
        at = [0]

        def wk(n):
            at[0] += n
            return expert_mem[:, at[0] - n:at[0]]
        U = N_HEADS
        qk = wk(TT * U * HD).rearrange("p (a u c) -> p a u c", a=TT, u=U)
        sq = wk(TT * U * HD).rearrange("p (a u c) -> p a u c", a=TT, u=U)
        v_tok = wk(TT * P).rearrange("p (a c) -> p a c", a=TT)
        qkT = wk((U // 2) * T).rearrange("p (j t) -> p j t", j=U // 2)
        uT = wk(4 * (T + 16)).rearrange("p (g t) -> p g t", g=4)
        s2 = wk(4 * (T + 16)).rearrange("p (g t) -> p g t", g=4)
        s4 = wk(4 * (T + 16)).rearrange("p (g t) -> p g t", g=4)
        poolT = wk(4 * T).rearrange("p (g t) -> p g t", g=4)
        poolY = wk(4 * T).rearrange("p (g t) -> p g t", g=4)
        sig = wk(16 * T).rearrange("p (k t) -> p k t", k=16)
        prob = [wk(N_Q * P).rearrange("p (h k) -> p h k", h=N_Q), wk(N_Q * 2 * P).rearrange("p (h k) -> p h k", h=N_Q)]
        pT = wk(N_Q * 3 * P)
        oT = wk(4 * T).rearrange("p (j t) -> p j t", j=4)
        merged = wk(KD * T).rearrange("p (k t) -> p k t", k=KD)
        small_q = wk(TT * U * 2 + 64 + 4 * TT * U * 8)
        assert at[0] <= RING * EXP_F
        ms = small_q[:, 0:TT * U].rearrange("p (a u) -> p a u", a=TT)
        half = ROT // 2
        rt = [small_q[:, 64 + i * TT * U * half:64 + (i + 1) * TT * U * half].rearrange(
            "p (a u c) -> p a u c", a=TT, u=U) for i in range(4)]
        stat = small_q[:, TT * U:TT * U + 40]

        got = {}
        for j in range(3):
            dense_ready(PE, j)
            w = dense_ring[j][:, :].rearrange("p (k n) -> p k n", k=KD)
            buf = bank[1 + j]
            PE.wait(buf.free)
            for tt in range(TT):
                for k in range(KD):
                    PE.wait(h_state.ready[k])
                    ins = mm(buf.ap[:, tt * CHUNK:(tt + 1) * CHUNK], hT[:, k, tt * P:(tt + 1) * P], w[:, k, :],
                             start=k == 0, stop=k == KD - 1)
            t = PE.done(ins)
            dense_release(j, t)
            ACT.wait(t)
            for tt in range(TT):
                src = buf.ap[:, tt * CHUNK:(tt + 1) * CHUNK]
                if j < 2:
                    dst = qk[:, tt, 0:N_Q, :].rearrange("p (i g) c -> p i g c", g=2)[:, :, j, :]
                    buf.free = ACT.done(nc.scalar.copy(dst, src.rearrange("p (i c) -> p i c", i=4)))
                else:
                    ACT.done(nc.scalar.copy(qk[:, tt, N_Q:U, :].rearrange("p u c -> p (u c)"), src[:, 0:P]))
                    buf.free = ACT.done(nc.scalar.copy(v_tok[:, tt, :], src[:, P:2 * P]))
        v_ready = ACT.last()

        def head_norm_rope():
            DVE.wait(v_ready)
            qf = qk.rearrange("p a u c -> p (a u) c")
            sf = sq.rearrange("p a u c -> p (a u) c")
            mf = ms.rearrange("p a u -> p (a u)")
            DVE.then(V.tensor_tensor(sf, qf, qf, ALU.mult))
            DVE.then(V.tensor_reduce(mf, sf, X, ALU.add))
            t = DVE.then(V.tensor_scalar(mf, mf, 1.0 / HD, EPS, ALU.mult, ALU.add))
            ACT.wait(t)
            t = ACT.done(nc.scalar.activation(mf, mf, ACTF.Sqrt))
            DVE.wait(t)
            DVE.then(V.reciprocal(mf, mf))
            DVE.then(V.tensor_tensor(qf, qf, mf.unsqueeze(2).to_broadcast([P, TT * U, HD]), ALU.mult))
            for tt in range(TT):
                for (u0, u1, g) in ((0, N_Q, "q_norm_2"), (N_Q, U, "k_norm_2")):
                    gain = S(g, layer * HD, HD).unsqueeze(1).to_broadcast([P, u1 - u0, HD])
                    t = DVE.done(V.tensor_tensor(qk[:, tt, u0:u1, :], qk[:, tt, u0:u1, :], gain, ALU.mult))
            DVE.wait(t)
            x1, x2 = qk[:, :, :, 0:half], qk[:, :, :, half:ROT]
            for tt in range(TT):
                c, s = (C(n)[:, tt * half:(tt + 1) * half].unsqueeze(1).to_broadcast([P, U, half]) for n in ("cos", "sin"))
                for i, (x, f) in enumerate(((x1, c), (x2, s), (x2, c), (x1, s))):
                    t = DVE.done(V.tensor_tensor(rt[i][:, tt], x[:, tt], f, ALU.mult))
            DVE.wait(t)
            for tt in range(TT):
                DVE.done(V.tensor_tensor(x1[:, tt], rt[0][:, tt], rt[1][:, tt], ALU.subtract))
                t = DVE.done(V.tensor_tensor(x2[:, tt], rt[2][:, tt], rt[3][:, tt], ALU.add))
            DVE.wait(t)
            return t

        def heads_to_features():
            PE.wait(got["rope"])
            for tt in range(TT):
                for j0, j1 in ((0, 4), (4, 5)):
                    buf = bank[1 + 2 * tt + j0 // 4]
                    PE.wait(buf.free)
                    for j in range(j0, j1):
                        ins = nc.tensor.transpose(buf.ap[:, (j - j0) * P:(j - j0 + 1) * P],
                                                  qk[:, tt, 2 * j:2 * j + 2, :].rearrange("p g c -> p (g c)"), C("ident"))
                    t = PE.done(ins)
                    ACT.wait(t)
                    buf.free = copy_out(ACT, qkT[:, j0:j1, tt * P:(tt + 1) * P],
                                        buf.ap[:, 0:(j1 - j0) * P].rearrange("p (j t) -> p j t", t=P))
            return ACT.last()

        def scores():
            PE.wait(got["qkT"])
            for b in (0, 1, 2, 3, 4, 5):
                PE.wait(bank[b].free)
            for j in range(4):
                for g in range(2):
                    r = slice(g * HD, (g + 1) * HD)
                    b1 = bank[2 * g + j // 2].ap
                    mm(b1[:, (j % 2) * 2 * P:(j % 2 + 1) * 2 * P], qkT[r, j, P:2 * P], qkT[r, 4, :],
                       start=True, stop=True)
                    ins = mm(bank[4 + g].ap[:, j * P:(j + 1) * P], qkT[r, j, 0:P], qkT[r, 4, 0:P],
                             start=True, stop=True)
            return PE.done(ins)

        def softmax():
            DVE.wait(got["scores"])
            nm, mx, sk, sm = stat[:, 0:8], stat[:, 8:16], stat[:, 16:24], stat[:, 24:32]
            for blk in (1, 0):
                w = (1 + blk) * P
                pb = prob[blk]
                band = C("band")[:, 2 * P - w:2 * P]
                for q in range(4 if blk else 2):
                    nh = 2 if blk else 4
                    src = bank[q if blk else 4 + q]
                    part = pb[:, q * nh:(q + 1) * nh, :]
                    src.free = DVE.done(V.scalar_tensor_tensor(
                        part, src.ap.rearrange("p (h k) -> p h k", h=nh), HD ** -0.5,
                        band.unsqueeze(1).to_broadcast([P, nh, w]), ALU.mult, ALU.add))
                DVE.wait(src.free)
                DVE.then(V.tensor_reduce(mx, pb, X, ALU.max))
                sink = S("sinks_2", layer * N_Q, N_Q)
                DVE.then(V.tensor_tensor(mx, mx, sink, ALU.max))
                DVE.then(V.tensor_scalar(nm, mx, -1.0, None, ALU.mult))
                t = DVE.then(V.tensor_tensor(sk, sink, mx, ALU.subtract))
                ACT.wait(t)
                for h in range(N_Q):
                    ACT.done(nc.scalar.activation(pb[:, h, :], pb[:, h, :], ACTF.Exp, bias=nm[:, h:h + 1],
                                                  accum_out=sm[:, h:h + 1]))
                t = ACT.done(nc.scalar.activation(sk, sk, ACTF.Exp))
                DVE.wait(t)
                DVE.then(V.tensor_tensor(sm, sm, sk, ALU.add))
                DVE.then(V.reciprocal(sm, sm))
                got["prob", blk] = DVE.then(V.tensor_tensor(pb, pb, sm.unsqueeze(2).to_broadcast([P, N_Q, w]), ALU.mult))

        def pooling():
            L = T + 16
            src, dst = uT, s2
            for n, w in enumerate(WINDOWS):
                sh = w // 2
                DVE.then(V.tensor_tensor(dst[:, n:, 16:L], src[:, n:, 16:L], src[:, n:, 16 - sh:L - sh], ALU.add))
                DVE.done(V.tensor_scalar(poolT[:, n, EDGE:], dst[:, n, 16 + EDGE:L], 1.0 / w, None, ALU.mult))
                DVE.then(V.tensor_tensor(poolT[:, n, 0:EDGE], dst[:, n, 16:16 + EDGE],
                                         C("rcount")[:, n * EDGE:(n + 1) * EDGE], ALU.mult))
                t = DVE.then(V.tensor_tensor(poolT[:, n, :], poolT[:, n, :], uT[:, n, 16:L], ALU.subtract))
                src, dst = dst, (s4 if dst is s2 else s2)
            return t

        for buf in (uT, s2, s4):
            t = DVE.done(V.memset(buf[:, :, 0:16], 0.0))
        DVE.wait(t)
        got["rope"] = head_norm_rope()
        for j in range(3, 13):
            s = j % RING
            dense_ready(PE, s)
            w = dense_ring[s][:, :].rearrange("p (k n) -> p k n", k=KD)
            buf = bank[6 + j % 2]
            PE.wait(buf.free)
            for f in range(2):
                for k in range(KD):
                    ins = mm(buf.ap[:, f * T:(f + 1) * T], w[:, k, f * P:(f + 1) * P], hT[:, k, :],
                             start=k == 0, stop=k == KD - 1)
            t = PE.done(ins)
            dense_release(s, t)
            ACT.wait(t)
            src = buf.ap.rearrange("p (f t) -> p f t", f=2)
            if j < 5:
                buf.free = ACT.done(nc.scalar.copy(uT[:, 2 * (j - 3):2 * (j - 3) + 2, 16:], src))
            else:
                c = 2 * (j - 5)
                buf.free = ACT.done(nc.scalar.activation(sig[:, c:c + 2, :], src, ACTF.Tanh, scale=0.5))
                if j == 6:
                    got["sig"] = None
            if j == 4:
                u_ready = ACT.last()
            if j == 5:
                got["qkT"] = heads_to_features()
            if j == 6:
                got["scores"] = scores()
                softmax()
                DVE.wait(u_ready)
                got["pool"] = pooling()
        sig_ready = ACT.last()
        h_state.free = PE.last()
        dense_ready(PE, 13 % RING)
        wp = dense_ring[13 % RING][:, 0:4 * P].rearrange("p (g d) -> p g d", g=4)
        PE.wait(got["pool"], bank[6].free, bank[7].free)
        for g in range(4):
            ins = mm(bank[6 + g // 2].ap[:, (g % 2) * T:(g % 2 + 1) * T], wp[:, g, :], poolT[:, g, :], start=True, stop=True)
        t = PE.done(ins)
        dense_release(13 % RING, t)
        DVE.wait(t)
        for g in range(4):
            b = bank[6 + g // 2]
            b.free = DVE.done(V.tensor_scalar(poolY[:, g, :], b.ap[:, (g % 2) * T:(g % 2 + 1) * T],
                                              S("pool_scale_2", layer * 4 + g, 1), None, ALU.mult))
        pool_ready = DVE.last()
        PE.wait(got["prob", 0], got["prob", 1])
        srcs = [(0, h, 0) for h in range(N_Q)] + [(1, h, kb) for h in range(N_Q) for kb in range(2)]
        p_done = transpose_block(lambda i: prob[srcs[i][0]][:, srcs[i][1], srcs[i][2] * P:(srcs[i][2] + 1) * P],
                                 pT, 3 * N_Q, 0)
        PE.wait(p_done)
        DVE.wait(DVE.last())

        def pT_of(blk, h, kb):
            i = h if blk == 0 else N_Q + 2 * h + kb
            return pT[:, i * P:(i + 1) * P]
        PE.wait(bank[6].free, bank[7].free)
        for j in range(4):
            for g in range(2):
                h = g * 4 + j
                o = bank[6 + j // 2].ap[g * HD:(g + 1) * HD, (j % 2) * T:(j % 2 + 1) * T]
                mm(o[:, 0:P], v_tok[:, 0, g * HD:(g + 1) * HD], pT_of(0, h, 0), start=True, stop=True)
                mm(o[:, P:2 * P], v_tok[:, 0, g * HD:(g + 1) * HD], pT_of(1, h, 0), start=True, stop=False)
                ins = mm(o[:, P:2 * P], v_tok[:, 1, g * HD:(g + 1) * HD], pT_of(1, h, 1), start=False, stop=True)
        t = PE.done(ins)
        ACT.wait(t)
        for q in range(2):
            bank[6 + q].free = ACT.done(nc.scalar.copy(
                oT[:, 2 * q:2 * q + 2, :], bank[6 + q].ap.rearrange("p (j t) -> p j t", j=2)))
        o_ready = ACT.last()
        DVE.wait(sig_ready)
        for br in range(2):
            rhs = (poolY, oT)[br]
            PE.wait((pool_ready, o_ready)[br])
            for c in range(2):
                s = (14 + 2 * br + c) % RING
                dense_ready(PE, s)
                w = dense_ring[s][:, :].rearrange("p (j n) -> p j n", j=4)
                for q in range(2):
                    buf = bank[(br * 4 + c * 2 + q) % 8]
                    PE.wait(buf.free)
                    for f in range(2):
                        for k in range(4):
                            ins = mm(buf.ap[:, f * T:(f + 1) * T], w[:, k, (2 * q + f) * P:(2 * q + f + 1) * P],
                                     rhs[:, k, :], start=k == 0, stop=k == 3)
                    t = PE.done(ins)
                    DVE.wait(t)
                    k0 = c * 4 + 2 * q
                    src = buf.ap.rearrange("p (f t) -> p f t", f=2)
                    dst = merged[:, k0:k0 + 2, :] if br == 0 else sig[:, 8 + k0:8 + k0 + 2, :]
                    buf.free = DVE.then(V.scalar_tensor_tensor(dst, sig[:, br * 8 + k0:br * 8 + k0 + 2, :], 1.0,
                                                               src, ALU.add, ALU.mult))
                    if br == 1:
                        got["m", k0] = DVE.done(V.tensor_tensor(merged[:, k0:k0 + 2, :], merged[:, k0:k0 + 2, :], dst, ALU.add))
                dense_release(s, t)
        project(4, lambda k: merged[:, k, :], KD, add_to_x(0.5), lambda j: [j],
                rhs_ready=[got["m", k // 2 * 2] for k in range(KD)])
        work_state.free = [PE.last(), DVE.last(), ACT.last()]

    def finish(final_norm=True):
        if final_norm:
            rms_norm(S("norm_final_g"))
            src = hT
            PE.wait(h_state.ready)
        else:
            src = xT
            PE.wait(x_state.ready)
        for e in compute:
            e.wait(work_state.free)
        o_tok = work[:, 0:TT * D]
        for tt in range(TT):
            done = transpose_block(lambda i, tt=tt: src[:, i, tt * P:(tt + 1) * P],
                                   o_tok[:, tt * D:(tt + 1) * D], KD, 1 + 2 * tt)
            SP.wait(done)
            t = load("out", out[tt * P:(tt + 1) * P, :], o_tok[:, tt * D:(tt + 1) * D])
        SP.wait(t)
        for s in range(RING):
            SP.wait(pr.now(slot_count[s]), pr.now(exp_count[s]))

    def stages():
        yield "ab", lambda: (rms_norm(S("norm_mix_g", 0, KD)), mixer_ab())
        yield "moe0", lambda: moe(0)
        yield "rglru", lambda: (rms_norm(S("norm_mix_g", KD, KD)), mixer_rglru())
        yield "moe1", lambda: moe(1)
        yield "final", final_of_block1
        for layer in range(2):
            yield f"ffn1_{layer}", lambda layer=layer: ffn(layer, 0, S("ln_ffn1_2", layer * KD, KD))
            yield f"mix_{layer}", lambda layer=layer: mixer2(layer)
            yield f"ffn2_{layer}", lambda layer=layer: ffn(layer, 1, S("ln_ffn2_2", layer * KD, KD))

    def final_of_block1():
        rms_norm(S("norm_final_g"))
        DVE.wait(h_state.ready)
        for q in range(2):
            DVE.then(nc.vector.tensor_copy(xT[:, 4 * q:4 * q + 4, :], hT[:, 4 * q:4 * q + 4, :]))
        x_state.ready = DVE.last()

    for name, stage in stages():
        stage()
        if name == upto:
            break
    finish(final_norm=False)
    return pr.new_rates, pr.new_marks


WEIGHTS = ["a_ws", "ab_w_in", "ab_w_out", "c_w_in", "c_w_a", "c_w_x", "c_w_out", "moe_w_rg", "moe_w_re",
           "moe_w_gate", "moe_w_up", "moe_w_down", "w_ffn1_gu_2", "w_ffn1_down_2", "w_in_2", "pool_w_2",
           "w_pool_branch_2", "w_attn_branch_2", "w_out_2", "w_ffn2_gu_2", "w_ffn2_down_2"]


def lay_out(inputs):
    f = lambda n: np.asarray(inputs[n])
    col = lambda v: np.moveaxis(v.reshape(*v.shape[:-1], v.shape[-1] // P, P), -1, 0).reshape(P, -1)
    row = lambda v: np.broadcast_to(v.reshape(1, -1), (P, v.size))
    parts = [col(f(n)) for n in ("norm_mix_g", "norm_ffn_g", "norm_final_g", "b_conv_w", "c_conv_w", "c_conv_b",
                                 "c_b_a", "c_b_x", "c_lambda", "ln_ffn1_2", "ln_mix_2", "ln_ffn2_2", "pool_scale_2")]
    moe_b = np.concatenate([f("moe_b_rg"), f("moe_b_re")], axis=1)
    parts += [row(v) for v in (f("a_ln_g"), f("a_ws_b"), moe_b, f("q_norm_2"), f("k_norm_2"), f("sinks_2"))]
    small = np.ascontiguousarray(np.concatenate(parts, axis=1))
    arrays = {"x": f("x").reshape(T, D), "consts": constant_table()[1], "small": small}
    for n in WEIGHTS:
        v = f(n)
        if n.startswith(("a_", "ab_", "c_")):
            v = v[0]
        elif n.startswith(("moe_w_gate", "moe_w_up", "moe_w_down")):
            v = v.reshape(2 * N_EXP, *v.shape[2:])
        arrays[n] = v
    return {n: np.ascontiguousarray(v) for n, v in arrays.items()}


def make(arrays, new_core, upto=None):
    counts = ({}, {})
    for _ in range(2):
        nc = new_core()
        aps = {n: nc.dram_tensor("in_" + n, v.shape, mybir.dt.from_np(v.dtype), kind="ExternalInput").ap()
               for n, v in arrays.items()}
        out = nc.dram_tensor("out", (T, D), F32, kind="ExternalOutput").ap()
        counts = build(nc, aps, out, *counts, upto=upto)
    return nc


def kernel(**inputs):
    import concourse.bacc as bacc
    from concourse.bass_utils import run_bass_kernel_spmd
    arrays = lay_out(inputs)
    nc = make(arrays, lambda: bacc.Bacc("TRN2", target_bir_lowering=False, num_devices=1))
    r = run_bass_kernel_spmd(nc, [{"in_" + n: v for n, v in arrays.items()}], core_ids=[0])
    return r.results[0]["out"].reshape(1, T, D)
```

```python
from contextlib import ExitStack, contextmanager

import numpy as np
import concourse.bass as bass
from concourse import mybir
from concourse.alu_op_type import AluOpType as ALU

F32 = mybir.dt.float32
I32 = mybir.dt.int32
BF16 = mybir.dt.bfloat16
F32R = mybir.dt.float32r
ACTF = mybir.ActivationFunctionType
X = mybir.AxisListType.X

P = 128
D = 1024
KD = D // P
T = 256
TT = T // P
EPS = 1e-6

D_A = 512
NA = D_A // P
N_GROUPS, PER_GROUP = 4, 8
N_EXP = N_GROUPS * PER_GROUP
D_EXP = 512
FE = D_EXP // P
CAP = 32
QUAD = P // CAP
QUADS = N_EXP // QUAD

D_FF = 2816
GF = 2
N_GRP = D_FF // P // GF
HD = 64
N_Q, N_KV = 8, 2
N_HEADS = N_Q + N_KV
WINDOWS = (2, 4, 8, 16)
EDGE = max(WINDOWS)
ROT = HD // 4
NEG = -1e30

RING = 6
CHUNK = 256
RING_F = KD * CHUNK
EXP_F = KD * D_EXP
WORK_F = 8320
SCRATCH_F = 10080


def constant_table():
    i = np.arange(P)
    parts = [("ident", np.eye(P)), ("ones", np.ones((P, P)))]
    parts.append(("causal", (i[None, :] <= i[:, None]) * 1.0))
    parts.append(("before", (i[:, None] < i[None, :]) * 1.0))
    parts.append(("iota", np.tile(np.arange(CAP, dtype=np.float64), (P, 1))))
    parts.append(("rank_g", np.tile(N_GROUPS - np.arange(N_GROUPS), (P, 1))))
    parts.append(("rank_e", np.tile(N_EXP - np.arange(N_EXP), (P, 1))))
    pos = np.arange(T, dtype=np.float32)
    freq = np.float32(500000.0) ** (-np.arange(0, ROT, 2, dtype=np.float32) / np.float32(ROT))
    ang = (pos[:, None] * freq[None, :].astype(np.float32)).astype(np.float32)
    half = ROT // 2
    for name, v in (("cos", np.cos(ang)), ("sin", np.sin(ang))):
        parts.append((name, v.reshape(TT, P, half).transpose(1, 0, 2).reshape(P, TT * half)))
    cnt = np.stack([1.0 / np.minimum(np.arange(EDGE) + 1, w) for w in WINDOWS])
    parts.append(("rcount", np.tile(cnt.reshape(1, -1), (P, 1))))
    q, k = i[:, None], np.arange(2 * P)[None, :]
    diff = q + P - k
    parts.append(("band", np.where((diff >= 0) & (diff < P), 0.0, NEG)))
    where, at = {}, 0
    for name, v in parts:
        where[name] = (at, v.shape[1])
        at += v.shape[1]
    return where, np.concatenate([v for _, v in parts], axis=1).astype(np.float32)


def small_layout():
    cols = [("norm_mix_g", 2 * KD), ("norm_ffn_g", 2 * KD), ("norm_final_g", KD),
            ("b_conv_w", 3 * NA), ("c_conv_w", 4 * KD), ("c_conv_b", KD), ("c_b_a", KD),
            ("c_b_x", KD), ("c_lambda", KD), ("ln_ffn1_2", 2 * KD), ("ln_mix_2", 2 * KD),
            ("ln_ffn2_2", 2 * KD), ("pool_scale_2", 2 * 4),
            ("a_ln_g", D_A), ("a_ws_b", NA * P), ("moe_b", 2 * (N_GROUPS + N_EXP)),
            ("q_norm_2", 2 * HD), ("k_norm_2", 2 * HD), ("sinks_2", 2 * N_Q)]
    where, at = {}, 0
    for name, n in cols:
        where[name] = (at, n)
        at += n
    return where, at


class Counter:

    def __init__(self, name, sem, step):
        self.name, self.sem, self.step, self.const = name, sem, step, 0


class Ticket:

    def __init__(self, counter, const, loops):
        self.counter, self.const, self.loops = counter, const, loops


class Loop:

    def __init__(self, prog, name, n, carried):
        self.prog, self.name, self.n, self.open, self.carried = prog, name, n, True, carried
        self.entry = {c.name: c.const for c in prog.counters}

    def rate(self, counter):
        return self.prog.rates.get((self.name, counter.name), 0)

    def last_time(self, name, counter=None):
        left = self.prog.marks.get((self.name, name))
        if left is None:
            return None
        counter = self.prog.by_name[left[0]]
        c = self.entry.get(counter.name, 0) + left[1] - self.rate(counter)
        return Ticket(counter, c, tuple(self.prog.loops))

    def leave(self, tickets):
        for name, t in tickets.items():
            if t is not None and t.loops and t.loops[-1] is self:
                off = t.const - self.entry.get(t.counter.name, 0)
                self.prog.new_marks[(self.name, name)] = (t.counter.name, off)


class Program:
    def __init__(self, nc, rates, marks):
        self.nc, self.rates, self.marks = nc, rates, marks
        self.new_rates, self.new_marks = {}, {}
        self.loops, self.counters, self.engines, self.by_name = [], [], [], {}
        self.turns = nc.alloc_semaphore("turns")

    def counter(self, name, step=1):
        c = Counter(name, self.nc.alloc_semaphore(name), step)
        self.counters.append(c)
        self.by_name[name] = c
        return c

    def now(self, counter):
        return Ticket(counter, counter.const, tuple(self.loops))

    @contextmanager
    def loop(self, name, n, carried=None, engines=()):
        for e in engines:
            e.wait(list(carried.values()))
        lp = Loop(self, name, n, carried)
        with self.nc.Fori(0, n) as i:
            lp.i = i
            self.loops.append(lp)
            if carried is not None:
                for k in list(carried):
                    carried[k] = lp.last_time(k) or carried[k]
            yield lp
            if carried is not None:
                lp.leave(carried)
            self.loops.pop()
            for e in self.engines:
                e.seen = {k: v for k, v in e.seen.items() if lp not in k[1]}
        lp.open = False
        for c in self.counters:
            per = c.const - lp.entry.get(c.name, 0)
            self.new_rates[(name, c.name)] = per
            c.const += (n - 1) * per


class Engine:
    def __init__(self, prog, e, name):
        self.prog, self.e, self.name, self.seen = prog, e, name, {}
        self.count = prog.counter(name)
        self.settle = name == "sp_done"
        prog.engines.append(self)

    def wait(self, *tickets):
        for t in tickets:
            if t is None:
                continue
            if isinstance(t, (list, tuple)):
                self.wait(*t)
                continue
            const, live = t.const, []
            for lp in t.loops:
                if lp.open:
                    live.append(lp)
                else:
                    const += (lp.n - 1) * lp.rate(t.counter)
            if const <= 0 and not live:
                continue
            key = (t.counter, tuple(live))
            if self.seen.get(key, -1) >= const:
                continue
            self.seen[key] = const
            value = const
            for lp in live:
                if lp.rate(t.counter):
                    value = value + lp.i * lp.rate(t.counter)
            self.e.wait_ge(t.counter.sem, value)
            if live and self.settle:
                self.step()

    def done(self, instruction):
        instruction.then_inc(self.count.sem, 1)
        self.count.const += 1
        return self.prog.now(self.count)

    def then(self, instruction):
        t = self.done(instruction)
        self.wait(t)
        return t

    def last(self):
        return self.prog.now(self.count)

    def step(self):
        self.e.sem_inc(self.prog.turns, 1)


class Buffer:

    def __init__(self, ap=None):
        self.ap, self.ready, self.free = ap, None, None


def build(nc, a, out, rates=None, marks=None, upto=None):
    pr = Program(nc, rates or {}, marks or {})
    PE, ACT, DVE, POOL, SP = (Engine(pr, e, n) for e, n in (
        (nc.tensor, "pe_done"), (nc.scalar, "act_done"), (nc.vector, "dve_done"),
        (nc.gpsimd, "pool_done"), (nc.sync, "sp_done")))
    compute = (PE, ACT, DVE)
    mm = nc.tensor.matmul

    def sb(name, cols, dt=F32):
        return nc.alloc_sbuf_tensor(name, [P, cols], dt)

    cw, _ = constant_table()
    n_const = sum(n for _, n in cw.values())
    sw, n_small = small_layout()
    consts, small = sb("consts", n_const), sb("small", n_small)

    def C(name):
        return consts[:, cw[name][0]:cw[name][0] + cw[name][1]]

    def S(name, at=0, n=None):
        c0, width = sw[name]
        return small[:, c0 + at:c0 + at + (width - at if n is None else n)]

    xT = sb("xT", KD * T)[:, :].rearrange("p (k t) -> p k t", k=KD)
    hT = sb("hT", KD * T)[:, :].rearrange("p (k t) -> p k t", k=KD)
    work = sb("work", WORK_F)
    rinv = sb("rinv", T)
    most_tokens = sb("most_tokens", 2, I32)
    zeros = sb("zeros", 512, BF16)
    dense_ring = [sb(f"dense_ring{s}", RING_F) for s in range(RING)]
    block1_memory = ExitStack()
    expert_mem = block1_memory.enter_context(nc.sbuf_tensor("expert_ring", [P, RING * EXP_F], F32))
    expert_ring = [expert_mem[:, s * EXP_F:(s + 1) * EXP_F] for s in range(RING)]
    ps = nc.alloc_psum_tensor("ps", [P, 8, 512], F32)
    bank = [Buffer(ps[:, b, :]) for b in range(8)]
    x_state, h_state, work_state = Buffer(xT), Buffer(hT), Buffer()

    once = {}

    def load(name, dst, src, eng=SP):
        c = once.get(name) or pr.counter("ld_" + name, 16)
        once[name] = c
        eng.e.dma_start(dst, src).then_inc(c.sem, 16)
        c.const += 16
        return pr.now(c)

    x_tok = work[:, 0:TT * D].rearrange("p (a d) -> p a d", a=TT)
    x_loaded = load("x", x_tok, a["x"].rearrange("(a p) d -> p a d", p=P))
    consts_loaded = load("consts", consts[:, :], a["consts"])
    small_loaded = load("small", small[:, :], a["small"])

    slot_count = [pr.counter(f"dense{s}_loaded", 16) for s in range(RING)]
    slot_queue = [[] for _ in range(RING)]

    def dense_load(s, pieces):
        for dst, src in pieces(dense_ring[s]):
            nc.sync.dma_start(dst, src).then_inc(slot_count[s].sem, 16)
            slot_count[s].const += 16

    def queue_stage(chunks):
        for j, c in enumerate(chunks):
            slot_queue[j % RING].append(c)

    def dense_release(s, ticket):
        if slot_queue[s]:
            SP.wait(ticket)
            dense_load(s, slot_queue[s].pop(0))

    def dense_ready(engine, s):
        engine.wait(pr.now(slot_count[s]))

    def cols(w, c0, n=CHUNK, k=KD):
        def pieces(buf):
            return [(buf[:, 0:k * n].rearrange("p (k n) -> p k n", k=k),
                     w[:, c0:c0 + n].rearrange("(k p) n -> p k n", p=P))]
        return pieces

    def rows(w, r):
        def pieces(buf):
            src = w[bass.ds(r * GF * P, GF * P), :]
            return [(buf[:, 0:GF * D].rearrange("p (f n) -> p f n", f=GF),
                     src.rearrange("(f p) n -> p f n", p=P))]
        return pieces

    def cols_at(w, g, base):
        def pieces(buf):
            src = w[:, bass.ds(g * CHUNK + base, CHUNK)]
            return [(buf[:, :].rearrange("p (k n) -> p k n", k=KD),
                     src.rearrange("(k p) n -> p k n", p=P))]
        return pieces

    exp_count = [pr.counter(f"expert{s}_loaded", 16) for s in range(RING)]

    def expert_piece(layer, pair, s):
        e, m = pair * 2 + s % 2, s // 2
        w = a[("moe_w_gate", "moe_w_up", "moe_w_down")[m]]
        src = w[bass.ds(e + layer * N_EXP, 1), :, :].rearrange("o (k p) n -> p (o k) n", p=P)
        return expert_ring[s].rearrange("p (k n) -> p k n", k=KD if m < 2 else FE), src

    def expert_load(layer, pair, s, counts=None):
        c = (counts or exp_count)[s]
        nc.sync.dma_start(*expert_piece(layer, pair, s)).then_inc(c.sem, 16)
        c.const += 16

    ffn_w = [(a["w_ffn1_gu_2"], a["w_ffn1_down_2"]), (a["w_ffn2_gu_2"], a["w_ffn2_down_2"])]

    def queue_ffn(layer, which):
        gu, dn = (w[layer] for w in ffn_w[which])
        first = []
        for g in range(2):
            first += [cols_at(gu, g, 0), cols_at(gu, g, D_FF), rows(dn, g)]
        queue_stage(first)
        last = N_GRP - 1
        slot_queue[2] += [rows(dn, last - 2), rows(dn, last)]
        slot_queue[0].append(cols_at(gu, last, 0))
        slot_queue[1].append(cols_at(gu, last, D_FF))
        slot_queue[5].append(rows(dn, last - 1))

    def mixer2_chunks(layer):
        w_in = a["w_in_2"][layer]
        wa = a["w_attn_branch_2"][layer]
        order = [2, 3, 4, 0, 1] + list(range(5, 13))
        chunks = [cols(w_in, c * CHUNK) for c in order]

        def pool_w(buf):
            return [(buf[:, 0:4 * P].rearrange("p (g d) -> p g d", g=4),
                     a["pool_w_2"][layer].rearrange("g c d -> c g d"))]

        def attn_rows(c0):
            def pieces(buf):
                v = buf[:, :].rearrange("p (j n) -> p j n", j=4)
                return [(v[g * HD:(g + 1) * HD, :, :],
                         wa[g * 4 * HD:(g + 1) * 4 * HD, c0:c0 + 512].rearrange("(j c) n -> c j n", c=HD))
                        for g in range(2)]
            return pieces

        chunks.append(pool_w)
        wp = a["w_pool_branch_2"][layer]
        chunks += [cols(wp, 0, 512, 4), cols(wp, 512, 512, 4), attn_rows(0), attn_rows(512)]
        chunks += [cols(a["w_out_2"][layer], c * CHUNK) for c in range(4)]
        return chunks

    queue_stage([cols(a["ab_w_in"], c * CHUNK) for c in (2, 3, 6, 7, 8, 9, 4, 5, 0, 1)])
    queue_stage([cols(a["ab_w_out"], c * CHUNK) for c in range(4)])
    queue_stage([cols(a["c_w_in"], c * CHUNK) for c in (4, 5, 6, 7, 0, 1, 2, 3)])

    def lru_w(w):
        return lambda buf: [(buf[:, 0:KD * P].rearrange("p (h d) -> p h d", h=KD),
                             w.rearrange("h c d -> c h d"))]

    queue_stage([lru_w(a["c_w_a"]), lru_w(a["c_w_x"])]
                + [cols(a["c_w_out"], c * CHUNK) for c in range(4)])
    for layer in range(2):
        queue_ffn(layer, 0)
        queue_stage(mixer2_chunks(layer))
        queue_ffn(layer, 1)

    for s in range(RING):
        dense_load(s, slot_queue[s].pop(0))
    ws_rows = work[:, 6144:6144 + NA * P].rearrange("p (h s) -> p h s", h=NA)
    ws_loaded = load("ws", ws_rows, a["a_ws"].rearrange("h t s -> t h s"))
    for s in range(RING):
        expert_load(0, 0, s)

    PE.wait(consts_loaded)
    DVE.wait(consts_loaded, small_loaded)
    ACT.wait(consts_loaded, small_loaded)
    z_ready = DVE.done(nc.vector.memset(zeros[:, :], 0.0))
    PE.wait(z_ready)

    def copy_out(engine, dst, src):
        return engine.done(nc.scalar.copy(dst, src) if engine is ACT else nc.vector.tensor_copy(dst, src))

    def transpose_block(src_of, dst, n, bank0, width=P, engines=(ACT, DVE)):
        tickets = []
        for b in range((n + 3) // 4):
            m = min(4, n - 4 * b)
            buf = bank[(bank0 + b) % 8]
            PE.wait(buf.free)
            for j in range(m):
                ins = nc.tensor.transpose(buf.ap[:, j * P:(j + 1) * P], src_of(4 * b + j), C("ident"))
            t = PE.done(ins)
            e = engines[b % len(engines)]
            e.wait(t)
            buf.free = copy_out(e, dst[:, 4 * b * P:(4 * b + m) * P], buf.ap[:, 0:m * P])
            tickets.append(buf.free)
        return tickets

    def flat(ap):
        return ap.rearrange("p k t -> p (k t)")

    def rms_norm(gain, halves=None, meanwhile=None):
        ACT.wait(x_state.ready, h_state.free)
        DVE.wait(h_state.free)
        PE.wait(bank[0].free)
        for q in range(4):
            t = ACT.done(nc.scalar.activation(hT[:, 2 * q:2 * q + 2, :], xT[:, 2 * q:2 * q + 2, :], ACTF.Square))
            PE.wait(t)
            for k in (2 * q, 2 * q + 1):
                ins = mm(bank[0].ap[:, 0:T], C("ones"), hT[:, k, :], start=k == 0, stop=k == KD - 1)
        if meanwhile:
            meanwhile()
        DVE.wait(PE.done(ins))
        t = DVE.done(nc.vector.tensor_scalar(rinv[:, :], bank[0].ap[:, 0:T], 1.0 / D, EPS, ALU.mult, ALU.add))
        bank[0].free = t
        ACT.wait(t)
        t = ACT.done(nc.scalar.activation(rinv[:, :], rinv[:, :], ACTF.Sqrt))
        DVE.wait(t)
        DVE.then(nc.vector.reciprocal(rinv[:, :], rinv[:, :]))
        h_state.ready = []
        for k in range(KD):
            h_state.ready.append(DVE.done(nc.vector.scalar_tensor_tensor(
                hT[:, k, :], xT[:, k, :], gain[:, k:k + 1], rinv[:, :], ALU.mult, ALU.mult)))
        if halves:
            h_state.ready = [halve(tuple(h[:, k, :] for h in halves), hT[:, k, :], h_state.ready[k])
                             for k in range(KD)]

    def halve(dst, src, ready, free=None):
        hi, lo = dst
        ACT.wait(ready, free)
        t = ACT.done(nc.scalar.copy(hi, src))
        DVE.wait(t, ready, free)
        return DVE.done(nc.vector.tensor_tensor(lo, src, hi.bitcast(F32), ALU.subtract))

    def products(out, w, x, start, stop, **kw):
        mm(out, w[0], x[0], start=start, stop=False, **kw)
        mm(out, w[0], x[1], start=False, stop=False, **kw)
        return mm(out, w[1], x[0], start=False, stop=stop, **kw)

    def project(n_chunks, rhs, nk, evacuate, bank_of, tiles=2, rhs_ready=None):
        for j in range(n_chunks):
            s = j % RING
            dense_ready(PE, s)
            w = dense_ring[s][:, 0:nk * tiles * P].rearrange("p (k n) -> p k n", k=nk)
            bufs = [bank[b] for b in bank_of(j)]
            for f in range(tiles):
                buf = bufs[f // 2]
                PE.wait(buf.free)
                for k in range(nk):
                    if rhs_ready and f == 0:
                        PE.wait(rhs_ready[k])
                    ins = mm(buf.ap[:, (f % 2) * T:(f % 2 + 1) * T], w[:, k, f * P:(f + 1) * P], rhs(k),
                             start=k == 0, stop=k == nk - 1)
            t = PE.done(ins)
            dense_release(s, t)
            evacuate(j, bufs, t)

    def add_to_x(scale=None):
        def evacuate(j, bufs, t):
            DVE.wait(t)
            xs = flat(xT)[:, j * 2 * T:(j + 1) * 2 * T]
            if scale is None:
                ins = nc.vector.tensor_tensor(xs, bufs[0].ap, xs, ALU.add)
            else:
                ins = nc.vector.scalar_tensor_tensor(xs, bufs[0].ap, scale, xs, ALU.mult, ALU.add)
            bufs[0].free = x_state.ready = DVE.done(ins)
        return evacuate

    PE.wait(x_loaded)
    tk = []
    for tt in range(TT):
        for kq in range(2):
            buf = bank[tt * 2 + kq]
            for j in range(4):
                ins = nc.tensor.transpose(buf.ap[:, j * P:(j + 1) * P],
                                          x_tok[:, tt, (kq * 4 + j) * P:(kq * 4 + j + 1) * P], C("ident"))
            t = PE.done(ins)
            e = (ACT, DVE)[kq]
            e.wait(t)
            buf.free = copy_out(e, xT[:, kq * 4:kq * 4 + 4, tt * P:(tt + 1) * P],
                                buf.ap.rearrange("p (j t) -> p j t", j=4))
            tk.append(buf.free)
    x_state.ready = tk
    work_state.free = [PE.last()] + tk
    DVE.wait(tk)

    def mixer_ab():
        def tile(at, n, w=T):
            return work[:, at:at + n * w].rearrange("p (k t) -> p k t", k=n)
        yT = tile(0, KD)
        v_tok = tile(2048, TT, D_A)
        PAD = 2
        gx = tile(3072, NA, T + PAD)
        acc = tile(3072 + NA * (T + PAD), NA)
        wsT = work[:, 5632:5632 + NA * P].rearrange("p (h t) -> p h t", h=NA)
        stat = work[:, 6656:6656 + 16]
        for e in (ACT, DVE):
            e.wait(work_state.free)
        DVE.then(nc.vector.memset(gx[:, :, 0:PAD], 0.0))
        DVE.wait(ws_loaded)
        for h in range(NA):
            t = DVE.done(nc.vector.tensor_tensor(ws_rows[:, h, :], ws_rows[:, h, :], C("causal"), ALU.mult))
        PE.wait(t)
        ws_done = transpose_block(lambda h: ws_rows[:, h, :], flat(wsT), NA, 7, engines=(ACT,))

        v_done = []
        for j in range(2):
            dense_ready(PE, j)
            w = dense_ring[j][:, :].rearrange("p (k n) -> p k n", k=KD)
            buf = bank[1 + j]
            PE.wait(buf.free)
            for tt in range(TT):
                for k in range(KD):
                    PE.wait(h_state.ready[k])
                    ins = mm(buf.ap[:, tt * CHUNK:(tt + 1) * CHUNK], hT[:, k, tt * P:(tt + 1) * P], w[:, k, :],
                             start=k == 0, stop=k == KD - 1)
            t = PE.done(ins)
            dense_release(j, t)
            ACT.wait(t)
            buf.free = ACT.done(nc.scalar.activation(
                v_tok[:, :, j * CHUNK:(j + 1) * CHUNK], buf.ap.rearrange("p (a n) -> p a n", a=TT),
                ACTF.Gelu_apprx_tanh))
            v_done.append(buf.free)

        def layer_norm():
            DVE.wait(v_done)
            cen = tile(0, TT, D_A)
            for tt in range(TT):
                s = stat[:, 4 * tt:4 * tt + 4]
                DVE.then(nc.vector.tensor_reduce(s[:, 0:1], v_tok[:, tt, :], X, ALU.add))
                DVE.then(nc.vector.tensor_scalar(s[:, 0:1], s[:, 0:1], 1.0 / D_A, None, ALU.mult))
                DVE.then(nc.vector.tensor_scalar(v_tok[:, tt, :], v_tok[:, tt, :], s[:, 0:1], None, ALU.subtract))
                DVE.then(nc.vector.tensor_tensor(cen[:, tt, :], v_tok[:, tt, :], v_tok[:, tt, :], ALU.mult))
                DVE.then(nc.vector.tensor_reduce(s[:, 1:2], cen[:, tt, :], X, ALU.add))
                t = DVE.done(nc.vector.tensor_scalar(s[:, 1:2], s[:, 1:2], 1.0 / D_A, EPS, ALU.mult, ALU.add))
                ACT.wait(t)
                t = ACT.done(nc.scalar.activation(s[:, 2:3], s[:, 1:2], ACTF.Sqrt))
                DVE.wait(t)
                DVE.then(nc.vector.reciprocal(s[:, 3:4], s[:, 2:3]))
                t = DVE.then(nc.vector.scalar_tensor_tensor(v_tok[:, tt, :], v_tok[:, tt, :], s[:, 3:4],
                                                            S("a_ln_g"), ALU.mult, ALU.mult))
            return t
        state = {}

        def evacuate(j, bufs, t):
            jj, src = j % 2, bufs[0].ap
            src2 = src.rearrange("p (f t) -> p f t", f=2)
            part = slice(2 * jj, 2 * jj + 2)
            kind = j // 2
            if kind == 0:
                ACT.wait(t)
                bufs[0].free = ACT.done(nc.scalar.copy(acc[:, part, :], src2))
                state["gc", jj] = bufs[0].free
            elif kind == 1:
                DVE.wait(t, state["gc", jj])
                bufs[0].free = DVE.then(nc.vector.tensor_tensor(gx[:, part, PAD:], src2, acc[:, part, :], ALU.mult))
                for c in (2 * jj, 2 * jj + 1):
                    DVE.then(nc.vector.tensor_scalar(acc[:, c, :], gx[:, c, 0:T], S("b_conv_w", c, 1), None, ALU.mult))
                    for tap in (1, 2):
                        DVE.then(nc.vector.scalar_tensor_tensor(
                            acc[:, c, :], gx[:, c, tap:tap + T], S("b_conv_w", tap * NA + c, 1),
                            acc[:, c, :], ALU.mult, ALU.add))
            elif kind == 2:
                if jj == 0:
                    state["ln"] = layer_norm()
                DVE.wait(t)
                bufs[0].free = DVE.done(nc.vector.tensor_tensor(
                    yT[:, NA + 2 * jj:NA + 2 * jj + 2, :], src2, acc[:, part, :], ALU.mult))
                state["yb"] = bufs[0].free
            else:
                ACT.wait(t, state["ln"])
                bufs[0].free = ACT.done(nc.scalar.activation(yT[:, part, :], src2, ACTF.Gelu_apprx_tanh))
                state["u"] = bufs[0].free

        def seq(n):
            return [3 + n % 4]
        for j in range(8):
            s = (j + 2) % RING
            dense_ready(PE, s)
            w = dense_ring[s][:, :].rearrange("p (k n) -> p k n", k=KD)
            buf = bank[seq(j)[0]]
            PE.wait(buf.free)
            for f in range(2):
                for k in range(KD):
                    ins = mm(buf.ap[:, f * T:(f + 1) * T], w[:, k, f * P:(f + 1) * P], hT[:, k, :],
                             start=k == 0, stop=k == KD - 1)
            t = PE.done(ins)
            dense_release(s, t)
            evacuate(j, [buf], t)
        h_state.free = PE.last()
        PE.wait(state["ln"], ws_done, bank[0].free, bank[1].free)
        for h in range(NA):
            for c in range(TT):
                ins = mm(bank[h // 2].ap[:, (h % 2) * T + c * P:(h % 2) * T + (c + 1) * P],
                         v_tok[:, c, h * P:(h + 1) * P], wsT[:, h, :], start=True, stop=True)
        t = PE.done(ins)
        DVE.wait(t, state["u"], DVE.last())
        y_ready = []
        for h in range(NA):
            m = bank[h // 2].ap[:, (h % 2) * T:(h % 2 + 1) * T].rearrange("p (c t) -> p c t", c=TT)
            bias = S("a_ws_b", h * P, P).unsqueeze(1).to_broadcast([P, TT, P])
            tmp = acc[:, h, :].rearrange("p (c t) -> p c t", c=TT)
            DVE.then(nc.vector.tensor_tensor(tmp, m, bias, ALU.add))
            y_ready.append(DVE.done(nc.vector.tensor_tensor(yT[:, h, :], acc[:, h, :], yT[:, h, :], ALU.mult)))
        bank[0].free = bank[1].free = y_ready[-1]
        y_ready += [state["yb"]] * NA
        project(4, lambda k: yT[:, k, :], KD, add_to_x(), lambda j: [2 + j % 4], rhs_ready=y_ready)
        work_state.free = [PE.last(), DVE.last(), ACT.last()]

    def mixer_rglru():
        def tile(at, n=KD, w=T):
            return work[:, at:at + n * w].rearrange("p (k t) -> p k t", k=n)
        PAD = 3
        gate = tile(0)
        pad = tile(2048, KD, T + PAD)
        bx = tile(2048)
        xr = tile(2048 + KD * (T + PAD))
        ra = tile(2048 + KD * (T + PAD) + KD * T)
        cst = work[:, 8256:8256 + 6 * KD].rearrange("p (n k) -> p n k", k=KD)
        for e in compute:
            e.wait(work_state.free)
        DVE.then(nc.vector.memset(pad[:, :, 0:PAD], 0.0))
        lam = S("c_lambda")
        y, s, s2, pol = (cst[:, n, :] for n in range(1, 5))
        DVE.then(nc.vector.tensor_scalar(s, lam, -1.0, None, ALU.mult))
        t = DVE.then(nc.vector.tensor_tensor(s, s, lam, ALU.min))
        ACT.wait(t)
        t = ACT.done(nc.scalar.activation(y, s, ACTF.Exp))
        DVE.wait(t)
        DVE.then(nc.vector.tensor_scalar(s, y, 2.0, None, ALU.add))
        DVE.then(nc.vector.reciprocal(s, s))
        DVE.then(nc.vector.tensor_tensor(s, s, y, ALU.mult))
        DVE.then(nc.vector.tensor_tensor(s2, s, s, ALU.mult))
        terms = 9
        DVE.then(nc.vector.tensor_scalar(pol, s2, 1.0 / (2 * terms + 1), 1.0 / (2 * terms - 1), ALU.mult, ALU.add))
        for n in range(terms - 2, -1, -1):
            DVE.then(nc.vector.tensor_tensor(pol, pol, s2, ALU.mult))
            DVE.then(nc.vector.tensor_scalar(pol, pol, 1.0 / (2 * n + 1), None, ALU.add))
        DVE.then(nc.vector.tensor_tensor(pol, pol, s, ALU.mult))
        DVE.then(nc.vector.tensor_scalar(s, lam, 0.0, None, ALU.min))
        DVE.then(nc.vector.scalar_tensor_tensor(pol, pol, -2.0, s, ALU.mult, ALU.add))
        DVE.then(nc.vector.tensor_scalar(cst[:, 0, :], pol, 8.0, None, ALU.mult))
        DVE.then(nc.vector.tensor_scalar(cst[:, 4, :], S("c_b_a"), 0.5, None, ALU.mult))
        half_b = DVE.then(nc.vector.tensor_scalar(cst[:, 5, :], S("c_b_x"), 0.5, None, ALU.mult))

        xr_ready = {}

        def evacuate(j, bufs, t):
            part, src = slice(2 * (j % 4), 2 * (j % 4) + 2), bufs[0].ap.rearrange("p (f t) -> p f t", f=2)
            ACT.wait(t)
            if j >= 4:
                bufs[0].free = ACT.done(nc.scalar.activation(gate[:, part, :], src, ACTF.Gelu_apprx_tanh))
                return
            bufs[0].free = ACT.done(nc.scalar.copy(pad[:, part, PAD:], src))
            DVE.wait(bufs[0].free)
            for c in (2 * j, 2 * j + 1):
                DVE.then(nc.vector.tensor_scalar(xr[:, c, :], pad[:, c, 0:T], S("c_conv_w", c, 1),
                                                 S("c_conv_b", c, 1), ALU.mult, ALU.add))
                for tap in (1, 2, 3):
                    xr_ready[c] = DVE.then(nc.vector.scalar_tensor_tensor(
                        xr[:, c, :], pad[:, c, tap:tap + T], S("c_conv_w", tap * KD + c, 1),
                        xr[:, c, :], ALU.mult, ALU.add))
        project(8, lambda k: hT[:, k, :], KD, evacuate, lambda j: [1 + j % 6], rhs_ready=h_state.ready)
        h_state.free = PE.last()
        gate_ready = ACT.last()
        ACT.wait(half_b, DVE.last())
        for m in range(2):
            dense_ready(PE, m)
            w = dense_ring[m][:, 0:KD * P].rearrange("p (h d) -> p h d", h=KD)
            for h in range(KD):
                buf = bank[h]
                PE.wait(xr_ready[h], buf.free)
                ins = mm(buf.ap[:, 0:T], w[:, h, :], xr[:, h, :], start=True, stop=True)
                t = PE.done(ins)
                ACT.wait(t)
                dst = (ra, bx)[m]
                buf.free = tt_ = ACT.done(nc.scalar.activation(
                    dst[:, h, :], buf.ap[:, 0:T], ACTF.Tanh, bias=cst[:, 4 + m, h:h + 1], scale=0.5))
            dense_release(m, t)
        DVE.wait(tt_)
        DVE.then(nc.vector.tensor_scalar(flat(ra), flat(ra), 0.5, 0.5, ALU.mult, ALU.add))
        for h in range(KD):
            t = DVE.done(nc.vector.tensor_scalar(ra[:, h, :], ra[:, h, :], cst[:, 0, h:h + 1], None, ALU.mult))
        DVE.wait(t)
        ACT.wait(t, h_state.free)
        hf = flat(hT)
        t1 = ACT.done(nc.scalar.activation(hf, flat(ra), ACTF.Tanh, scale=-1.0))
        t2 = ACT.done(nc.scalar.activation(flat(ra), flat(ra), ACTF.Exp))
        DVE.then(nc.vector.tensor_scalar(flat(bx), flat(bx), 0.5, 0.5, ALU.mult, ALU.add))
        DVE.then(nc.vector.tensor_tensor(flat(bx), flat(bx), flat(xr), ALU.mult))
        DVE.wait(t1, t2)
        DVE.then(nc.vector.tensor_tensor(flat(xr), flat(ra), flat(ra), ALU.mult))
        DVE.then(nc.vector.scalar_tensor_tensor(flat(xr), flat(xr), 1.0, hf, ALU.add, ALU.mult))
        t = DVE.last()
        ACT.wait(t)
        t = ACT.done(nc.scalar.activation(flat(xr), flat(xr), ACTF.Sqrt))
        DVE.wait(t, gate_ready)
        DVE.then(nc.vector.tensor_tensor(flat(bx), flat(bx), flat(xr), ALU.mult))
        y_ready = []
        for h in range(KD):
            DVE.then(nc.vector.tensor_tensor_scan(xr[:, h, :], ra[:, h, :], bx[:, h, :], 0.0, ALU.mult, ALU.add))
            y_ready.append(DVE.done(nc.vector.tensor_tensor(gate[:, h, :], gate[:, h, :], xr[:, h, :], ALU.mult)))
        for j in range(4):
            s = 2 + j
            dense_ready(PE, s)
            w = dense_ring[s][:, :].rearrange("p (k n) -> p k n", k=KD)
            buf = bank[j]
            PE.wait(buf.free)
            for f in range(2):
                for k in range(KD):
                    PE.wait(y_ready[k])
                    ins = mm(buf.ap[:, f * T:(f + 1) * T], w[:, k, f * P:(f + 1) * P], gate[:, k, :],
                             start=k == 0, stop=k == KD - 1)
            t = PE.done(ins)
            dense_release(s, t)
            add_to_x()(j, [buf], t)
        work_state.free = [PE.last(), DVE.last(), ACT.last()]
        h_state.free = [PE.last(), DVE.last()]

    def moe(layer):
        NG, NE = N_GROUPS, N_EXP
        at = [0]

        def wk(n):
            at[0] += n
            assert at[0] <= WORK_F
            return work[:, at[0] - n:at[0]]
        h_tok = wk(TT * D)
        xs = wk(KD * P).rearrange("p (k c) -> p k c", k=KD)
        y_slots = wk(D)
        silu_g = [wk(2 * P) for _ in range(2)]
        hid = [wk(2 * P) for _ in range(2)]
        hidT = [wk(2 * P) for _ in range(2)]
        pick = wk(TT * P)
        pick_g = wk(TT * P)
        spread = wk(T)
        w_route = wk(KD * (NG + NE))
        lg = wk(TT * (NG + NE)).rearrange("p (a n) -> p a n", a=TT)
        posm, gates, chosen, tmp_e, one1 = (wk(TT * NE).rearrange("p (a n) -> p a n", a=TT) for _ in range(5))
        gmx = wk(TT * 8).rearrange("p (a n) -> p a n", a=TT)
        goh = wk(TT * NG).rearrange("p (a n) -> p a n", a=TT)
        flag = most_tokens[:, layer:layer + 1]
        for e in compute:
            e.wait(work_state.free)
        SP.wait(work_state.free)
        wr = w_route.rearrange("p (k n) -> p k n", k=KD)
        load("route", wr[:, :, 0:NG], a["moe_w_rg"][layer].rearrange("(k p) n -> p k n", p=P))
        w_loaded = load("route", wr[:, :, NG:], a["moe_w_re"][layer].rearrange("(k p) n -> p k n", p=P))

        rms_norm(S("norm_ffn_g", layer * KD, KD))
        PE.wait(h_state.ready)
        h_done = transpose_block(lambda i: hT[:, i % KD, (i // KD) * P:(i // KD + 1) * P], h_tok, TT * KD, 1)
        PE.wait(w_loaded, bank[6].free)
        n = NG + NE
        for tt in range(TT):
            for k in range(KD):
                ins = mm(bank[6].ap[:, tt * n:(tt + 1) * n], hT[:, k, tt * P:(tt + 1) * P], wr[:, k, :],
                         start=k == 0, stop=k == KD - 1)
        t = PE.done(ins)
        h_state.free = t
        DVE.wait(t)
        V = nc.vector
        bias = S("moe_b", layer * n, n).unsqueeze(1).to_broadcast([P, TT, n])
        bank[6].free = DVE.then(V.tensor_tensor(lg, bank[6].ap[:, 0:TT * n].rearrange("p (a n) -> p a n", a=TT), bias, ALU.add))

        def bc(ap, m):
            return ap.to_broadcast([P, TT, m])

        def first_max(dst, values, rank, m, mx, mi):
            DVE.then(V.tensor_reduce(mx, values, X, ALU.max))
            DVE.then(V.tensor_tensor(dst, values, bc(mx, m), ALU.is_equal))
            DVE.then(V.tensor_tensor(dst, dst, rank.unsqueeze(1).to_broadcast([P, TT, m]), ALU.mult))
            DVE.then(V.tensor_reduce(mi, dst, X, ALU.max))
            DVE.then(V.tensor_tensor(dst, dst, bc(mi, m), ALU.is_equal))

        g = lg[:, :, 0:NG]
        col = [gmx[:, :, i:i + 1] for i in range(8)]
        first_max(goh, g, C("rank_g"), NG, col[0], col[1])
        t = DVE.then(V.tensor_tensor(g, g, bc(col[0], NG), ALU.subtract))
        ACT.wait(t)
        t = ACT.done(nc.scalar.activation(g, g, ACTF.Exp))
        DVE.wait(t)
        DVE.then(V.tensor_reduce(col[2], g, X, ALU.add))
        DVE.then(V.reciprocal(col[2], col[2]))
        e4 = lg[:, :, NG:].rearrange("p a (g j) -> p a g j", g=NG)
        in_g = goh.unsqueeze(3).to_broadcast([P, TT, NG, PER_GROUP])
        DVE.then(V.tensor_scalar(tmp_e.rearrange("p a (g j) -> p a g j", g=NG), in_g, -1.0, -NEG, ALU.add, ALU.mult))
        for tt in range(TT):
            t = DVE.done(V.tensor_tensor(e4[:, tt], e4[:, tt], in_g[:, tt], ALU.mult))
        DVE.wait(t)
        ev = lg[:, :, NG:]
        DVE.then(V.tensor_tensor(ev, ev, tmp_e, ALU.add))
        first_max(one1, ev, C("rank_e"), NE, col[3], col[1])
        DVE.then(V.tensor_scalar(tmp_e, one1, 2 * NEG, None, ALU.mult))
        DVE.then(V.tensor_tensor(ev, ev, tmp_e, ALU.add))
        first_max(tmp_e, ev, C("rank_e"), NE, col[4], col[1])
        t = DVE.then(V.tensor_tensor(col[4], col[4], col[3], ALU.subtract))
        ACT.wait(t)
        t = ACT.done(nc.scalar.activation(col[4], col[4], ACTF.Exp))
        DVE.wait(t)
        DVE.then(V.tensor_scalar(col[5], col[4], 1.0, None, ALU.add))
        DVE.then(V.reciprocal(col[5], col[5]))
        DVE.then(V.tensor_tensor(col[5], col[5], col[2], ALU.mult))
        DVE.then(V.tensor_tensor(col[4], col[4], col[5], ALU.mult))
        DVE.then(V.tensor_tensor(chosen, one1, tmp_e, ALU.add))
        DVE.then(V.tensor_tensor(gates, one1, bc(col[5], NE), ALU.mult))
        DVE.then(V.tensor_tensor(tmp_e, tmp_e, bc(col[4], NE), ALU.mult))
        t = DVE.then(V.tensor_tensor(gates, gates, tmp_e, ALU.add))
        PE.wait(t, bank[7].free)
        B7 = bank[7].ap
        mm(B7[:, 0:NE], C("before"), chosen[:, 0, :], start=True, stop=True)
        mm(B7[:, NE:2 * NE], C("ones"), chosen[:, 0, :], start=True, stop=False)
        mm(B7[:, NE:2 * NE], C("before"), chosen[:, 1, :], start=False, stop=True)
        mm(B7[:, 2 * NE:3 * NE], C("ones"), chosen[:, 0, :], start=True, stop=False)
        t = PE.done(mm(B7[:, 2 * NE:3 * NE], C("ones"), chosen[:, 1, :], start=False, stop=True))
        DVE.wait(t)
        r2 = B7[:, 0:TT * NE].rearrange("p (a n) -> p a n", a=TT)
        DVE.then(V.scalar_tensor_tensor(posm, r2, 1.0, chosen, ALU.add, ALU.mult))
        DVE.then(V.tensor_scalar(posm, posm, -1.0, None, ALU.add))
        DVE.then(V.tensor_reduce(col[6][:, 0], B7[:, 2 * NE:3 * NE], X, ALU.max))
        flag_ready = DVE.then(V.tensor_copy(flag[:, 0:1], col[6][:, 0]))
        bank[7].free = flag_ready

        DVE.wait(h_done)
        ACT.wait(h_done)
        PE.wait(h_done)
        for b in bank:
            PE.wait(b.free)
            b.free = None
        start = [DVE.last(), ACT.last(), PE.last()]
        for e in compute:
            e.wait(start)
        iota = C("iota").unsqueeze(1).to_broadcast([P, QUAD, CAP])
        ends = {}

        def quad_body(quad, counts, release, before):
            DVE.wait(before("pick", PE), before("pick_dve", DVE))
            es = bass.ds(quad * QUAD, QUAD)
            for tt in range(TT):
                slot_of = posm[:, tt, es].unsqueeze(2).to_broadcast([P, QUAD, CAP])
                gate_of = gates[:, tt, es].unsqueeze(2).to_broadcast([P, QUAD, CAP])
                d = pick[:, tt * P:(tt + 1) * P].rearrange("p (e c) -> p e c", e=QUAD)
                dg = pick_g[:, tt * P:(tt + 1) * P].rearrange("p (e c) -> p e c", e=QUAD)
                DVE.then(V.tensor_tensor(d, slot_of, iota, ALU.is_equal))
                picked = DVE.done(V.tensor_tensor(dg, d, gate_of, ALU.mult))
            ends["pick_dve"] = picked
            PE.wait(picked)
            xs_ready = []
            for k in range(KD):
                b = k // 4
                if k % 4 == 0:
                    PE.wait(before(f"bank{b}", DVE))
                for tt in range(TT):
                    ins = mm(bank[b].ap[:, (k % 4) * P:(k % 4 + 1) * P],
                             h_tok[:, tt * D + k * P:tt * D + (k + 1) * P],
                             pick[:, tt * P:(tt + 1) * P], start=tt == 0, stop=tt == TT - 1)
                if k % 4 == 3:
                    t = PE.done(ins)
                    e = (ACT, DVE)[b]
                    e.wait(t, before("xs", PE))
                    xs_ready.append(copy_out(e, xs.rearrange("p k c -> p (k c)")[:, (k - 3) * P:(k + 1) * P], bank[b].ap))
            PE.wait(before("bank5", DVE))
            for tt in range(TT):
                ins = nc.tensor.transpose(bank[5].ap[:, tt * P:(tt + 1) * P], pick_g[:, tt * P:(tt + 1) * P], C("ident"))
            t = ends["pick"] = PE.done(ins)
            ACT.wait(t, before("spread", PE))
            spread_ready = copy_out(ACT, spread, bank[5].ap[:, 0:T])
            PE.wait(xs_ready)
            for pair in range(2):
                b = bank[2 + pair]
                PE.wait(before(f"bank{2 + pair}", DVE))
                half = D_EXP // 2
                for m in range(2):
                    for x in range(2):
                        PE.wait(pr.now(counts[2 * m + x]))
                    for k in range(KD):
                        for x in range(2):
                            w = expert_ring[2 * m + x].rearrange("p (k n) -> p k n", k=KD)
                            slots = xs[:, k, (2 * pair + x) * CAP:(2 * pair + x + 1) * CAP]
                            for hf in range(2):
                                c = (2 * x + hf) * CAP
                                ins = mm(b.ap[c:c + CAP, m * half:(m + 1) * half], slots,
                                         w[:, k, hf * half:(hf + 1) * half], start=k == 0, stop=k == KD - 1)
                    t = PE.done(ins)
                    for x in range(2):
                        release(quad * 2 + pair, 2 * m + x, t)
                if pair == 1:
                    ends["xs"] = t
                ACT.wait(t, before(f"silu{pair}", DVE))
                silu_ready = ACT.done(nc.scalar.activation(silu_g[pair], b.ap[:, 0:half], ACTF.Silu))
                DVE.wait(silu_ready, before(f"hid{pair}", PE))
                t = DVE.done(V.tensor_tensor(hid[pair], silu_g[pair], b.ap[:, half:], ALU.mult))
                ends[f"bank{2 + pair}"] = ends[f"silu{pair}"] = t
                PE.wait(t, before("bank4", DVE) if pair == 0 else hidT_ready)
                for q in range(2):
                    ins = nc.tensor.transpose(bank[4].ap[:, q * P:(q + 1) * P], hid[pair][:, q * P:(q + 1) * P], C("ident"))
                t = ends[f"hid{pair}"] = PE.done(ins)
                DVE.wait(t, before(f"hidT{pair}", PE))
                hidT_ready = copy_out(DVE, hidT[pair], bank[4].ap[:, 0:2 * P])
                PE.wait(hidT_ready, before("y_bank", ACT), before("y_bank_dve", DVE))
                for x in range(2):
                    PE.wait(pr.now(counts[4 + x]))
                for n in range(2):
                    for f in range(FE):
                        for x in range(2):
                            w = expert_ring[4 + x].rearrange("p (k n) -> p k n", k=FE)
                            c = (f % 2) * P + x * 2 * CAP + (f // 2) * CAP
                            r0 = (2 * pair + x) * CAP
                            ins = mm(bank[6 + n].ap[r0:r0 + CAP, :], hidT[pair][:, c:c + CAP],
                                     w[:, f, n * 512:(n + 1) * 512], start=f == 0, stop=f == FE - 1)
                t = ends[f"hidT{pair}"] = PE.done(ins)
                for x in range(2):
                    release(quad * 2 + pair, 4 + x, t)
            ACT.wait(t, before("y", PE))
            y_ready = [copy_out(ACT, y_slots[:, 0:512], bank[6].ap)]
            ends["y_bank"] = y_ready[0]
            DVE.wait(t, before("y", PE))
            y_ready.append(copy_out(DVE, y_slots[:, 512:1024], bank[7].ap))
            ends["y_bank_dve"] = y_ready[1]
            PE.wait(y_ready, spread_ready)
            for q, bn in enumerate((5, 0, 1, 4)):
                b = bank[bn]
                for j in range(2):
                    ins = mm(b.ap[:, j * T:(j + 1) * T], y_slots[:, (2 * q + j) * P:(2 * q + j + 1) * P], spread,
                             start=True, stop=True)
                t = PE.done(ins)
                DVE.wait(t, before("x_dve", DVE) if q == 0 else None)
                xsl = flat(xT)[:, q * 2 * T:(q + 1) * 2 * T]
                ends[f"bank{bn}"] = ends["x_dve"] = DVE.done(V.tensor_tensor(xsl, b.ap, xsl, ALU.add))
            ends["y"] = ends["spread"] = t

        DVE.wait(x_state.ready)
        with pr.loop(f"quads{layer}", QUADS - 1) as lp:
            def load_next(pair, s, t):
                SP.wait(t)
                expert_load(layer, pair + 1, s)
            quad_body(lp.i, exp_count, load_next, lambda name, e: lp.last_time(name))
            lp.leave(ends)
        closed = dict(ends)

        def load_last(pair, s, t):
            if pair == 2 * QUADS - 2:
                load_next(pair, s, t)
        quad_body(QUADS - 1, exp_count, load_last, lambda name, e: closed[name])

        def more(tag, above, passes):
            for e in pr.engines:
                e.wait(flag_ready, PE.last(), ACT.last(), DVE.last())
            most = nc.values_load(flag[0:1, 0:1], min_val=0, max_val=T)
            keep = [(e, e.count, dict(e.seen)) for e in pr.engines]
            with nc.If(most > above):
                for e in pr.engines:
                    e.count = pr.counter(f"{e.name}_{tag}{layer}")
                counts = [pr.counter(f"expert{s}_{tag}{layer}", 16) for s in range(RING)]

                def one_pass():
                    DVE.then(V.tensor_scalar(posm, posm, -float(CAP), None, ALU.add))
                    DVE.step()
                    with pr.loop(f"quads_{tag}{layer}", QUADS) as lq:
                        for s in range(RING):
                            expert_load(layer, lq.i * 2, s, counts)

                        def load_second(pair, s, t):
                            if len(seconds) < RING:
                                seconds.append(s)
                                SP.wait(t)
                                expert_load(layer, pair + 1, s, counts)
                        seconds = []
                        quad_body(lq.i, counts, load_second, lambda name, e: None)
                        turn = [PE.last(), ACT.last(), DVE.last()]
                        for e in (PE, ACT, DVE, SP):
                            e.wait(turn)
                            e.step()
                if passes == 1:
                    one_pass()
                else:
                    with pr.loop(f"passes_{tag}{layer}", passes):
                        one_pass()
            for e, c, seen in keep:
                e.count, e.seen = c, seen
        more("more", CAP, 1)
        more("rest", 2 * CAP, T // CAP - 2)
        x_state.ready = DVE.last()
        if layer == 0:
            for s in range(RING):
                expert_load(1, 0, s)
        for b in bank:
            b.free = DVE.last()
        for e in compute:
            e.wait(DVE.last(), ACT.last(), PE.last())
        work_state.free = [PE.last(), DVE.last(), ACT.last()]

    b2 = {}

    def open_block2():
        block1_memory.close()
        for name, n in (("hi", RING_F), ("lo", RING_F)):
            b2["w_" + name] = [sb(f"w_{name}{i}", n, F32R) for i in range(2)]
            b2["h_" + name] = sb("h_" + name, KD * T, F32R)[:, :].rearrange("p (k t) -> p k t", k=KD)
            b2["hid_" + name] = [sb(f"hid_{name}{i}", GF * T, F32R) for i in range(2)]
        b2["scratch"] = sb("scratch", SCRATCH_F)
        b2["h"] = (b2["h_hi"], b2["h_lo"])
        for i in range(2):
            for f in range(2):
                tickets[f"w_free{i}{f}"] = PE.last()
        for e in compute:
            e.wait(PE.last(), ACT.last(), DVE.last())

    tickets = {}
    turn_of = [0]

    def half_view(buf, by_rows, f):
        if by_rows:
            return buf[:, f * D:(f + 1) * D]
        return buf[:, :].rearrange("p (k n) -> p k n", k=KD)[:, :, f * P:(f + 1) * P]

    def halve_chunk(s, release, by_rows=False):
        i = turn_of[0] % 2
        turn_of[0] += 1
        dense_ready(ACT, s)
        dense_ready(DVE, s)
        for f in range(2):
            src = half_view(dense_ring[s], by_rows, f)
            dst = tuple(b2["w_" + n][i][:, f * D:(f + 1) * D] for n in ("hi", "lo"))
            if not by_rows:
                dst = tuple(d.rearrange("p (k n) -> p k n", k=KD) for d in dst)
            tickets[f"w_ready{i}{f}"] = halve(dst, src, None, tickets[f"w_free{i}{f}"])
        release(s, [ACT.last(), tickets[f"w_ready{i}1"]])
        return i

    def halved(i):
        return tuple(b2["w_" + h][i][:, :].rearrange("p (f j n) -> p f j n", f=2, n=P) for h in ("hi", "lo"))

    def tile_products(i, buf, x, x_ready):
        w = halved(i)
        PE.wait(buf.free)
        for f in range(2):
            PE.wait(tickets[f"w_ready{i}{f}"])
            for k in range(KD):
                PE.wait(x_ready[k])
                ins = products(buf.ap[:, f * T:(f + 1) * T], tuple(v[:, f, k, :] for v in w),
                               tuple(v[:, k, :] for v in x), k == 0, k == KD - 1)
            t = tickets[f"w_free{i}{f}"] = PE.done(ins)
        return t

    silu_f = [work[:, i * GF * T:(i + 1) * GF * T] for i in range(2)]
    hid_f = [work[:, (2 + i) * GF * T:(3 + i) * GF * T] for i in range(2)]

    def ffn(layer, which, gain):
        gu, dn = (w[layer] for w in ffn_w[which])
        first = []

        def load_group(ahead, base=0):
            def go(s, t):
                SP.wait(t)
                g = base + ahead
                m = s % 3
                dense_load(s, rows(dn, g) if m == 2 else cols_at(gu, g, 0 if m == 0 else D_FF))
            return go

        rms_norm(gain, b2["h"], lambda: first.extend([halve_chunk(0, load_group(2)), halve_chunk(1, load_group(2))]))
        for e in compute:
            e.wait(work_state.free)
        acc = [bank[4 + q] for q in range(4)]
        for b in acc:
            PE.wait(b.free)
            mm(b.ap, zeros[:, 0:P], zeros[:, :], start=True, stop=False, skip_group_check=True)
        for par in range(2):
            tickets[f"gate_bank{par}"], tickets[f"up_bank{par}"] = bank[2 * par].free, bank[2 * par + 1].free
            tickets[f"hid_free{par}"] = tickets[f"hid_ready{par}"] = None

        def gate(par, i):
            b = bank[2 * par]
            b.free = tickets[f"gate_bank{par}"]
            return tile_products(i, b, b2["h"], h_state.ready)

        def silu(par, t):
            ACT.wait(t, tickets[f"up_bank{par}"])
            t = ACT.done(nc.scalar.activation(silu_f[par], bank[2 * par].ap, ACTF.Silu))
            tickets[f"gate_bank{par}"] = t

        def up(par, i):
            b = bank[2 * par + 1]
            b.free = tickets[f"up_bank{par}"]
            return tile_products(i, b, b2["h"], h_state.ready)

        def hidden(par, t):
            DVE.wait(t, tickets[f"gate_bank{par}"], tickets[f"hid_ready{par}"])
            t = tickets[f"up_bank{par}"] = DVE.done(nc.vector.tensor_tensor(
                hid_f[par], silu_f[par], bank[2 * par + 1].ap, ALU.mult))
            tickets[f"hid_ready{par}"] = halve((b2["hid_hi"][par][:, :], b2["hid_lo"][par][:, :]), hid_f[par], t,
                                               tickets[f"hid_free{par}"])

        def down(par, i):
            w = halved(i)
            PE.wait(tickets[f"hid_ready{par}"])
            for f in range(GF):
                PE.wait(tickets[f"w_ready{i}{f}"])
                for k in range(KD):
                    ins = products(acc[k // 2].ap[:, (k % 2) * T:(k % 2 + 1) * T],
                                   tuple(v[:, f, k, :] for v in w),
                                   tuple(b2["hid_" + n][par][:, f * T:(f + 1) * T] for n in ("hi", "lo")),
                                   False, False, skip_group_check=True)
                tickets[f"w_free{i}{f}"] = PE.done(ins)
            tickets[f"hid_free{par}"] = PE.last()

        t = gate(0, first[0])
        g1 = halve_chunk(3, load_group(3))
        silu(0, t)
        t = up(0, first[1])
        u1 = halve_chunk(4, load_group(3))
        hidden(0, t)

        def turn(g1, u1, base, release):
            t = gate(1, g1)
            d0 = halve_chunk(2, release(2), True)
            silu(1, t)
            t = up(1, u1)
            g2 = halve_chunk(0, release(4))
            hidden(1, t)
            down(0, d0)
            u2 = halve_chunk(1, release(4))
            t = gate(0, g2)
            d1 = halve_chunk(5, release(3), True)
            silu(0, t)
            t = up(0, u2)
            g3 = halve_chunk(3, release(5)) if base is not None else None
            hidden(0, t)
            if base is None:
                d2 = halve_chunk(2, release(0), True)
            down(1, d1)
            if base is None:
                down(0, d2)
                return
            return g3, halve_chunk(4, release(5))

        turns = (N_GRP - 1) // 2
        with pr.loop(f"ffn{layer}{which}", turns - 2, tickets, compute) as lp:
            assert turn(g1, u1, lp.i * 2, lambda ahead: load_group(ahead, lp.i * 2)) == (g1, u1)
        static = lambda ahead: dense_release
        turn(g1, u1, 0, static)
        turn(g1, u1, None, static)
        DVE.wait(PE.last())
        for q in range(4):
            xsl = flat(xT)[:, q * 2 * T:(q + 1) * 2 * T]
            acc[q].free = x_state.ready = DVE.done(nc.vector.scalar_tensor_tensor(
                xsl, acc[q].ap, 0.5, xsl, ALU.mult, ALU.add))
        for par in range(2):
            bank[2 * par].free, bank[2 * par + 1].free = tickets[f"gate_bank{par}"], tickets[f"up_bank{par}"]
        h_state.free = [PE.last(), DVE.last(), ACT.last()]
        work_state.free = [PE.last(), DVE.last(), ACT.last()]

    def mixer2(layer):
        V = nc.vector
        ahead = []
        rms_norm(S("ln_mix_2", layer * KD, KD), b2["h"],
                 lambda: ahead.extend([halve_chunk(0, dense_release), halve_chunk(1, dense_release)]))
        for e in (PE, ACT, DVE, POOL):
            e.wait(work_state.free)
        at = {"scratch": 0, "work": 0}

        def wk(n, where="scratch"):
            at[where] += n
            return (b2["scratch"] if where == "scratch" else work)[:, at[where] - n:at[where]]
        U = N_HEADS
        L = T + EDGE

        def of_tokens(m):
            return m[:, 0:TT * U * HD].rearrange("p (a u c) -> p a u c", a=TT, u=U)
        heads = wk(2 * TT * U * HD)
        qk = of_tokens(heads)
        qkT = heads[:, TT * U * HD:].rearrange("p (j t) -> p j t", j=U // 2)
        merged = heads[:, 0:KD * T].rearrange("p (k t) -> p k t", k=KD)
        windows = wk(3 * 4 * L)
        uT, s2, s4 = (windows[:, i * 4 * L:(i + 1) * 4 * L].rearrange("p (g t) -> p g t", g=4) for i in range(3))
        pT = windows[:, 0:N_Q * 3 * P]
        sig = wk(16 * T).rearrange("p (k t) -> p k t", k=16)
        p1 = wk(N_Q * 2 * P, "work")
        sq = of_tokens(p1)
        prob = [wk(N_Q * P, "work").rearrange("p (h k) -> p h k", h=N_Q), p1.rearrange("p (h k) -> p h k", h=N_Q)]
        poolT = wk(4 * T, "work").rearrange("p (g t) -> p g t", g=4)
        poolY = wk(4 * T, "work").rearrange("p (g t) -> p g t", g=4)
        oT = wk(4 * T, "work").rearrange("p (j t) -> p j t", j=4)
        v_tok = wk(TT * P, "work").rearrange("p (a c) -> p a c", a=TT)
        small_q = wk(2 * TT * U + 64 + 4 * TT * U * (ROT // 2), "work")
        assert at["scratch"] <= SCRATCH_F and at["work"] <= WORK_F
        ms = small_q[:, 0:TT * U].rearrange("p (a u) -> p a u", a=TT)
        half = ROT // 2
        rt = [small_q[:, 104 + i * TT * U * half:104 + (i + 1) * TT * U * half].rearrange(
            "p (a u c) -> p a u c", a=TT, u=U) for i in range(4)]
        stat = small_q[:, TT * U:TT * U + 64]

        got = {}

        def qkv_products(j):
            w, i = halved(ahead[j]), ahead[j]
            buf = bank[1 + j]
            PE.wait(buf.free, tickets[f"w_ready{i}0"], tickets[f"w_ready{i}1"])
            for tt in range(TT):
                for k in range(KD):
                    PE.wait(h_state.ready[k])
                    ins = products(buf.ap[:, tt * CHUNK:(tt + 1) * CHUNK],
                                   tuple(h[:, k, tt * P:(tt + 1) * P] for h in b2["h"]),
                                   tuple(v[:, :, k, :] for v in w), k == 0, k == KD - 1)
            tickets[f"w_free{i}0"] = tickets[f"w_free{i}1"] = PE.done(ins)
            return tickets[f"w_free{i}0"]

        def qkv_out(j, t):
            buf = bank[1 + j]
            ACT.wait(t)
            for tt in range(TT):
                src = buf.ap[:, tt * CHUNK:(tt + 1) * CHUNK]
                if j < 2:
                    dst = qk[:, tt, 0:N_Q, :].rearrange("p (i g) c -> p i g c", g=2)[:, :, j, :]
                    buf.free = ACT.done(nc.scalar.copy(dst, src.rearrange("p (i c) -> p i c", i=4)))
                else:
                    ACT.done(nc.scalar.copy(qk[:, tt, N_Q:U, :].rearrange("p u c -> p (u c)"), src[:, 0:P]))
                    buf.free = ACT.done(nc.scalar.copy(v_tok[:, tt, :], src[:, P:2 * P]))

        def head_norm_rope():
            ACT.wait(ACT.last())
            DVE.wait(ACT.last())
            qf = qk.rearrange("p a u c -> p (a u) c")
            sf = sq.rearrange("p a u c -> p (a u) c")
            mf = ms.rearrange("p a u -> p (a u)")
            t = ACT.done(nc.scalar.activation(sf, qf, ACTF.Square))
            DVE.wait(t)
            DVE.then(V.tensor_reduce(mf, sf, X, ALU.add))
            t = DVE.then(V.tensor_scalar(mf, mf, 1.0 / HD, EPS, ALU.mult, ALU.add))
            ACT.wait(t)
            t = ACT.done(nc.scalar.activation(mf, mf, ACTF.Sqrt))
            yield
            DVE.wait(t)
            DVE.then(V.reciprocal(mf, mf))
            t = DVE.done(V.tensor_tensor(qf, qf, mf.unsqueeze(2).to_broadcast([P, TT * U, HD]), ALU.mult))
            yield
            DVE.wait(t)
            for tt in range(TT):
                for (u0, u1, g) in ((0, N_Q, "q_norm_2"), (N_Q, U, "k_norm_2")):
                    gain = S(g, layer * HD, HD).unsqueeze(1).to_broadcast([P, u1 - u0, HD])
                    t = DVE.done(V.tensor_tensor(qk[:, tt, u0:u1, :], qk[:, tt, u0:u1, :], gain, ALU.mult))
            yield
            DVE.wait(t)
            x1, x2 = qk[:, :, :, 0:half], qk[:, :, :, half:ROT]
            for tt in range(TT):
                c, s = (C(n)[:, tt * half:(tt + 1) * half].unsqueeze(1).to_broadcast([P, U, half]) for n in ("cos", "sin"))
                for i, (x, f) in enumerate(((x1, c), (x2, s), (x2, c), (x1, s))):
                    t = DVE.done(V.tensor_tensor(rt[i][:, tt], x[:, tt], f, ALU.mult))
            DVE.wait(t)
            for tt in range(TT):
                DVE.done(V.tensor_tensor(x1[:, tt], rt[0][:, tt], rt[1][:, tt], ALU.subtract))
                t = DVE.done(V.tensor_tensor(x2[:, tt], rt[2][:, tt], rt[3][:, tt], ALU.add))
            got["rope"] = t

        def heads_to_features():
            PE.wait(got["rope"])
            for tt in range(TT):
                for j0, j1 in ((0, 4), (4, 5)):
                    buf = bank[1 + 2 * tt + j0 // 4]
                    PE.wait(buf.free)
                    for j in range(j0, j1):
                        ins = nc.tensor.transpose(buf.ap[:, (j - j0) * P:(j - j0 + 1) * P],
                                                  qk[:, tt, 2 * j:2 * j + 2, :].rearrange("p g c -> p (g c)"), C("ident"))
                    t = PE.done(ins)
                    ACT.wait(t)
                    buf.free = copy_out(ACT, qkT[:, j0:j1, tt * P:(tt + 1) * P],
                                        buf.ap[:, 0:(j1 - j0) * P].rearrange("p (j t) -> p j t", t=P))
            return ACT.last()

        def scores():
            PE.wait(got["qkT"])
            for b in (0, 1, 2, 3, 4, 5):
                PE.wait(bank[b].free)
            for j in range(4):
                for g in range(2):
                    r = slice(g * HD, (g + 1) * HD)
                    b1 = bank[2 * g + j // 2].ap
                    mm(b1[:, (j % 2) * 2 * P:(j % 2 + 1) * 2 * P], qkT[r, j, P:2 * P], qkT[r, 4, :],
                       start=True, stop=True)
                    ins = mm(bank[4 + g].ap[:, j * P:(j + 1) * P], qkT[r, j, 0:P], qkT[r, 4, 0:P],
                             start=True, stop=True)
            return PE.done(ins)

        def softmax(blk):
            nm, mx, sk, sm = stat[:, 0:8], stat[:, 8:16], stat[:, 16:24], stat[:, 24:32]
            w = (1 + blk) * P
            pb = prob[blk]
            band = C("band")[:, 2 * P - w:2 * P]
            DVE.wait(got["scores"])
            for q in range(4 if blk else 2):
                nh = 2 if blk else 4
                src = bank[q if blk else 4 + q]
                part = pb[:, q * nh:(q + 1) * nh, :]
                src.free = DVE.done(V.scalar_tensor_tensor(
                    part, src.ap.rearrange("p (h k) -> p h k", h=nh), HD ** -0.5,
                    band.unsqueeze(1).to_broadcast([P, nh, w]), ALU.mult, ALU.add))
            DVE.wait(src.free)
            yield
            DVE.then(V.tensor_reduce(mx, pb, X, ALU.max))
            sink = S("sinks_2", layer * N_Q, N_Q)
            DVE.then(V.tensor_tensor(mx, mx, sink, ALU.max))
            DVE.then(V.tensor_scalar(nm, mx, -1.0, None, ALU.mult))
            t = DVE.then(V.tensor_tensor(sk, sink, mx, ALU.subtract))
            ACT.wait(t)
            for h in range(N_Q):
                ACT.done(nc.scalar.activation(pb[:, h, :], pb[:, h, :], ACTF.Exp, bias=nm[:, h:h + 1],
                                              accum_out=sm[:, h:h + 1]))
            t = ACT.done(nc.scalar.activation(sk, sk, ACTF.Exp))
            yield
            DVE.wait(t)
            DVE.then(V.tensor_tensor(sm, sm, sk, ALU.add))
            DVE.then(V.reciprocal(sm, sm))
            got["prob", blk] = DVE.then(V.tensor_tensor(pb, pb, sm.unsqueeze(2).to_broadcast([P, N_Q, w]), ALU.mult))

        def pooling():
            G = nc.gpsimd
            POOL.wait(u_ready)
            src, dst = uT, s2
            for n, w in enumerate(WINDOWS):
                sh = w // 2
                POOL.then(G.tensor_tensor(dst[:, n:, EDGE:L], src[:, n:, EDGE:L], src[:, n:, EDGE - sh:L - sh], ALU.add))
                POOL.done(G.tensor_scalar(poolT[:, n, EDGE:], dst[:, n, 2 * EDGE:L], 1.0 / w, None, ALU.mult))
                POOL.then(G.tensor_tensor(poolT[:, n, 0:EDGE], dst[:, n, EDGE:2 * EDGE],
                                          C("rcount")[:, n * EDGE:(n + 1) * EDGE], ALU.mult))
                t = POOL.then(G.tensor_tensor(poolT[:, n, :], poolT[:, n, :], uT[:, n, EDGE:L], ALU.subtract))
                src, dst = dst, (s4 if dst is s2 else s2)
            return t

        for buf in (uT, s2, s4):
            t = POOL.done(nc.gpsimd.memset(buf[:, :, 0:EDGE], 0.0))
        POOL.wait(t)
        ACT.wait(t)

        def attention():
            yield from head_norm_rope()
            yield
            got["qkT"] = heads_to_features()
            yield
            got["scores"] = scores()
            for blk in (1, 0):
                yield from softmax(blk)
                yield

        pieces = attention()
        n_in = 13
        for j in range(n_in):
            if j < 3:
                t = qkv_products(j)
            else:
                buf = bank[6 + j % 2]
                t = tile_products(ahead[j], buf, b2["h"], h_state.ready)
            if j + 2 < n_in:
                ahead.append(halve_chunk((j + 2) % RING, dense_release))
            if j < 3:
                qkv_out(j, t)
                continue
            ACT.wait(t)
            src = buf.ap.rearrange("p (f t) -> p f t", f=2)
            if j < 5:
                buf.free = ACT.done(nc.scalar.copy(uT[:, 2 * (j - 3):2 * (j - 3) + 2, EDGE:], src))
            else:
                c = 2 * (j - 5)
                buf.free = ACT.done(nc.scalar.activation(sig[:, c:c + 2, :], src, ACTF.Tanh, scale=0.5))
            if j == 4:
                u_ready = ACT.last()
                got["pool"] = pooling()
            next(pieces, None)
        for _ in pieces:
            pass
        sig_ready = ACT.last()
        halves_free = PE.last()
        dense_ready(PE, 13 % RING)
        wp = dense_ring[13 % RING][:, 0:4 * P].rearrange("p (g d) -> p g d", g=4)
        PE.wait(got["pool"], bank[6].free, bank[7].free)
        for g in range(4):
            ins = mm(bank[6 + g // 2].ap[:, (g % 2) * T:(g % 2 + 1) * T], wp[:, g, :], poolT[:, g, :], start=True, stop=True)
        t = PE.done(ins)
        dense_release(13 % RING, t)
        DVE.wait(t)
        for g in range(4):
            b = bank[6 + g // 2]
            b.free = DVE.done(V.tensor_scalar(poolY[:, g, :], b.ap[:, (g % 2) * T:(g % 2 + 1) * T],
                                              S("pool_scale_2", layer * 4 + g, 1), None, ALU.mult))
        pool_ready = DVE.last()
        PE.wait(got["prob", 0], got["prob", 1])
        srcs = [(0, h, 0) for h in range(N_Q)] + [(1, h, kb) for h in range(N_Q) for kb in range(2)]
        p_done = transpose_block(lambda i: prob[srcs[i][0]][:, srcs[i][1], srcs[i][2] * P:(srcs[i][2] + 1) * P],
                                 pT, 3 * N_Q, 0)
        PE.wait(p_done)
        DVE.wait(DVE.last())

        def pT_of(blk, h, kb):
            i = h if blk == 0 else N_Q + 2 * h + kb
            return pT[:, i * P:(i + 1) * P]
        PE.wait(bank[6].free, bank[7].free)
        for j in range(4):
            for g in range(2):
                h = g * 4 + j
                o = bank[6 + j // 2].ap[g * HD:(g + 1) * HD, (j % 2) * T:(j % 2 + 1) * T]
                mm(o[:, 0:P], v_tok[:, 0, g * HD:(g + 1) * HD], pT_of(0, h, 0), start=True, stop=True)
                mm(o[:, P:2 * P], v_tok[:, 0, g * HD:(g + 1) * HD], pT_of(1, h, 0), start=True, stop=False)
                ins = mm(o[:, P:2 * P], v_tok[:, 1, g * HD:(g + 1) * HD], pT_of(1, h, 1), start=False, stop=True)
        t = PE.done(ins)
        ACT.wait(t)
        for q in range(2):
            bank[6 + q].free = ACT.done(nc.scalar.copy(
                oT[:, 2 * q:2 * q + 2, :], bank[6 + q].ap.rearrange("p (j t) -> p j t", j=2)))
        o_ready = ACT.last()
        DVE.wait(sig_ready)
        ahead = [halve_chunk(s, dense_release) for s in (0, 1)]
        for br in range(2):
            rhs = (poolY, oT)[br]
            PE.wait((pool_ready, o_ready)[br])
            for c in range(2):
                s = (14 + 2 * br + c) % RING
                dense_ready(PE, s)
                w = dense_ring[s][:, :].rearrange("p (j n) -> p j n", j=4)
                for q in range(2):
                    buf = bank[(br * 4 + c * 2 + q) % 8]
                    PE.wait(buf.free)
                    for f in range(2):
                        for k in range(4):
                            ins = mm(buf.ap[:, f * T:(f + 1) * T], w[:, k, (2 * q + f) * P:(2 * q + f + 1) * P],
                                     rhs[:, k, :], start=k == 0, stop=k == 3)
                    t = PE.done(ins)
                    DVE.wait(t)
                    k0 = c * 4 + 2 * q
                    src = buf.ap.rearrange("p (f t) -> p f t", f=2)
                    dst = merged[:, k0:k0 + 2, :] if br == 0 else sig[:, 8 + k0:8 + k0 + 2, :]
                    buf.free = DVE.then(V.scalar_tensor_tensor(dst, sig[:, br * 8 + k0:br * 8 + k0 + 2, :], 1.0,
                                                               src, ALU.add, ALU.mult))
                    if br == 1:
                        m = merged[:, k0:k0 + 2, :]
                        t = DVE.done(V.tensor_tensor(m, m, dst, ALU.add))
                        got["m", k0] = got["m", k0 + 1] = halve(tuple(h[:, k0:k0 + 2, :] for h in b2["h"]), m, t, halves_free)
                dense_release(s, t)
        for j in range(4):
            buf = bank[j]
            t = tile_products(ahead[j], buf, b2["h"], [got["m", k] for k in range(KD)])
            if j + 2 < 4:
                ahead.append(halve_chunk(j + 2, dense_release))
            add_to_x(0.5)(j, [buf], t)
        h_state.free = work_state.free = [PE.last(), DVE.last(), ACT.last()]

    def finish(final_norm=True):
        if final_norm:
            rms_norm(S("norm_final_g"))
            src = hT
            PE.wait(h_state.ready)
        else:
            src = xT
            PE.wait(x_state.ready)
        for e in compute:
            e.wait(work_state.free)
        o_tok = work[:, 0:TT * D]
        for tt in range(TT):
            done = transpose_block(lambda i, tt=tt: src[:, i, tt * P:(tt + 1) * P],
                                   o_tok[:, tt * D:(tt + 1) * D], KD, 1 + 2 * tt)
            SP.wait(done)
            t = load("out", out[tt * P:(tt + 1) * P, :], o_tok[:, tt * D:(tt + 1) * D])
        SP.wait(t)
        for s in range(RING):
            SP.wait(pr.now(slot_count[s]), pr.now(exp_count[s]))

    def stages():
        yield "ab", lambda: (rms_norm(S("norm_mix_g", 0, KD)), mixer_ab())
        yield "moe0", lambda: moe(0)
        yield "rglru", lambda: (rms_norm(S("norm_mix_g", KD, KD)), mixer_rglru())
        yield "moe1", lambda: moe(1)
        yield "final", final_of_block1
        for layer in range(2):
            yield f"ffn1_{layer}", lambda layer=layer: ffn(layer, 0, S("ln_ffn1_2", layer * KD, KD))
            yield f"mix_{layer}", lambda layer=layer: mixer2(layer)
            yield f"ffn2_{layer}", lambda layer=layer: ffn(layer, 1, S("ln_ffn2_2", layer * KD, KD))

    def final_of_block1():
        rms_norm(S("norm_final_g"))
        DVE.wait(h_state.ready)
        for q in range(2):
            DVE.then(nc.vector.tensor_copy(xT[:, 4 * q:4 * q + 4, :], hT[:, 4 * q:4 * q + 4, :]))
        x_state.ready = DVE.last()

    for name, stage in stages():
        if name == "ffn1_0":
            open_block2()
        stage()
        if name == upto:
            break
    finish(final_norm=False)
    return pr.new_rates, pr.new_marks


WEIGHTS = ["a_ws", "ab_w_in", "ab_w_out", "c_w_in", "c_w_a", "c_w_x", "c_w_out", "moe_w_rg", "moe_w_re",
           "moe_w_gate", "moe_w_up", "moe_w_down", "w_ffn1_gu_2", "w_ffn1_down_2", "w_in_2", "pool_w_2",
           "w_pool_branch_2", "w_attn_branch_2", "w_out_2", "w_ffn2_gu_2", "w_ffn2_down_2"]


def lay_out(inputs):
    f = lambda n: np.asarray(inputs[n])
    col = lambda v: np.moveaxis(v.reshape(*v.shape[:-1], v.shape[-1] // P, P), -1, 0).reshape(P, -1)
    row = lambda v: np.broadcast_to(v.reshape(1, -1), (P, v.size))
    parts = [col(f(n)) for n in ("norm_mix_g", "norm_ffn_g", "norm_final_g", "b_conv_w", "c_conv_w", "c_conv_b",
                                 "c_b_a", "c_b_x", "c_lambda", "ln_ffn1_2", "ln_mix_2", "ln_ffn2_2", "pool_scale_2")]
    moe_b = np.concatenate([f("moe_b_rg"), f("moe_b_re")], axis=1)
    parts += [row(v) for v in (f("a_ln_g"), f("a_ws_b"), moe_b, f("q_norm_2"), f("k_norm_2"), f("sinks_2"))]
    small = np.ascontiguousarray(np.concatenate(parts, axis=1))
    arrays = {"x": f("x").reshape(T, D), "consts": constant_table()[1], "small": small}
    for n in WEIGHTS:
        v = f(n)
        if n.startswith(("a_", "ab_", "c_")):
            v = v[0]
        elif n.startswith(("moe_w_gate", "moe_w_up", "moe_w_down")):
            v = v.reshape(2 * N_EXP, *v.shape[2:])
        arrays[n] = v
    return {n: np.ascontiguousarray(v) for n, v in arrays.items()}


def make(arrays, new_core, upto=None):
    counts = ({}, {})
    for _ in range(2):
        nc = new_core()
        aps = {n: nc.dram_tensor("in_" + n, v.shape, mybir.dt.from_np(v.dtype), kind="ExternalInput").ap()
               for n, v in arrays.items()}
        out = nc.dram_tensor("out", (T, D), F32, kind="ExternalOutput").ap()
        counts = build(nc, aps, out, *counts, upto=upto)
    return nc


def kernel(**inputs):
    import concourse.bacc as bacc
    from concourse.bass_utils import run_bass_kernel_spmd
    arrays = lay_out(inputs)
    nc = make(arrays, lambda: bacc.Bacc("TRN2", target_bir_lowering=False, num_devices=1))
    r = run_bass_kernel_spmd(nc, [{"in_" + n: v for n, v in arrays.items()}], core_ids=[0])
    return r.results[0]["out"].reshape(1, T, D)
```

```python
from contextlib import ExitStack, contextmanager

import numpy as np
import concourse.bass as bass
from concourse import mybir
from concourse.alu_op_type import AluOpType as ALU

F32 = mybir.dt.float32
I32 = mybir.dt.int32
BF16 = mybir.dt.bfloat16
F32R = mybir.dt.float32r
ACTF = mybir.ActivationFunctionType
X = mybir.AxisListType.X

P = 128
D = 1024
KD = D // P
T = 256
TT = T // P
EPS = 1e-6

D_A = 512
NA = D_A // P
N_GROUPS, PER_GROUP = 4, 8
N_EXP = N_GROUPS * PER_GROUP
D_EXP = 512
FE = D_EXP // P
CAP = 32
QUAD = P // CAP
QUADS = N_EXP // QUAD

D_FF = 2816
GF = 2
N_GRP = D_FF // P // GF
HD = 64
N_Q, N_KV = 8, 2
N_HEADS = N_Q + N_KV
WINDOWS = (2, 4, 8, 16)
EDGE = max(WINDOWS)
ROT = HD // 4
NEG = -1e30

RING = 6
LENT = 3
CHUNK = 256
RING_F = KD * CHUNK
EXP_F = KD * D_EXP
WORK_F = 8320
SCRATCH_F = 10080


def constant_table():
    i = np.arange(P)
    parts = [("ident", np.eye(P)), ("ones", np.ones((P, P))), ("mean", np.full((P, P), 1.0 / D))]
    parts.append(("causal", (i[None, :] <= i[:, None]) * 1.0))
    parts.append(("before", (i[:, None] < i[None, :]) * 1.0))
    parts.append(("eps", np.full((P, 1), EPS)))
    parts.append(("iota", np.tile(np.arange(CAP, dtype=np.float64), (P, 1))))
    parts.append(("rank_g", np.tile(N_GROUPS - np.arange(N_GROUPS), (P, 1))))
    parts.append(("rank_e", np.tile(N_EXP - np.arange(N_EXP), (P, 1))))
    pos = np.arange(T, dtype=np.float32)
    freq = np.float32(500000.0) ** (-np.arange(0, ROT, 2, dtype=np.float32) / np.float32(ROT))
    ang = (pos[:, None] * freq[None, :].astype(np.float32)).astype(np.float32)
    half = ROT // 2
    for name, v in (("cos", np.cos(ang)), ("sin", np.sin(ang))):
        parts.append((name, v.reshape(TT, P, half).transpose(1, 0, 2).reshape(P, TT * half)))
    cnt = np.stack([1.0 / np.minimum(np.arange(EDGE) + 1, w) for w in WINDOWS])
    parts.append(("rcount", np.tile(cnt.reshape(1, -1), (P, 1))))
    q, k = i[:, None], np.arange(2 * P)[None, :]
    diff = q + P - k
    parts.append(("band", np.where((diff >= 0) & (diff < P), 0.0, NEG)))
    where, at = {}, 0
    for name, v in parts:
        where[name] = (at, v.shape[1])
        at += v.shape[1]
    return where, np.concatenate([v for _, v in parts], axis=1).astype(np.float32)


def small_layout():
    cols = [("norm_mix_g", 2 * KD), ("norm_ffn_g", 2 * KD), ("norm_final_g", KD),
            ("b_conv_w", 3 * NA), ("c_conv_w", 4 * KD), ("c_conv_b", KD), ("c_b_a", KD),
            ("c_b_x", KD), ("c_lambda", KD), ("ln_ffn1_2", 2 * KD), ("ln_mix_2", 2 * KD),
            ("ln_ffn2_2", 2 * KD), ("pool_scale_2", 2 * 4),
            ("a_ln_g", D_A), ("a_ws_b", NA * P), ("moe_b", 2 * (N_GROUPS + N_EXP)),
            ("q_norm_2", 2 * HD), ("k_norm_2", 2 * HD), ("sinks_2", 2 * N_Q)]
    where, at = {}, 0
    for name, n in cols:
        where[name] = (at, n)
        at += n
    return where, at


class Counter:

    def __init__(self, name, sem, step):
        self.name, self.sem, self.step, self.const = name, sem, step, 0


class Ticket:

    def __init__(self, counter, const, loops):
        self.counter, self.const, self.loops = counter, const, loops


class Loop:

    def __init__(self, prog, name, n, carried):
        self.prog, self.name, self.n, self.open, self.carried = prog, name, n, True, carried
        self.entry = {c.name: c.const for c in prog.counters}

    def rate(self, counter):
        return self.prog.rates.get((self.name, counter.name), 0)

    def last_time(self, name, counter=None):
        left = self.prog.marks.get((self.name, name))
        if left is None:
            return None
        counter = self.prog.by_name[left[0]]
        c = self.entry.get(counter.name, 0) + left[1] - self.rate(counter)
        return Ticket(counter, c, tuple(self.prog.loops))

    def first_turn_covers(self, name, ticket):
        left = self.prog.marks.get((self.name, name))
        if left is None or not isinstance(ticket, Ticket) or left[0] != ticket.counter.name:
            return False
        first = self.entry.get(left[0], 0) + left[1] - self.rate(ticket.counter)
        return not ticket.loops and first >= ticket.const

    def leave(self, tickets):
        for name, t in tickets.items():
            if t is not None and t.loops and t.loops[-1] is self:
                off = t.const - self.entry.get(t.counter.name, 0)
                self.prog.new_marks[(self.name, name)] = (t.counter.name, off)


class Program:
    def __init__(self, nc, rates, marks):
        self.nc, self.rates, self.marks = nc, rates, marks
        self.new_rates, self.new_marks = {}, {}
        self.loops, self.counters, self.engines, self.by_name = [], [], [], {}
        self.turns = nc.alloc_semaphore("turns")

    def counter(self, name, step=1):
        c = Counter(name, self.nc.alloc_semaphore(name), step)
        self.counters.append(c)
        self.by_name[name] = c
        return c

    def now(self, counter):
        return Ticket(counter, counter.const, tuple(self.loops))

    @contextmanager
    def loop(self, name, n, carried=None, engines=()):
        lp = Loop(self, name, n, carried)
        for e in engines:
            e.wait([t for k, t in carried.items() if not lp.first_turn_covers(k, t)])
        with self.nc.Fori(0, n) as i:
            lp.i = i
            self.loops.append(lp)
            if carried is not None:
                for k in list(carried):
                    carried[k] = lp.last_time(k) or carried[k]
            yield lp
            if carried is not None:
                lp.leave(carried)
            self.loops.pop()
            for e in self.engines:
                e.seen = {k: v for k, v in e.seen.items() if lp not in k[1]}
        lp.open = False
        for c in self.counters:
            per = c.const - lp.entry.get(c.name, 0)
            self.new_rates[(name, c.name)] = per
            c.const += (n - 1) * per


class Engine:
    def __init__(self, prog, e, name):
        self.prog, self.e, self.name, self.seen = prog, e, name, {}
        self.count = prog.counter(name)
        self.settle = name == "sp_done"
        prog.engines.append(self)

    def wait(self, *tickets):
        for t in tickets:
            if t is None:
                continue
            if isinstance(t, (list, tuple)):
                self.wait(*t)
                continue
            const, live = t.const, []
            for lp in t.loops:
                if lp.open:
                    live.append(lp)
                else:
                    const += (lp.n - 1) * lp.rate(t.counter)
            if const <= 0 and not live:
                continue
            key = (t.counter, tuple(live))
            if self.seen.get(key, -1) >= const:
                continue
            self.seen[key] = const
            value = const
            for lp in live:
                if lp.rate(t.counter):
                    value = value + lp.i * lp.rate(t.counter)
            self.e.wait_ge(t.counter.sem, value)
            if live and self.settle:
                self.step()

    def done(self, instruction):
        instruction.then_inc(self.count.sem, 1)
        self.count.const += 1
        return self.prog.now(self.count)

    def then(self, instruction):
        t = self.done(instruction)
        self.wait(t)
        return t

    def last(self):
        return self.prog.now(self.count)

    def step(self):
        self.e.sem_inc(self.prog.turns, 1)


class Buffer:

    def __init__(self, ap=None):
        self.ap, self.ready, self.free = ap, None, None


def build(nc, a, out, rates=None, marks=None, upto=None):
    pr = Program(nc, rates or {}, marks or {})
    PE, ACT, DVE, POOL, SP = (Engine(pr, e, n) for e, n in (
        (nc.tensor, "pe_done"), (nc.scalar, "act_done"), (nc.vector, "dve_done"),
        (nc.gpsimd, "pool_done"), (nc.sync, "sp_done")))
    compute = (PE, ACT, DVE)
    mm = nc.tensor.matmul

    def sb(name, cols, dt=F32):
        return nc.alloc_sbuf_tensor(name, [P, cols], dt)

    cw, _ = constant_table()
    n_const = sum(n for _, n in cw.values())
    sw, n_small = small_layout()
    consts, small = sb("consts", n_const), sb("small", n_small)

    def C(name):
        return consts[:, cw[name][0]:cw[name][0] + cw[name][1]]

    def S(name, at=0, n=None):
        c0, width = sw[name]
        return small[:, c0 + at:c0 + at + (width - at if n is None else n)]

    xT = sb("xT", KD * T)[:, :].rearrange("p (k t) -> p k t", k=KD)
    hT = sb("hT", KD * T)[:, :].rearrange("p (k t) -> p k t", k=KD)
    work = sb("work", WORK_F)
    rinv = sb("rinv", T)
    most_tokens = sb("most_tokens", 2, I32)
    zeros = sb("zeros", 512, BF16)
    dense_mem = sb("dense_ring", RING * RING_F)
    dense_ring = [dense_mem[:, s * RING_F:(s + 1) * RING_F] for s in range(RING)]
    w_route = [sb(f"routers{l}", KD * (N_GROUPS + N_EXP))[:, :].rearrange("p (k n) -> p k n", k=KD) for l in range(2)]
    probe = sb("probe", 1)
    held, lent = ExitStack(), ExitStack()
    expert_ring = [held.enter_context(nc.sbuf_tensor(f"expert_ring{s}", [P, EXP_F], F32))[:, :]
                   for s in range(RING - LENT)] + [None] * LENT
    w_halves, h_halves, hid_halves = [None] * 2, [None] * 2, [None] * 2
    taken = [0]

    def take(owner, name, n, dt=F32):
        taken[0] += 1
        return owner.enter_context(nc.sbuf_tensor(f"{name}_{taken[0]}", [P, n], dt))[:, :]

    def lend_to_halves():
        lent.close()
        for i in range(2):
            w_halves[i] = tuple(take(lent, "w_" + h, RING_F, F32R) for h in ("hi", "lo"))
        h_halves[:] = [take(lent, "h_" + h, KD * T, F32R).rearrange("p (k t) -> p k t", k=KD) for h in ("hi", "lo")]

    def lend_to_experts():
        lent.close()
        for s in range(RING - LENT, RING):
            expert_ring[s] = take(lent, f"expert_ring{s}", EXP_F)

    def lend_to_block2():
        lent.close()
        held.close()
        lend_to_halves()
        for par in range(2):
            hid_halves[par] = tuple(take(lent, "hid_" + h, GF * T, F32R) for h in ("hi", "lo"))
        return take(lent, "scratch", SCRATCH_F)
    ps = nc.alloc_psum_tensor("ps", [P, 8, 512], F32)
    bank = [Buffer(ps[:, b, :]) for b in range(8)]
    x_state, h_state, work_state = Buffer(xT), Buffer(hT), Buffer()

    once = {}

    def load(name, dst, src, eng=SP):
        c = once.get(name) or pr.counter("ld_" + name, 16)
        once[name] = c
        eng.e.dma_start(dst, src).then_inc(c.sem, 16)
        c.const += 16
        return pr.now(c)

    x_tok = work[:, 0:TT * D].rearrange("p (a d) -> p a d", a=TT)
    x_loaded = load("x", x_tok, a["x"].rearrange("(a p) d -> p a d", p=P))
    consts_loaded = load("consts", consts[:, :], a["consts"])
    small_loaded = load("small", small[:, :], a["small"])

    slot_count = [pr.counter(f"dense{s}_loaded", 16) for s in range(RING)]
    slot_queue = [[] for _ in range(RING)]

    def dense_load(s, pieces):
        for dst, src in pieces(dense_ring[s]):
            nc.sync.dma_start(dst, src).then_inc(slot_count[s].sem, 16)
            slot_count[s].const += 16

    def queue_stage(chunks):
        for j, c in enumerate(chunks):
            slot_queue[j % RING].append(c)

    HOLD = "hold"
    EXTRA = [(4, 5), (0, 1), (2, 3)]
    extra = [dense_mem[:, s0 * RING_F:s0 * RING_F + EXP_F] for s0, _ in EXTRA]
    extra_count = [pr.counter(f"extra{i}_loaded", 16) for i in range(len(EXTRA))]
    held_back = {}
    next_moe = [0]

    def dense_release(s, ticket):
        if slot_queue[s] and slot_queue[s][0] is HOLD:
            slot_queue[s].pop(0)
            held_back[s] = ticket
            i = [s in both for both in EXTRA].index(True)
            if all(b in held_back for b in EXTRA[i]):
                SP.wait([held_back[b] for b in EXTRA[i]])
                _, src = expert_piece(next_moe[0], 1, i)
                nc.sync.dma_start(extra[i].rearrange("p (k n) -> p k n", k=KD), src).then_inc(extra_count[i].sem, 16)
                extra_count[i].const += 16
        elif slot_queue[s]:
            SP.wait(ticket)
            dense_load(s, slot_queue[s].pop(0))

    def dense_ready(engine, s):
        engine.wait(pr.now(slot_count[s]))

    def cols(w, c0, n=CHUNK, k=KD):
        def pieces(buf):
            return [(buf[:, 0:k * n].rearrange("p (k n) -> p k n", k=k),
                     w[:, c0:c0 + n].rearrange("(k p) n -> p k n", p=P))]
        return pieces

    def rows(w, r):
        def pieces(buf):
            src = w[bass.ds(r * GF * P, GF * P), :]
            return [(buf[:, 0:GF * D].rearrange("p (f n) -> p f n", f=GF),
                     src.rearrange("(f p) n -> p f n", p=P))]
        return pieces

    def cols_at(w, g, base):
        def pieces(buf):
            src = w[:, bass.ds(g * CHUNK + base, CHUNK)]
            return [(buf[:, :].rearrange("p (k n) -> p k n", k=KD),
                     src.rearrange("(k p) n -> p k n", p=P))]
        return pieces

    exp_count = [pr.counter(f"expert{s}_loaded", 16) for s in range(RING)]

    for l in range(2):
        load("route", w_route[l][:, :, 0:N_GROUPS], a["moe_w_rg"][l].rearrange("(k p) n -> p k n", p=P))
        routers_loaded = load("route", w_route[l][:, :, N_GROUPS:], a["moe_w_re"][l].rearrange("(k p) n -> p k n", p=P))

    def expert_piece(layer, pair, s):
        e, m = pair * 2 + s % 2, s // 2
        w = a[("moe_w_gate", "moe_w_up", "moe_w_down")[m]]
        src = w[bass.ds(e + layer * N_EXP, 1), :, :].rearrange("o (k p) n -> p (o k) n", p=P)
        return expert_ring[s].rearrange("p (k n) -> p k n", k=KD if m < 2 else FE), src

    def expert_load(layer, pair, s, counts=None):
        c = (counts or exp_count)[s]
        nc.sync.dma_start(*expert_piece(layer, pair, s)).then_inc(c.sem, 16)
        c.const += 16

    ffn_w = [(a["w_ffn1_gu_2"], a["w_ffn1_down_2"]), (a["w_ffn2_gu_2"], a["w_ffn2_down_2"])]

    def queue_ffn(layer, which):
        gu, dn = (w[layer] for w in ffn_w[which])
        first = []
        for g in range(2):
            first += [cols_at(gu, g, 0), cols_at(gu, g, D_FF), rows(dn, g)]
        queue_stage(first)
        last = N_GRP - 1
        slot_queue[2] += [rows(dn, last - 2), rows(dn, last)]
        slot_queue[0].append(cols_at(gu, last, 0))
        slot_queue[1].append(cols_at(gu, last, D_FF))
        slot_queue[5].append(rows(dn, last - 1))

    def mixer2_chunks(layer):
        w_in = a["w_in_2"][layer]
        wa = a["w_attn_branch_2"][layer]
        order = [2, 3, 4, 0, 1] + list(range(5, 13))
        chunks = [cols(w_in, c * CHUNK) for c in order]

        def pool_w(buf):
            return [(buf[:, 0:4 * P].rearrange("p (g d) -> p g d", g=4),
                     a["pool_w_2"][layer].rearrange("g c d -> c g d"))]

        def attn_rows(c0):
            def pieces(buf):
                v = buf[:, :].rearrange("p (j n) -> p j n", j=4)
                return [(v[g * HD:(g + 1) * HD, :, :],
                         wa[g * 4 * HD:(g + 1) * 4 * HD, c0:c0 + 512].rearrange("(j c) n -> c j n", c=HD))
                        for g in range(2)]
            return pieces

        chunks.append(pool_w)
        wp = a["w_pool_branch_2"][layer]
        chunks += [cols(wp, 0, 512, 4), cols(wp, 512, 512, 4), attn_rows(0), attn_rows(512)]
        chunks += [cols(a["w_out_2"][layer], c * CHUNK) for c in range(4)]
        return chunks

    queue_stage([cols(a["ab_w_in"], c * CHUNK) for c in (2, 3, 6, 7, 8, 9, 4, 5, 0, 1)])
    queue_stage([cols(a["ab_w_out"], c * CHUNK) for c in range(4)])
    for queue in slot_queue:
        queue.append(HOLD)

    def lru_w(w):
        return lambda buf: [(buf[:, 0:KD * P].rearrange("p (h d) -> p h d", h=KD),
                             w.rearrange("h c d -> c h d"))]

    queue_stage([cols(a["c_w_in"], c * CHUNK) for c in (4, 5, 6, 7)] + [lru_w(a["c_w_a"]), lru_w(a["c_w_x"])]
                + [cols(a["c_w_in"], c * CHUNK) for c in (0, 1, 2, 3)])
    for s, c in ((4, 0), (5, 1), (0, 2), (1, 3)):
        slot_queue[s].append(cols(a["c_w_out"], c * CHUNK))
    for queue in slot_queue:
        queue.append(HOLD)
    for layer in range(2):
        queue_ffn(layer, 0)
        queue_stage(mixer2_chunks(layer))
        queue_ffn(layer, 1)

    for s in range(RING):
        dense_load(s, slot_queue[s].pop(0))
    ws_rows = work[:, 6144:6144 + NA * P].rearrange("p (h s) -> p h s", h=NA)
    ws_loaded = load("ws", ws_rows, a["a_ws"].rearrange("h t s -> t h s"))
    for s in range(RING - LENT):
        expert_load(0, 0, s)

    z_ready = DVE.done(nc.vector.memset(zeros[:, :], 0.0))
    for e in compute:
        e.wait(consts_loaded)
    PE.wait(z_ready)

    def copy_out(engine, dst, src):
        return engine.done(nc.scalar.copy(dst, src) if engine is ACT else nc.vector.tensor_copy(dst, src))

    def transpose_block(src_of, dst, n, bank0, width=P, engines=(ACT, DVE)):
        tickets = []
        for b in range((n + 3) // 4):
            m = min(4, n - 4 * b)
            buf = bank[(bank0 + b) % 8]
            PE.wait(buf.free)
            for j in range(m):
                ins = nc.tensor.transpose(buf.ap[:, j * P:(j + 1) * P], src_of(4 * b + j), C("ident"))
            t = PE.done(ins)
            e = engines[b % len(engines)]
            e.wait(t)
            buf.free = copy_out(e, dst[:, 4 * b * P:(4 * b + m) * P], buf.ap[:, 0:m * P])
            tickets.append(buf.free)
        return tickets

    def flat(ap):
        return ap.rearrange("p k t -> p (k t)")

    probed = [None]

    def fetch_table(function):
        ACT.wait(probed[0])
        probed[0] = ACT.done(nc.scalar.activation(probe[:, :], C("eps"), function))

    squared = [0]

    def square_and_sum(q):
        if q == 0:
            fetch_table(ACTF.Sqrt)
            ACT.wait(h_state.free)
            PE.wait(bank[0].free)
        ACT.wait(x_state.ready[q])
        t = ACT.done(nc.scalar.activation(hT[:, 2 * q:2 * q + 2, :], xT[:, 2 * q:2 * q + 2, :], ACTF.Square))
        PE.wait(t)
        for k in (2 * q, 2 * q + 1):
            ins = mm(bank[0].ap[:, 0:T], C("mean"), hT[:, k, :], start=k == 0, stop=k == KD - 1)
        PE.done(ins)
        squared[0] = q + 1

    x_complete = [None]

    def rms_norm(gain, halves=None, meanwhile=None):
        for q in range(squared[0], 4):
            square_and_sum(q)
        squared[0] = 0
        t = PE.last()
        DVE.wait(h_state.free)
        if meanwhile:
            meanwhile()
        ACT.wait(t)
        t = bank[0].free = ACT.done(nc.scalar.activation(rinv[:, :], bank[0].ap[:, 0:T], ACTF.Sqrt, bias=C("eps")))
        DVE.wait(t)
        DVE.then(nc.vector.reciprocal(rinv[:, :], rinv[:, :]))
        DVE.wait(x_state.ready)
        h_state.ready, rounded = [], []
        for k in range(KD + 1):
            if k < KD:
                h_state.ready.append(DVE.done(nc.vector.scalar_tensor_tensor(
                    hT[:, k, :], xT[:, k, :], gain[:, k:k + 1], rinv[:, :], ALU.mult, ALU.mult)))
                if halves:
                    ACT.wait(h_state.ready[k], tickets["h_halves_free"])
                    rounded.append(ACT.done(nc.scalar.copy(halves[0][:, k, :], hT[:, k, :])))
            if halves and k:
                DVE.wait(rounded[k - 1], tickets["h_halves_free"])
                h_state.ready[k - 1] = DVE.done(nc.vector.tensor_tensor(
                    halves[1][:, k - 1, :], hT[:, k - 1, :], halves[0][:, k - 1, :].bitcast(F32), ALU.subtract))
        h_state.free = [DVE.last(), ACT.last()]

    tickets = {}

    def halve(dst, src, ready, free=None):
        hi, lo = dst
        ACT.wait(ready, free)
        t = ACT.done(nc.scalar.copy(hi, src))
        DVE.wait(t, ready, free)
        return DVE.done(nc.vector.tensor_tensor(lo, src, hi.bitcast(F32), ALU.subtract))

    def products(out, w, x, start, stop, **kw):
        mm(out, w[0], x[0], start=start, stop=False, **kw)
        mm(out, w[0], x[1], start=False, stop=False, **kw)
        return mm(out, w[1], x[0], start=False, stop=stop, **kw)

    turn_of = [0]

    def half_view(buf, by_rows, f):
        if by_rows:
            return buf[:, f * D:(f + 1) * D]
        return buf[:, :].rearrange("p (k n) -> p k n", k=KD)[:, :, f * P:(f + 1) * P]

    def halve_chunk(s, release, by_rows=False, tiles=(0, 1), i=None):
        if i is None:
            i = turn_of[0] % 2
            turn_of[0] += 1
        dense_ready(ACT, s)
        dense_ready(DVE, s)
        for f in tiles:
            src = half_view(dense_ring[s], by_rows, f)
            dst = tuple(w[:, f * D:(f + 1) * D] for w in w_halves[i])
            if not by_rows:
                dst = tuple(d.rearrange("p (k n) -> p k n", k=KD) for d in dst)
            tickets[f"w_ready{i}{f}"] = halve(dst, src, None, tickets[f"w_free{i}{f}"])
        if 1 in tiles:
            release(s, [ACT.last(), tickets[f"w_ready{i}1"]])
        return i

    def halved(i):
        return tuple(w.rearrange("p (f j n) -> p f j n", f=2, n=P) for w in w_halves[i])

    scratch = None

    def open_halves():
        if scratch is None:
            lend_to_halves()
        tickets["h_halves_free"] = PE.last()
        for i in range(2):
            for f in range(2):
                tickets[f"w_free{i}{f}"] = PE.last()
        for e in compute:
            e.wait(PE.last(), ACT.last(), DVE.last())

    of_next_stage = []
    halve_for_next = [None]

    def halving(slots):
        pairs = list(of_next_stage)
        slots = list(slots)[len(pairs):]
        of_next_stage.clear()

        def halve_next():
            if slots:
                pairs.append(halve_chunk(slots.pop(0), dense_release))
            elif halve_for_next[0] and not of_next_stage:
                of_next_stage.append(halve_for_next[0]())
        return pairs, halve_next

    def tile_products(i, buf, x, x_ready, order=range(KD)):
        w = halved(i)
        PE.wait(buf.free)
        for f in range(2):
            PE.wait(tickets[f"w_ready{i}{f}"])
            for n, k in enumerate(order):
                PE.wait(x_ready[k])
                ins = products(buf.ap[:, f * T:(f + 1) * T], tuple(v[:, f, k, :] for v in w),
                               tuple(v[:, k, :] for v in x), n == 0, n == KD - 1)
            t = tickets[f"w_free{i}{f}"] = PE.done(ins)
        return t

    def token_products(i, buf):
        w = halved(i)
        PE.wait(buf.free, tickets[f"w_ready{i}0"], tickets[f"w_ready{i}1"])
        for tt in range(TT):
            for k in range(KD):
                PE.wait(h_state.ready[k])
                ins = products(buf.ap[:, tt * CHUNK:(tt + 1) * CHUNK],
                               tuple(h[:, k, tt * P:(tt + 1) * P] for h in h_halves),
                               tuple(v[:, :, k, :] for v in w), k == 0, k == KD - 1)
        tickets[f"w_free{i}0"] = tickets[f"w_free{i}1"] = PE.done(ins)
        return PE.last()

    def project_to_x(pair_of, ready, halve_next, scale=1.0, order=range(KD)):
        work_state.free = [PE.last(), DVE.last(), ACT.last()]
        for j in range(4):
            buf = bank[1 + j]
            t = tile_products(pair_of(j), buf, h_halves, ready, order)
            if j:
                x_complete[0](j - 1)
            halve_next()
            DVE.wait(t)
            xs = flat(xT)[:, j * 2 * T:(j + 1) * 2 * T]
            buf.free = x_state.ready[j] = DVE.done(nc.vector.scalar_tensor_tensor(xs, buf.ap, scale, xs, ALU.mult, ALU.add))
        x_complete[0](3)

    PE.wait(x_loaded)
    x_state.ready = []
    for q in range(4):
        buf = bank[1 + q]
        for k in range(2):
            for tt in range(TT):
                ins = nc.tensor.transpose(buf.ap[:, k * T + tt * P:k * T + (tt + 1) * P],
                                          x_tok[:, tt, (2 * q + k) * P:(2 * q + k + 1) * P], C("ident"))
        e = (ACT, DVE)[q % 2]
        e.wait(PE.done(ins))
        buf.free = copy_out(e, xT[:, 2 * q:2 * q + 2, :], buf.ap.rearrange("p (k t) -> p k t", k=2))
        x_state.ready.append(buf.free)
    for q in range(4):
        square_and_sum(q)
    work_state.free = [PE.last()] + x_state.ready
    DVE.wait(x_state.ready, small_loaded)
    ACT.wait(small_loaded)

    def mixer_ab():
        def tile(at, n, w=T):
            return work[:, at:at + n * w].rearrange("p (k t) -> p k t", k=n)
        yT = tile(0, KD)
        v_tok = tile(2048, TT, D_A)
        PAD = 2
        gx = tile(3072, NA, T + PAD)
        acc = tile(3072 + NA * (T + PAD), NA)
        wsT = work[:, 5632:5632 + NA * P].rearrange("p (h t) -> p h t", h=NA)
        stat = work[:, 6656:6656 + 16]
        open_halves()
        pairs, halve_next = halving([0, 1, 2, 3, 4, 5, 0, 1, 2, 3] + [0, 1, 2, 3])
        halve_next()
        rms_norm(S("norm_mix_g", 0, KD), h_halves)
        halve_next()
        for e in (ACT, DVE):
            e.wait(work_state.free)
        DVE.then(nc.vector.memset(gx[:, :, 0:PAD], 0.0))
        v_done = []
        for j in range(2):
            buf = bank[1 + j]
            t = token_products(pairs[j], buf)
            halve_next()
            ACT.wait(t)
            buf.free = ACT.done(nc.scalar.activation(
                v_tok[:, :, j * CHUNK:(j + 1) * CHUNK], buf.ap.rearrange("p (a n) -> p a n", a=TT),
                ACTF.Gelu_apprx_tanh))
            v_done.append(buf.free)

        def layer_norm():
            DVE.wait(v_done)
            cen = tile(0, TT, D_A)
            for tt in range(TT):
                s = stat[:, 4 * tt:4 * tt + 4]
                DVE.then(nc.vector.tensor_reduce(s[:, 0:1], v_tok[:, tt, :], X, ALU.add))
                DVE.then(nc.vector.tensor_scalar(s[:, 0:1], s[:, 0:1], 1.0 / D_A, None, ALU.mult))
                DVE.then(nc.vector.tensor_scalar(v_tok[:, tt, :], v_tok[:, tt, :], s[:, 0:1], None, ALU.subtract))
                DVE.then(nc.vector.tensor_tensor(cen[:, tt, :], v_tok[:, tt, :], v_tok[:, tt, :], ALU.mult))
                DVE.then(nc.vector.tensor_reduce(s[:, 1:2], cen[:, tt, :], X, ALU.add))
                t = DVE.done(nc.vector.tensor_scalar(s[:, 1:2], s[:, 1:2], 1.0 / D_A, EPS, ALU.mult, ALU.add))
                ACT.wait(t)
                t = ACT.done(nc.scalar.activation(s[:, 2:3], s[:, 1:2], ACTF.Sqrt))
                DVE.wait(t)
                DVE.then(nc.vector.reciprocal(s[:, 3:4], s[:, 2:3]))
                t = DVE.then(nc.vector.scalar_tensor_tensor(v_tok[:, tt, :], v_tok[:, tt, :], s[:, 3:4],
                                                            S("a_ln_g"), ALU.mult, ALU.mult))
            return t
        state = {}

        def evacuate(j, bufs, t):
            jj, src = j % 2, bufs[0].ap
            src2 = src.rearrange("p (f t) -> p f t", f=2)
            part = slice(2 * jj, 2 * jj + 2)
            kind = j // 2
            if kind == 0:
                ACT.wait(t)
                bufs[0].free = ACT.done(nc.scalar.copy(acc[:, part, :], src2))
                state["gc", jj] = bufs[0].free
            elif kind == 1:
                DVE.wait(t, state["gc", jj])
                bufs[0].free = DVE.then(nc.vector.tensor_tensor(gx[:, part, PAD:], src2, acc[:, part, :], ALU.mult))
                for c in (2 * jj, 2 * jj + 1):
                    DVE.then(nc.vector.tensor_scalar(acc[:, c, :], gx[:, c, 0:T], S("b_conv_w", c, 1), None, ALU.mult))
                    for tap in (1, 2):
                        DVE.then(nc.vector.scalar_tensor_tensor(
                            acc[:, c, :], gx[:, c, tap:tap + T], S("b_conv_w", tap * NA + c, 1),
                            acc[:, c, :], ALU.mult, ALU.add))
            elif kind == 2:
                if jj == 0:
                    state["ln"] = layer_norm()
                DVE.wait(t)
                bufs[0].free = DVE.done(nc.vector.tensor_tensor(
                    yT[:, NA + 2 * jj:NA + 2 * jj + 2, :], src2, acc[:, part, :], ALU.mult))
                state["yb"] = bufs[0].free
            else:
                ACT.wait(t, state["ln"])
                bufs[0].free = ACT.done(nc.scalar.activation(yT[:, part, :], src2, ACTF.Gelu_apprx_tanh))
                state["u"] = bufs[0].free

        for j in range(8):
            buf = bank[3 + j % 4]
            t = tile_products(pairs[2 + j], buf, h_halves, h_state.ready)
            halve_next()
            evacuate(j, [buf], t)
        tickets["h_halves_free"] = PE.last()
        DVE.wait(ws_loaded)
        for h in range(NA):
            t = DVE.done(nc.vector.tensor_tensor(ws_rows[:, h, :], ws_rows[:, h, :], C("causal"), ALU.mult))
        PE.wait(t)
        ws_done = transpose_block(lambda h: ws_rows[:, h, :], flat(wsT), NA, 7, engines=(ACT,))
        ready = {}

        def halve_y(k0, of):
            return halve(tuple(h[:, k0:k0 + 2, :] for h in h_halves), yT[:, k0:k0 + 2, :], of,
                         tickets["h_halves_free"])
        for k0 in (4, 6):
            ready[k0] = ready[k0 + 1] = halve_y(k0, state["yb"])
        PE.wait(state["ln"], ws_done, bank[0].free, bank[1].free)
        for h in range(NA):
            for c in range(TT):
                ins = mm(bank[h // 2].ap[:, (h % 2) * T + c * P:(h % 2) * T + (c + 1) * P],
                         v_tok[:, c, h * P:(h + 1) * P], wsT[:, h, :], start=True, stop=True)
        t = PE.done(ins)
        DVE.wait(t, state["u"], DVE.last())
        y_ready = []
        for h in range(NA):
            m = bank[h // 2].ap[:, (h % 2) * T:(h % 2 + 1) * T].rearrange("p (c t) -> p c t", c=TT)
            bias = S("a_ws_b", h * P, P).unsqueeze(1).to_broadcast([P, TT, P])
            tmp = acc[:, h, :].rearrange("p (c t) -> p c t", c=TT)
            DVE.then(nc.vector.tensor_tensor(tmp, m, bias, ALU.add))
            y_ready.append(DVE.done(nc.vector.tensor_tensor(yT[:, h, :], acc[:, h, :], yT[:, h, :], ALU.mult)))
        bank[0].free = bank[1].free = y_ready[-1]
        for k0 in (0, 2):
            ready[k0] = ready[k0 + 1] = halve_y(k0, y_ready[k0 + 1])
        project_to_x(lambda j: pairs[10 + j], ready, halve_next, order=(4, 5, 6, 7, 0, 1, 2, 3))
        work_state.free = [PE.last(), DVE.last(), ACT.last()]

    def mixer_rglru():
        def tile(at, n=KD, w=T):
            return work[:, at:at + n * w].rearrange("p (k t) -> p k t", k=n)
        PAD = 3
        gate = tile(0)
        pad = tile(2048, KD, T + PAD)
        bx = tile(2048)
        xr = tile(2048 + KD * (T + PAD))
        ra = tile(2048 + KD * (T + PAD) + KD * T)
        cst = work[:, 8256:8256 + 6 * KD].rearrange("p (n k) -> p n k", k=KD)
        open_halves()
        pairs, halve_next = halving([0, 1, 2, 3] + [0, 1, 2, 3] + [4, 5, 0, 1])
        rms_norm(S("norm_mix_g", KD, KD), h_halves, halve_next)
        halve_next()
        for e in compute:
            e.wait(work_state.free)
        DVE.then(nc.vector.memset(pad[:, :, 0:PAD], 0.0))
        lam = S("c_lambda")
        y, s, s2, pol = (cst[:, n, :] for n in range(1, 5))
        DVE.then(nc.vector.tensor_scalar(s, lam, -1.0, None, ALU.mult))
        t = DVE.then(nc.vector.tensor_tensor(s, s, lam, ALU.min))
        ACT.wait(t)
        t = ACT.done(nc.scalar.activation(y, s, ACTF.Exp))
        DVE.wait(t)
        DVE.then(nc.vector.tensor_scalar(s, y, 2.0, None, ALU.add))
        DVE.then(nc.vector.reciprocal(s, s))
        DVE.then(nc.vector.tensor_tensor(s, s, y, ALU.mult))
        DVE.then(nc.vector.tensor_tensor(s2, s, s, ALU.mult))
        terms = 9
        DVE.then(nc.vector.tensor_scalar(pol, s2, 1.0 / (2 * terms + 1), 1.0 / (2 * terms - 1), ALU.mult, ALU.add))
        for n in range(terms - 2, -1, -1):
            DVE.then(nc.vector.tensor_tensor(pol, pol, s2, ALU.mult))
            DVE.then(nc.vector.tensor_scalar(pol, pol, 1.0 / (2 * n + 1), None, ALU.add))
        DVE.then(nc.vector.tensor_tensor(pol, pol, s, ALU.mult))
        DVE.then(nc.vector.tensor_scalar(s, lam, 0.0, None, ALU.min))
        DVE.then(nc.vector.scalar_tensor_tensor(pol, pol, -2.0, s, ALU.mult, ALU.add))
        DVE.then(nc.vector.tensor_scalar(cst[:, 0, :], pol, 4.0, None, ALU.mult))
        DVE.then(nc.vector.tensor_scalar(cst[:, 1, :], pol, -4.0, None, ALU.mult))
        DVE.then(nc.vector.tensor_scalar(cst[:, 4, :], S("c_b_a"), 0.5, None, ALU.mult))
        half_b = DVE.then(nc.vector.tensor_scalar(cst[:, 5, :], S("c_b_x"), 0.5, None, ALU.mult))

        xr_ready = {}
        gate_banks = []

        def gate_branch(j, meanwhile=None):
            gate_banks.append(tile_products(pairs[4 + j], bank[4 + j], h_halves, h_state.ready))
            if meanwhile:
                meanwhile()
            if j < 3:
                halve_next()

        def gelu(j):
            ACT.wait(gate_banks[j])
            bank[4 + j].free = ACT.done(nc.scalar.activation(
                gate[:, 2 * j:2 * j + 2, :], bank[4 + j].ap.rearrange("p (f t) -> p f t", f=2), ACTF.Gelu_apprx_tanh))
            return bank[4 + j].free

        for j in range(4):
            buf = bank[1 + j]
            t = tile_products(pairs[j], buf, h_halves, h_state.ready)
            halve_next()
            ACT.wait(t)
            buf.free = ACT.done(nc.scalar.copy(pad[:, 2 * j:2 * j + 2, PAD:], buf.ap.rearrange("p (f t) -> p f t", f=2)))
            DVE.wait(buf.free)
            for c in (2 * j, 2 * j + 1):
                DVE.then(nc.vector.tensor_scalar(xr[:, c, :], pad[:, c, 0:T], S("c_conv_w", c, 1),
                                                 S("c_conv_b", c, 1), ALU.mult, ALU.add))
                for tap in (1, 2, 3):
                    xr_ready[c] = DVE.then(nc.vector.scalar_tensor_tensor(
                        xr[:, c, :], pad[:, c, tap:tap + T], S("c_conv_w", tap * KD + c, 1),
                        xr[:, c, :], ALU.mult, ALU.add))
        padded_read = DVE.last()
        gate_branch(0)
        gelu_ready = [gelu(0)]
        wa, wx = (dense_ring[4 + m][:, 0:KD * P].rearrange("p (h d) -> p h d", h=KD) for m in range(2))
        dense_ready(PE, 4)
        dense_ready(PE, 5)
        ACT.wait(half_b, padded_read)
        tanh_ready = []
        for g in range(4):
            for m in range(2):
                buf = bank[(2 * g + m) % 4]
                PE.wait(buf.free)
                for f in range(2):
                    h = 2 * g + f
                    PE.wait(xr_ready[h])
                    ins = mm(buf.ap[:, f * T:(f + 1) * T], (wa, wx)[m][:, h, :], xr[:, h, :], start=True, stop=True)
                t = PE.done(ins)
                ACT.wait(t)
                for f in range(2):
                    h = 2 * g + f
                    t1 = ACT.done(nc.scalar.activation((ra, bx)[m][:, h, :], buf.ap[:, f * T:(f + 1) * T],
                                                       ACTF.Tanh, bias=cst[:, 4 + m, h:h + 1], scale=0.5))
                buf.free = t1
            tanh_ready.append(t1)
        dense_release(4, t)
        dense_release(5, t)
        pair_of = [slice(2 * g, 2 * g + 2) for g in range(4)]
        factor_ready = []

        def factors(g):
            q = pair_of[g]
            ACT.wait(tanh_ready[g])
            for h in (2 * g, 2 * g + 1):
                less = cst[:, 1, h:h + 1]
                ACT.done(nc.scalar.activation(hT[:, h, :], ra[:, h, :], ACTF.Tanh, bias=less, scale=less))
            ACT.wait(ACT.last())
            for h in (2 * g, 2 * g + 1):
                c = cst[:, 0, h:h + 1]
                t = ACT.done(nc.scalar.activation(ra[:, h, :], ra[:, h, :], ACTF.Exp, bias=c, scale=c))
            DVE.wait(tanh_ready[g])
            DVE.then(nc.vector.scalar_tensor_tensor(bx[:, q, :], bx[:, q, :], 1.0, xr[:, q, :], ALU.add, ALU.mult))
            DVE.wait(t)
            DVE.then(nc.vector.tensor_tensor(xr[:, q, :], ra[:, q, :], ra[:, q, :], ALU.mult))
            factor_ready.append(DVE.then(nc.vector.scalar_tensor_tensor(
                hT[:, q, :], xr[:, q, :], 1.0, hT[:, q, :], ALU.add, ALU.mult)))

        scanned = []

        def scans():
            for g in range(4):
                q = pair_of[g]
                ACT.wait(factor_ready[g])
                t = ACT.done(nc.scalar.activation(hT[:, q, :], hT[:, q, :], ACTF.Sqrt))
                DVE.wait(t)
                DVE.then(nc.vector.tensor_tensor(bx[:, q, :], bx[:, q, :], hT[:, q, :], ALU.mult))
                for h in (2 * g, 2 * g + 1):
                    t = DVE.done(nc.vector.tensor_tensor_scan(xr[:, h, :], ra[:, h, :], bx[:, h, :], 0.0, ALU.mult, ALU.add))
                scanned.append(t)
        gate_branch(1, lambda: (factors(0), factors(1)))
        gate_branch(2, lambda: (factors(2), factors(3)))
        gate_branch(3, scans)
        gelu_ready += [gelu(j) for j in (1, 2, 3)]
        DVE.wait(scanned[-1])
        tickets["h_halves_free"] = PE.last()
        ready = []
        for g in range(4):
            q = pair_of[g]
            DVE.wait(gelu_ready[g])
            t = DVE.done(nc.vector.tensor_tensor(gate[:, q, :], gate[:, q, :], xr[:, q, :], ALU.mult))
            ready += [halve(tuple(h[:, q, :] for h in h_halves), gate[:, q, :], t, tickets["h_halves_free"])] * 2
        halve_next()
        h_state.free = [DVE.last(), ACT.last()]
        project_to_x(lambda j: pairs[8 + j], ready, halve_next, 0.5)
        work_state.free = [PE.last(), DVE.last(), ACT.last()]

    def moe(layer):
        NG, NE = N_GROUPS, N_EXP
        at = [0]

        def wk(n):
            at[0] += n
            assert at[0] <= WORK_F
            return work[:, at[0] - n:at[0]]
        h_tok = wk(TT * D)
        xs = wk(KD * P).rearrange("p (k c) -> p k c", k=KD)
        y_slots = wk(D)
        silu_g = [wk(2 * P) for _ in range(2)]
        hid = [wk(2 * P) for _ in range(2)]
        hidT = [wk(2 * P) for _ in range(2)]
        pick = wk(TT * P)
        pick_g = wk(TT * P)
        spread = wk(T)
        lg = wk(TT * (NG + NE)).rearrange("p (a n) -> p a n", a=TT)
        posm, gates, chosen, tmp_e, one1 = (wk(TT * NE).rearrange("p (a n) -> p a n", a=TT) for _ in range(5))
        gmx = wk(TT * 8).rearrange("p (a n) -> p a n", a=TT)
        goh = wk(TT * NG).rearrange("p (a n) -> p a n", a=TT)
        flag = most_tokens[:, layer:layer + 1]
        for e in compute:
            e.wait(work_state.free)
        SP.wait(work_state.free)
        lend_to_experts()
        for s in range(RING - LENT, RING):
            expert_load(layer, 0, s)
        wr = w_route[layer]

        rms_norm(S("norm_ffn_g", layer * KD, KD))
        PE.wait(routers_loaded, bank[6].free)
        n = NG + NE
        for tt in range(TT):
            for k in range(KD):
                PE.wait(h_state.ready[k])
                ins = mm(bank[6].ap[:, tt * n:(tt + 1) * n], hT[:, k, tt * P:(tt + 1) * P], wr[:, k, :],
                         start=k == 0, stop=k == KD - 1)
        t = PE.done(ins)
        fetch_table(ACTF.Exp)
        DVE.wait(t)
        V = nc.vector
        bias = S("moe_b", layer * n, n).unsqueeze(1).to_broadcast([P, TT, n])
        bank[6].free = DVE.then(V.tensor_tensor(lg, bank[6].ap[:, 0:TT * n].rearrange("p (a n) -> p a n", a=TT), bias, ALU.add))

        def bc(ap, m):
            return ap.to_broadcast([P, TT, m])

        def first_max(dst, values, rank, m, mx, mi):
            DVE.then(V.tensor_reduce(mx, values, X, ALU.max))
            DVE.then(V.tensor_tensor(dst, values, bc(mx, m), ALU.is_equal))
            DVE.then(V.tensor_tensor(dst, dst, rank.unsqueeze(1).to_broadcast([P, TT, m]), ALU.mult))
            DVE.then(V.tensor_reduce(mi, dst, X, ALU.max))
            DVE.then(V.tensor_tensor(dst, dst, bc(mi, m), ALU.is_equal))

        g = lg[:, :, 0:NG]
        col = [gmx[:, :, i:i + 1] for i in range(8)]
        first_max(goh, g, C("rank_g"), NG, col[0], col[1])
        t = DVE.then(V.tensor_tensor(g, g, bc(col[0], NG), ALU.subtract))
        ACT.wait(t)
        t = ACT.done(nc.scalar.activation(g, g, ACTF.Exp))
        DVE.wait(t)
        DVE.then(V.tensor_reduce(col[2], g, X, ALU.add))
        DVE.then(V.reciprocal(col[2], col[2]))
        e4 = lg[:, :, NG:].rearrange("p a (g j) -> p a g j", g=NG)
        in_g = goh.unsqueeze(3).to_broadcast([P, TT, NG, PER_GROUP])
        DVE.then(V.tensor_scalar(tmp_e.rearrange("p a (g j) -> p a g j", g=NG), in_g, -1.0, -NEG, ALU.add, ALU.mult))
        for tt in range(TT):
            t = DVE.done(V.tensor_tensor(e4[:, tt], e4[:, tt], in_g[:, tt], ALU.mult))
        DVE.wait(t)
        ev = lg[:, :, NG:]
        DVE.then(V.tensor_tensor(ev, ev, tmp_e, ALU.add))
        first_max(one1, ev, C("rank_e"), NE, col[3], col[1])
        DVE.then(V.tensor_scalar(tmp_e, one1, 2 * NEG, None, ALU.mult))
        DVE.then(V.tensor_tensor(ev, ev, tmp_e, ALU.add))
        first_max(tmp_e, ev, C("rank_e"), NE, col[4], col[1])
        t = DVE.then(V.tensor_tensor(col[4], col[4], col[3], ALU.subtract))
        ACT.wait(t)
        t = ACT.done(nc.scalar.activation(col[4], col[4], ACTF.Exp))
        DVE.wait(t)
        h_done = transpose_block(lambda i: hT[:, i % KD, (i // KD) * P:(i // KD + 1) * P], h_tok, TT * KD, 1,
                                 engines=(ACT,))
        h_state.free = PE.last()
        chosen_ready = DVE.then(V.tensor_tensor(chosen, one1, tmp_e, ALU.add))
        PE.wait(chosen_ready, bank[7].free)
        B7 = bank[7].ap
        mm(B7[:, 0:NE], C("before"), chosen[:, 0, :], start=True, stop=True)
        mm(B7[:, NE:2 * NE], C("ones"), chosen[:, 0, :], start=True, stop=False)
        mm(B7[:, NE:2 * NE], C("before"), chosen[:, 1, :], start=False, stop=True)
        mm(B7[:, 2 * NE:3 * NE], C("ones"), chosen[:, 0, :], start=True, stop=False)
        ranked = PE.done(mm(B7[:, 2 * NE:3 * NE], C("ones"), chosen[:, 1, :], start=False, stop=True))
        DVE.then(V.tensor_scalar(col[5], col[4], 1.0, None, ALU.add))
        DVE.then(V.reciprocal(col[5], col[5]))
        DVE.then(V.tensor_tensor(col[5], col[5], col[2], ALU.mult))
        DVE.then(V.tensor_tensor(col[4], col[4], col[5], ALU.mult))
        DVE.then(V.tensor_tensor(gates, one1, bc(col[5], NE), ALU.mult))
        DVE.then(V.tensor_tensor(tmp_e, tmp_e, bc(col[4], NE), ALU.mult))
        DVE.then(V.tensor_tensor(gates, gates, tmp_e, ALU.add))
        DVE.wait(ranked)
        r2 = B7[:, 0:TT * NE].rearrange("p (a n) -> p a n", a=TT)
        DVE.then(V.scalar_tensor_tensor(posm, r2, 1.0, chosen, ALU.add, ALU.mult))
        DVE.then(V.tensor_scalar(posm, posm, -1.0, None, ALU.add))
        DVE.then(V.tensor_reduce(col[6][:, 0], B7[:, 2 * NE:3 * NE], X, ALU.max))
        flag_ready = DVE.then(V.tensor_copy(flag[:, 0:1], col[6][:, 0]))
        bank[7].free = flag_ready

        DVE.wait(h_done)
        ACT.wait(h_done)
        PE.wait(h_done)
        for b in bank:
            PE.wait(b.free)
            b.free = None
        start = [DVE.last(), ACT.last(), PE.last()]
        for e in compute:
            e.wait(start)
        iota = C("iota").unsqueeze(1).to_broadcast([P, QUAD, CAP])
        ends = {}

        def quad_body(quad, counts, release, before, lies=lambda pair, s: None):
            def matrix(pair, s):
                return lies(pair, s) or (expert_ring[s], pr.now(counts[s]))
            DVE.wait(before("pick", PE), before("pick_dve", DVE))
            es = bass.ds(quad * QUAD, QUAD)
            for tt in range(TT):
                slot_of = posm[:, tt, es].unsqueeze(2).to_broadcast([P, QUAD, CAP])
                gate_of = gates[:, tt, es].unsqueeze(2).to_broadcast([P, QUAD, CAP])
                d = pick[:, tt * P:(tt + 1) * P].rearrange("p (e c) -> p e c", e=QUAD)
                dg = pick_g[:, tt * P:(tt + 1) * P].rearrange("p (e c) -> p e c", e=QUAD)
                DVE.then(V.tensor_tensor(d, slot_of, iota, ALU.is_equal))
                picked = DVE.done(V.tensor_tensor(dg, d, gate_of, ALU.mult))
            ends["pick_dve"] = picked
            PE.wait(picked)
            xs_ready = []
            for k in range(KD):
                b = k // 4
                if k % 4 == 0:
                    PE.wait(before(f"bank{b}", DVE))
                for tt in range(TT):
                    ins = mm(bank[b].ap[:, (k % 4) * P:(k % 4 + 1) * P],
                             h_tok[:, tt * D + k * P:tt * D + (k + 1) * P],
                             pick[:, tt * P:(tt + 1) * P], start=tt == 0, stop=tt == TT - 1)
                if k % 4 == 3:
                    t = PE.done(ins)
                    e = (ACT, DVE)[b]
                    e.wait(t, before("xs", PE))
                    xs_ready.append(copy_out(e, xs.rearrange("p k c -> p (k c)")[:, (k - 3) * P:(k + 1) * P], bank[b].ap))
            PE.wait(before("bank5", DVE))
            for tt in range(TT):
                ins = nc.tensor.transpose(bank[5].ap[:, tt * P:(tt + 1) * P], pick_g[:, tt * P:(tt + 1) * P], C("ident"))
            t = ends["pick"] = PE.done(ins)
            ACT.wait(t, before("spread", PE))
            spread_ready = copy_out(ACT, spread, bank[5].ap[:, 0:T])
            PE.wait(xs_ready)
            for pair in range(2):
                b = bank[2 + pair]
                PE.wait(before(f"bank{2 + pair}", DVE))
                half = D_EXP // 2
                for m in range(2):
                    for x in range(2):
                        PE.wait(matrix(pair, 2 * m + x)[1])
                    for k in range(KD):
                        for x in range(2):
                            w = matrix(pair, 2 * m + x)[0].rearrange("p (k n) -> p k n", k=KD)
                            slots = xs[:, k, (2 * pair + x) * CAP:(2 * pair + x + 1) * CAP]
                            for hf in range(2):
                                c = (2 * x + hf) * CAP
                                ins = mm(b.ap[c:c + CAP, m * half:(m + 1) * half], slots,
                                         w[:, k, hf * half:(hf + 1) * half], start=k == 0, stop=k == KD - 1)
                    t = PE.done(ins)
                    for x in range(2):
                        release(quad * 2 + pair, 2 * m + x, t)
                if pair == 1:
                    ends["xs"] = t
                ACT.wait(t, before(f"silu{pair}", DVE))
                silu_ready = ACT.done(nc.scalar.activation(silu_g[pair], b.ap[:, 0:half], ACTF.Silu))
                DVE.wait(silu_ready, before(f"hid{pair}", PE))
                t = DVE.done(V.tensor_tensor(hid[pair], silu_g[pair], b.ap[:, half:], ALU.mult))
                ends[f"bank{2 + pair}"] = ends[f"silu{pair}"] = t
                PE.wait(t, before("bank4", DVE) if pair == 0 else hidT_ready)
                for q in range(2):
                    ins = nc.tensor.transpose(bank[4].ap[:, q * P:(q + 1) * P], hid[pair][:, q * P:(q + 1) * P], C("ident"))
                t = ends[f"hid{pair}"] = PE.done(ins)
                DVE.wait(t, before(f"hidT{pair}", PE))
                hidT_ready = copy_out(DVE, hidT[pair], bank[4].ap[:, 0:2 * P])
                PE.wait(hidT_ready, before("y_bank", ACT), before("y_bank_dve", DVE))
                for x in range(2):
                    PE.wait(pr.now(counts[4 + x]))
                for n in range(2):
                    for f in range(FE):
                        for x in range(2):
                            w = expert_ring[4 + x].rearrange("p (k n) -> p k n", k=FE)
                            c = (f % 2) * P + x * 2 * CAP + (f // 2) * CAP
                            r0 = (2 * pair + x) * CAP
                            ins = mm(bank[6 + n].ap[r0:r0 + CAP, :], hidT[pair][:, c:c + CAP],
                                     w[:, f, n * 512:(n + 1) * 512], start=f == 0, stop=f == FE - 1)
                t = ends[f"hidT{pair}"] = PE.done(ins)
                for x in range(2):
                    release(quad * 2 + pair, 4 + x, t)
            ACT.wait(t, before("y", PE))
            y_ready = [copy_out(ACT, y_slots[:, 0:512], bank[6].ap)]
            ends["y_bank"] = y_ready[0]
            DVE.wait(t, before("y", PE))
            y_ready.append(copy_out(DVE, y_slots[:, 512:1024], bank[7].ap))
            ends["y_bank_dve"] = y_ready[1]
            PE.wait(y_ready, spread_ready)
            x_ready = []
            for q, bn in enumerate((5, 0, 1, 4)):
                b = bank[bn]
                for j in range(2):
                    ins = mm(b.ap[:, j * T:(j + 1) * T], y_slots[:, (2 * q + j) * P:(2 * q + j + 1) * P], spread,
                             start=True, stop=True)
                t = PE.done(ins)
                DVE.wait(t, before("x_dve", DVE) if q == 0 else None)
                xsl = flat(xT)[:, q * 2 * T:(q + 1) * 2 * T]
                ends[f"bank{bn}"] = ends["x_dve"] = DVE.done(V.tensor_tensor(xsl, b.ap, xsl, ALU.add))
                x_ready.append(DVE.last())
            ends["y"] = ends["spread"] = t
            return x_ready

        DVE.wait(x_state.ready)
        last_extra = {}

        def load_first(pair, s, t):
            if pair == 1 and s < len(EXTRA):
                last_extra[s] = t
                return
            SP.wait(t)
            expert_load(layer, 2 if s < len(EXTRA) else pair + 1, s)
        quad_body(0, exp_count, load_first, lambda name, e: None,
                  lambda pair, s: (extra[s], pr.now(extra_count[s])) if pair == 1 and s < len(EXTRA) else None)
        with pr.loop(f"quads{layer}", QUADS - 2, ends, compute) as lp:
            def load_next(pair, s, t):
                SP.wait(t)
                expert_load(layer, pair + 1, s)
            prior = dict(ends)
            quad_body(lp.i + 1, exp_count, load_next, lambda name, e: prior.get(name))
        closed = dict(ends)

        def load_last(pair, s, t):
            if pair == 2 * QUADS - 2:
                load_next(pair, s, t)
        x_ready = quad_body(QUADS - 1, exp_count, load_last, lambda name, e: closed[name])

        SP.wait(list(last_extra.values()))
        for s in range(RING):
            dense_load(s, slot_queue[s].pop(0))
        held_back.clear()
        next_moe[0] += 1

        def more(tag, above, passes):
            for e in pr.engines:
                e.wait(flag_ready, PE.last(), ACT.last(), DVE.last())
            most = nc.values_load(flag[0:1, 0:1], min_val=0, max_val=T)
            keep = [(e, e.count, dict(e.seen)) for e in pr.engines]
            with nc.If(most > above):
                for e in pr.engines:
                    e.count = pr.counter(f"{e.name}_{tag}{layer}")
                counts = [pr.counter(f"expert{s}_{tag}{layer}", 16) for s in range(RING)]

                def one_pass():
                    DVE.then(V.tensor_scalar(posm, posm, -float(CAP), None, ALU.add))
                    DVE.step()
                    with pr.loop(f"quads_{tag}{layer}", QUADS) as lq:
                        for s in range(RING):
                            expert_load(layer, lq.i * 2, s, counts)

                        def load_second(pair, s, t):
                            if len(seconds) < RING:
                                seconds.append(s)
                                SP.wait(t)
                                expert_load(layer, pair + 1, s, counts)
                        seconds = []
                        quad_body(lq.i, counts, load_second, lambda name, e: None)
                        turn = [PE.last(), ACT.last(), DVE.last()]
                        for e in (PE, ACT, DVE, SP):
                            e.wait(turn)
                            e.step()
                if passes == 1:
                    one_pass()
                else:
                    with pr.loop(f"passes_{tag}{layer}", passes):
                        one_pass()
            for e, c, seen in keep:
                e.count, e.seen = c, seen
        more("more", CAP, 1)
        more("rest", 2 * CAP, T // CAP - 2)
        x_state.ready = x_ready
        if layer == 0:
            for s in range(RING - LENT):
                expert_load(1, 0, s)
        for b in bank:
            b.free = DVE.last()
        work_state.free = [PE.last(), DVE.last(), ACT.last()]

    silu_f = [work[:, i * GF * T:(i + 1) * GF * T] for i in range(2)]
    hid_f = [work[:, (2 + i) * GF * T:(3 + i) * GF * T] for i in range(2)]

    def ffn_loader(layer, which):
        gu, dn = (w[layer] for w in ffn_w[which])

        def load_group(ahead, base=0):
            def go(s, t):
                SP.wait(t)
                g = base + ahead
                m = s % 3
                dense_load(s, rows(dn, g) if m == 2 else cols_at(gu, g, 0 if m == 0 else D_FF))
            return go
        return load_group

    def ffn(layer, which, gain):
        load_group = ffn_loader(layer, which)
        pairs, halve_next = halving([0])
        rms_norm(gain, h_halves, lambda: pairs.append(halve_chunk(1, None, tiles=(0,))))
        halve_chunk(1, load_group(2), tiles=(1,), i=pairs[1])
        for e in compute:
            e.wait(work_state.free)
        acc = [bank[4 + q] for q in range(4)]
        for b in acc:
            PE.wait(b.free)
            mm(b.ap, zeros[:, 0:P], zeros[:, :], start=True, stop=False, skip_group_check=True)
        for par in range(2):
            tickets[f"gate_bank{par}"], tickets[f"up_bank{par}"] = bank[2 * par].free, bank[2 * par + 1].free
            tickets[f"hid_free{par}"] = tickets[f"hid_ready{par}"] = None

        def gate(par, i):
            b = bank[2 * par]
            b.free = tickets[f"gate_bank{par}"]
            return tile_products(i, b, h_halves, h_state.ready)

        def silu(par, t):
            ACT.wait(t, tickets[f"up_bank{par}"])
            t = ACT.done(nc.scalar.activation(silu_f[par], bank[2 * par].ap, ACTF.Silu))
            tickets[f"gate_bank{par}"] = t

        def up(par, i):
            b = bank[2 * par + 1]
            b.free = tickets[f"up_bank{par}"]
            return tile_products(i, b, h_halves, h_state.ready)

        def hidden(par, t):
            DVE.wait(t, tickets[f"gate_bank{par}"], tickets[f"hid_ready{par}"])
            t = tickets[f"up_bank{par}"] = DVE.done(nc.vector.tensor_tensor(
                hid_f[par], silu_f[par], bank[2 * par + 1].ap, ALU.mult))
            tickets[f"hid_ready{par}"] = halve(hid_halves[par], hid_f[par], t,
                                               tickets[f"hid_free{par}"])

        def down(par, i, last=False):
            w = halved(i)
            PE.wait(tickets[f"hid_ready{par}"])
            order = [(f, k) for f in range(GF) for k in range(KD)]
            if last:
                order = [(f, k) for q in range(4) for f in range(GF) for k in (2 * q, 2 * q + 1)]
                PE.wait(tickets[f"w_ready{i}1"])
            for n, (f, k) in enumerate(order):
                PE.wait(tickets[f"w_ready{i}{f}"])
                ins = products(acc[k // 2].ap[:, (k % 2) * T:(k % 2 + 1) * T],
                               tuple(v[:, f, k, :] for v in w),
                               tuple(h[:, f * T:(f + 1) * T] for h in hid_halves[par]),
                               False, False, skip_group_check=True)
                if last and n % 4 == 3:
                    add_group(n // 4, PE.done(ins))
                elif not last and k == KD - 1:
                    tickets[f"w_free{i}{f}"] = PE.done(ins)
            if last:
                tickets[f"w_free{i}0"] = tickets[f"w_free{i}1"] = PE.last()
            tickets[f"hid_free{par}"] = PE.last()

        def add_group(q, t):
            xsl = flat(xT)[:, q * 2 * T:(q + 1) * 2 * T]
            DVE.wait(t)
            acc[q].free = x_state.ready[q] = DVE.done(nc.vector.scalar_tensor_tensor(
                xsl, acc[q].ap, 0.5, xsl, ALU.mult, ALU.add))
            if q:
                x_complete[0](q - 1)

        t = gate(0, pairs[0])
        silu(0, t)
        t = up(0, pairs[1])
        g1 = halve_chunk(3, load_group(3))
        hidden(0, t)
        u1 = halve_chunk(4, load_group(3))

        def turn(g1, u1, base, release):
            t = gate(1, g1)
            d0 = halve_chunk(2, release(2), True)
            silu(1, t)
            t = up(1, u1)
            g2 = halve_chunk(0, release(4))
            hidden(1, t)
            down(0, d0)
            u2 = halve_chunk(1, release(4))
            t = gate(0, g2)
            d1 = halve_chunk(5, release(3), True)
            silu(0, t)
            t = up(0, u2)
            g3 = halve_chunk(3, release(5)) if base is not None else None
            hidden(0, t)
            if base is None:
                d2 = halve_chunk(2, release(0), True)
            down(1, d1)
            if base is None:
                halve_next()
                for par in range(2):
                    bank[2 * par].free, bank[2 * par + 1].free = tickets[f"gate_bank{par}"], tickets[f"up_bank{par}"]
                work_state.free = [PE.last(), DVE.last(), ACT.last()]
                down(0, d2, last=True)
                x_complete[0](3)
                return
            return g3, halve_chunk(4, release(5))

        turns = (N_GRP - 1) // 2
        with pr.loop(f"ffn{layer}{which}", turns - 2, tickets, compute) as lp:
            assert turn(g1, u1, lp.i * 2, lambda ahead: load_group(ahead, lp.i * 2)) == (g1, u1)
        static = lambda ahead: dense_release
        turn(g1, u1, 0, static)
        turn(g1, u1, None, static)
        tickets["h_halves_free"] = PE.last()
        work_state.free = [PE.last(), DVE.last(), ACT.last()]

    def mixer2(layer):
        V = nc.vector
        pairs, halve_next = halving([j % RING for j in range(13)] + [0, 1, 2, 3])
        rms_norm(S("ln_mix_2", layer * KD, KD), h_halves)
        halve_next()
        for e in (PE, ACT, DVE, POOL):
            e.wait(work_state.free)
        at = {"scratch": 0, "work": 0}

        def wk(n, where="scratch"):
            at[where] += n
            return (scratch if where == "scratch" else work)[:, at[where] - n:at[where]]
        U = N_HEADS
        L = T + EDGE

        def of_tokens(m):
            return m[:, 0:TT * U * HD].rearrange("p (a u c) -> p a u c", a=TT, u=U)
        heads = wk(2 * TT * U * HD)
        qk = of_tokens(heads)
        qkT = heads[:, TT * U * HD:].rearrange("p (j t) -> p j t", j=U // 2)
        merged = heads[:, 0:KD * T].rearrange("p (k t) -> p k t", k=KD)
        windows = wk(3 * 4 * L)
        uT, s2, s4 = (windows[:, i * 4 * L:(i + 1) * 4 * L].rearrange("p (g t) -> p g t", g=4) for i in range(3))
        pT = windows[:, 0:N_Q * 3 * P]
        sig = wk(16 * T).rearrange("p (k t) -> p k t", k=16)
        p1 = wk(N_Q * 2 * P, "work")
        sq = of_tokens(p1)
        prob = [wk(N_Q * P, "work").rearrange("p (h k) -> p h k", h=N_Q), p1.rearrange("p (h k) -> p h k", h=N_Q)]
        poolT = wk(4 * T, "work").rearrange("p (g t) -> p g t", g=4)
        poolY = wk(4 * T, "work").rearrange("p (g t) -> p g t", g=4)
        oT = wk(4 * T, "work").rearrange("p (j t) -> p j t", j=4)
        v_tok = wk(TT * P, "work").rearrange("p (a c) -> p a c", a=TT)
        small_q = wk(2 * TT * U + 64 + 4 * TT * U * (ROT // 2), "work")
        assert at["scratch"] <= SCRATCH_F and at["work"] <= WORK_F
        ms = small_q[:, 0:TT * U].rearrange("p (a u) -> p a u", a=TT)
        half = ROT // 2
        rt = [small_q[:, 104 + i * TT * U * half:104 + (i + 1) * TT * U * half].rearrange(
            "p (a u c) -> p a u c", a=TT, u=U) for i in range(4)]
        stat = small_q[:, TT * U:TT * U + 64]

        got = {}

        def qkv_out(j, t):
            buf = bank[1 + j]
            ACT.wait(t)
            for tt in range(TT):
                src = buf.ap[:, tt * CHUNK:(tt + 1) * CHUNK]
                if j < 2:
                    dst = qk[:, tt, 0:N_Q, :].rearrange("p (i g) c -> p i g c", g=2)[:, :, j, :]
                    buf.free = ACT.done(nc.scalar.copy(dst, src.rearrange("p (i c) -> p i c", i=4)))
                else:
                    ACT.done(nc.scalar.copy(qk[:, tt, N_Q:U, :].rearrange("p u c -> p (u c)"), src[:, 0:P]))
                    buf.free = ACT.done(nc.scalar.copy(v_tok[:, tt, :], src[:, P:2 * P]))

        def head_norm_rope():
            ACT.wait(ACT.last())
            DVE.wait(ACT.last())
            qf = qk.rearrange("p a u c -> p (a u) c")
            sf = sq.rearrange("p a u c -> p (a u) c")
            mf = ms.rearrange("p a u -> p (a u)")
            t = ACT.done(nc.scalar.activation(sf, qf, ACTF.Square))
            DVE.wait(t)
            DVE.then(V.tensor_reduce(mf, sf, X, ALU.add))
            t = DVE.then(V.tensor_scalar(mf, mf, 1.0 / HD, EPS, ALU.mult, ALU.add))
            ACT.wait(t)
            t = ACT.done(nc.scalar.activation(mf, mf, ACTF.Sqrt))
            yield
            DVE.wait(t)
            DVE.then(V.reciprocal(mf, mf))
            t = DVE.done(V.tensor_tensor(qf, qf, mf.unsqueeze(2).to_broadcast([P, TT * U, HD]), ALU.mult))
            yield
            DVE.wait(t)
            for tt in range(TT):
                for (u0, u1, g) in ((0, N_Q, "q_norm_2"), (N_Q, U, "k_norm_2")):
                    gain = S(g, layer * HD, HD).unsqueeze(1).to_broadcast([P, u1 - u0, HD])
                    t = DVE.done(V.tensor_tensor(qk[:, tt, u0:u1, :], qk[:, tt, u0:u1, :], gain, ALU.mult))
            yield
            DVE.wait(t)
            x1, x2 = qk[:, :, :, 0:half], qk[:, :, :, half:ROT]
            for tt in range(TT):
                c, s = (C(n)[:, tt * half:(tt + 1) * half].unsqueeze(1).to_broadcast([P, U, half]) for n in ("cos", "sin"))
                for i, (x, f) in enumerate(((x1, c), (x2, s), (x2, c), (x1, s))):
                    t = DVE.done(V.tensor_tensor(rt[i][:, tt], x[:, tt], f, ALU.mult))
            DVE.wait(t)
            for tt in range(TT):
                DVE.done(V.tensor_tensor(x1[:, tt], rt[0][:, tt], rt[1][:, tt], ALU.subtract))
                t = DVE.done(V.tensor_tensor(x2[:, tt], rt[2][:, tt], rt[3][:, tt], ALU.add))
            got["rope"] = t

        def heads_to_features():
            PE.wait(got["rope"])
            for tt in range(TT):
                for j0, j1 in ((0, 4), (4, 5)):
                    buf = bank[1 + 2 * tt + j0 // 4]
                    PE.wait(buf.free)
                    for j in range(j0, j1):
                        ins = nc.tensor.transpose(buf.ap[:, (j - j0) * P:(j - j0 + 1) * P],
                                                  qk[:, tt, 2 * j:2 * j + 2, :].rearrange("p g c -> p (g c)"), C("ident"))
                    t = PE.done(ins)
                    ACT.wait(t)
                    buf.free = copy_out(ACT, qkT[:, j0:j1, tt * P:(tt + 1) * P],
                                        buf.ap[:, 0:(j1 - j0) * P].rearrange("p (j t) -> p j t", t=P))
            return ACT.last()

        def scores():
            PE.wait(got["qkT"])
            for b in (0, 1, 2, 3, 4, 5):
                PE.wait(bank[b].free)
            for j in range(4):
                for g in range(2):
                    r = slice(g * HD, (g + 1) * HD)
                    b1 = bank[2 * g + j // 2].ap
                    mm(b1[:, (j % 2) * 2 * P:(j % 2 + 1) * 2 * P], qkT[r, j, P:2 * P], qkT[r, 4, :],
                       start=True, stop=True)
                    ins = mm(bank[4 + g].ap[:, j * P:(j + 1) * P], qkT[r, j, 0:P], qkT[r, 4, 0:P],
                             start=True, stop=True)
            return PE.done(ins)

        def softmax(blk):
            nm, mx, sk, sm = stat[:, 0:8], stat[:, 8:16], stat[:, 16:24], stat[:, 24:32]
            w = (1 + blk) * P
            pb = prob[blk]
            band = C("band")[:, 2 * P - w:2 * P]
            DVE.wait(got["scores"])
            for q in range(4 if blk else 2):
                nh = 2 if blk else 4
                src = bank[q if blk else 4 + q]
                part = pb[:, q * nh:(q + 1) * nh, :]
                src.free = DVE.done(V.scalar_tensor_tensor(
                    part, src.ap.rearrange("p (h k) -> p h k", h=nh), HD ** -0.5,
                    band.unsqueeze(1).to_broadcast([P, nh, w]), ALU.mult, ALU.add))
            DVE.wait(src.free)
            yield
            DVE.then(V.tensor_reduce(mx, pb, X, ALU.max))
            sink = S("sinks_2", layer * N_Q, N_Q)
            DVE.then(V.tensor_tensor(mx, mx, sink, ALU.max))
            DVE.then(V.tensor_scalar(nm, mx, -1.0, None, ALU.mult))
            t = DVE.then(V.tensor_tensor(sk, sink, mx, ALU.subtract))
            ACT.wait(t)
            for h in range(N_Q):
                ACT.done(nc.scalar.activation(pb[:, h, :], pb[:, h, :], ACTF.Exp, bias=nm[:, h:h + 1],
                                              accum_out=sm[:, h:h + 1]))
            t = ACT.done(nc.scalar.activation(sk, sk, ACTF.Exp))
            yield
            DVE.wait(t)
            DVE.then(V.tensor_tensor(sm, sm, sk, ALU.add))
            DVE.then(V.reciprocal(sm, sm))
            got["prob", blk] = DVE.then(V.tensor_tensor(pb, pb, sm.unsqueeze(2).to_broadcast([P, N_Q, w]), ALU.mult))

        def pooling():
            G = nc.gpsimd
            POOL.wait(u_ready)
            src, dst = uT, s2
            for n, w in enumerate(WINDOWS):
                sh = w // 2
                POOL.then(G.tensor_tensor(dst[:, n:, EDGE:L], src[:, n:, EDGE:L], src[:, n:, EDGE - sh:L - sh], ALU.add))
                POOL.done(G.tensor_scalar(poolT[:, n, EDGE:], dst[:, n, 2 * EDGE:L], 1.0 / w, None, ALU.mult))
                POOL.then(G.tensor_tensor(poolT[:, n, 0:EDGE], dst[:, n, EDGE:2 * EDGE],
                                          C("rcount")[:, n * EDGE:(n + 1) * EDGE], ALU.mult))
                t = POOL.then(G.tensor_tensor(poolT[:, n, :], poolT[:, n, :], uT[:, n, EDGE:L], ALU.subtract))
                src, dst = dst, (s4 if dst is s2 else s2)
            return t

        for buf in (uT, s2, s4):
            t = POOL.done(nc.gpsimd.memset(buf[:, :, 0:EDGE], 0.0))
        POOL.wait(t)
        ACT.wait(t)

        def attention():
            yield from head_norm_rope()
            yield
            got["qkT"] = heads_to_features()
            yield
            got["scores"] = scores()
            for blk in (1, 0):
                yield from softmax(blk)
                yield

        def pool_products():
            dense_ready(PE, 13 % RING)
            wp = dense_ring[13 % RING][:, 0:4 * P].rearrange("p (g d) -> p g d", g=4)
            PE.wait(got["pool"], bank[0].free, bank[1].free)
            for g in range(4):
                ins = mm(bank[g // 2].ap[:, (g % 2) * T:(g % 2 + 1) * T], wp[:, g, :], poolT[:, g, :], start=True, stop=True)
            t = PE.done(ins)
            dense_release(13 % RING, t)
            DVE.wait(t)
            for g in range(4):
                b = bank[g // 2]
                b.free = DVE.done(V.tensor_scalar(poolY[:, g, :], b.ap[:, (g % 2) * T:(g % 2 + 1) * T],
                                                  S("pool_scale_2", layer * 4 + g, 1), None, ALU.mult))
            return DVE.last()

        pieces = attention()
        n_in = 13
        for j in range(n_in):
            if j < 3:
                t = token_products(pairs[j], bank[1 + j])
            else:
                buf = bank[6 + j % 2]
                t = tile_products(pairs[j], buf, h_halves, h_state.ready)
            if j + 2 < n_in:
                halve_next()
            if j < 3:
                qkv_out(j, t)
                continue
            ACT.wait(t)
            src = buf.ap.rearrange("p (f t) -> p f t", f=2)
            if j < 5:
                buf.free = ACT.done(nc.scalar.copy(uT[:, 2 * (j - 3):2 * (j - 3) + 2, EDGE:], src))
            else:
                c = 2 * (j - 5)
                buf.free = ACT.done(nc.scalar.activation(sig[:, c:c + 2, :], src, ACTF.Tanh, scale=0.5))
            if j == 4:
                u_ready = ACT.last()
                got["pool"] = pooling()
            next(pieces, None)
            if j == n_in - 2:
                got["poolY"] = pool_products()
        sig_ready = ACT.last()
        halves_free = PE.last()

        def branch(br, rhs, rhs_ready):
            PE.wait(rhs_ready)
            merges = []
            for c in range(2):
                s = (14 + 2 * br + c) % RING
                dense_ready(PE, s)
                w = dense_ring[s][:, :].rearrange("p (j n) -> p j n", j=4)
                for q in range(2):
                    buf = bank[(br * 4 + c * 2 + q + 2) % 8]
                    PE.wait(buf.free)
                    for f in range(2):
                        for k in range(4):
                            ins = mm(buf.ap[:, f * T:(f + 1) * T], w[:, k, (2 * q + f) * P:(2 * q + f + 1) * P],
                                     rhs[:, k, :], start=k == 0, stop=k == 3)
                    merges.append(lambda buf=buf, k0=c * 4 + 2 * q, t=PE.done(ins): merge(br, buf, k0, t))
                dense_release(s, PE.last())
            return merges

        def merge(br, buf, k0, t):
            DVE.wait(t, sig_ready)
            src = buf.ap.rearrange("p (f t) -> p f t", f=2)
            dst = merged[:, k0:k0 + 2, :] if br == 0 else sig[:, 8 + k0:8 + k0 + 2, :]
            buf.free = DVE.then(V.scalar_tensor_tensor(dst, sig[:, br * 8 + k0:br * 8 + k0 + 2, :], 1.0,
                                                       src, ALU.add, ALU.mult))
            if br == 1:
                m = merged[:, k0:k0 + 2, :]
                t = DVE.done(V.tensor_tensor(m, m, dst, ALU.add))
                got["m", k0] = got["m", k0 + 1] = halve(tuple(h[:, k0:k0 + 2, :] for h in h_halves), m, t, halves_free)
        merges = branch(0, poolY, got["poolY"])
        for _ in pieces:
            pass
        for step in merges:
            step()
        PE.wait(got["prob", 0], got["prob", 1])
        srcs = [(0, h, 0) for h in range(N_Q)] + [(1, h, kb) for h in range(N_Q) for kb in range(2)]
        p_done = transpose_block(lambda i: prob[srcs[i][0]][:, srcs[i][1], srcs[i][2] * P:(srcs[i][2] + 1) * P],
                                 pT, 3 * N_Q, 0)
        PE.wait(p_done)
        DVE.wait(DVE.last())

        def pT_of(blk, h, kb):
            i = h if blk == 0 else N_Q + 2 * h + kb
            return pT[:, i * P:(i + 1) * P]
        PE.wait(bank[6].free, bank[7].free)
        for j in range(4):
            for g in range(2):
                h = g * 4 + j
                o = bank[6 + j // 2].ap[g * HD:(g + 1) * HD, (j % 2) * T:(j % 2 + 1) * T]
                mm(o[:, 0:P], v_tok[:, 0, g * HD:(g + 1) * HD], pT_of(0, h, 0), start=True, stop=True)
                mm(o[:, P:2 * P], v_tok[:, 0, g * HD:(g + 1) * HD], pT_of(1, h, 0), start=True, stop=False)
                ins = mm(o[:, P:2 * P], v_tok[:, 1, g * HD:(g + 1) * HD], pT_of(1, h, 1), start=False, stop=True)
        t = PE.done(ins)
        ACT.wait(t)
        for q in range(2):
            bank[6 + q].free = ACT.done(nc.scalar.copy(
                oT[:, 2 * q:2 * q + 2, :], bank[6 + q].ap.rearrange("p (j t) -> p j t", j=2)))
        merges = branch(1, oT, ACT.last())
        halve_next()
        halve_next()
        for step in merges:
            step()
        project_to_x(lambda j: pairs[13 + j], [got["m", k] for k in range(KD)], halve_next, 0.5)
        tickets["h_halves_free"] = PE.last()
        work_state.free = [PE.last(), DVE.last(), ACT.last()]

    o_tok = work[:, 0:TT * D].rearrange("p (a d) -> p a d", a=TT)
    put = []

    def put_out(q):
        e = (ACT, DVE)[q % 2]
        e.wait(work_state.free)
        buf = bank[q]
        PE.wait(x_state.ready[q], buf.free)
        for tt in range(TT):
            for k in range(2):
                ins = nc.tensor.transpose(buf.ap[:, (2 * tt + k) * P:(2 * tt + k + 1) * P],
                                          xT[:, 2 * q + k, tt * P:(tt + 1) * P], C("ident"))
        e.wait(PE.done(ins))
        buf.free = copy_out(e, o_tok[:, :, q * 2 * P:(q + 1) * 2 * P], buf.ap.rearrange("p (a d) -> p a d", a=TT))
        put.append(buf.free)
        if q % 2:
            SP.wait(put)
            half_d = slice((q - 1) * 2 * P, (q + 1) * 2 * P)
            load("out", out.rearrange("(a p) d -> p a d", p=P)[:, :, half_d], o_tok[:, :, half_d])

    def finish():
        for q in range(len(put), 4):
            put_out(q)
        SP.wait(pr.now(once["out"]))
        for s in range(RING):
            SP.wait(pr.now(slot_count[s]), pr.now(exp_count[s]))
        SP.wait([pr.now(c) for c in extra_count])

    def stages():
        yield "ab", mixer_ab
        yield "moe0", lambda: moe(0)
        yield "rglru", mixer_rglru
        yield "moe1", lambda: moe(1)
        yield "final", final_of_block1
        for layer in range(2):
            yield f"ffn1_{layer}", lambda layer=layer: ffn(layer, 0, S("ln_ffn1_2", layer * KD, KD))
            yield f"mix_{layer}", lambda layer=layer: mixer2(layer)
            yield f"ffn2_{layer}", lambda layer=layer: ffn(layer, 1, S("ln_ffn2_2", layer * KD, KD))

    def final_of_block1():
        nonlocal scratch
        scratch = lend_to_block2()
        open_halves()
        halving([])[1]()
        rms_norm(S("norm_final_g"))
        x_state.ready = []
        for q in range(4):
            DVE.wait(h_state.ready[2 * q + 1])
            x_state.ready.append(DVE.done(nc.vector.tensor_copy(xT[:, 2 * q:2 * q + 2, :], hT[:, 2 * q:2 * q + 2, :])))
        h_state.free = DVE.last()

    plan = list(stages())
    for n, (name, stage) in enumerate(plan):
        following = plan[n + 1][0] if n + 1 < len(plan) and name != upto else ""
        if name == "final":
            following = name if name == upto else "ffn1_0"
        release = dense_release
        if following.startswith("ffn"):
            release = ffn_loader(int(following[-1]), 0 if following.startswith("ffn1") else 1)(2)
        here = following.startswith(("ffn", "mix"))
        halve_for_next[0] = (lambda release=release: halve_chunk(0, release)) if here else None
        last = name == upto or n + 1 == len(plan)
        x_complete[0] = put_out if last else square_and_sum
        stage()
        if last:
            break
    finish()
    return pr.new_rates, pr.new_marks


WEIGHTS = ["a_ws", "ab_w_in", "ab_w_out", "c_w_in", "c_w_a", "c_w_x", "c_w_out", "moe_w_rg", "moe_w_re",
           "moe_w_gate", "moe_w_up", "moe_w_down", "w_ffn1_gu_2", "w_ffn1_down_2", "w_in_2", "pool_w_2",
           "w_pool_branch_2", "w_attn_branch_2", "w_out_2", "w_ffn2_gu_2", "w_ffn2_down_2"]


def lay_out(inputs):
    f = lambda n: np.asarray(inputs[n])
    col = lambda v: np.moveaxis(v.reshape(*v.shape[:-1], v.shape[-1] // P, P), -1, 0).reshape(P, -1)
    row = lambda v: np.broadcast_to(v.reshape(1, -1), (P, v.size))
    parts = [col(f(n)) for n in ("norm_mix_g", "norm_ffn_g", "norm_final_g", "b_conv_w", "c_conv_w", "c_conv_b",
                                 "c_b_a", "c_b_x", "c_lambda", "ln_ffn1_2", "ln_mix_2", "ln_ffn2_2", "pool_scale_2")]
    moe_b = np.concatenate([f("moe_b_rg"), f("moe_b_re")], axis=1)
    parts += [row(v) for v in (f("a_ln_g"), f("a_ws_b"), moe_b, f("q_norm_2"), f("k_norm_2"), f("sinks_2"))]
    small = np.ascontiguousarray(np.concatenate(parts, axis=1))
    arrays = {"x": f("x").reshape(T, D), "consts": constant_table()[1], "small": small}
    for n in WEIGHTS:
        v = f(n)
        if n.startswith(("a_", "ab_", "c_")):
            v = v[0]
        elif n.startswith(("moe_w_gate", "moe_w_up", "moe_w_down")):
            v = v.reshape(2 * N_EXP, *v.shape[2:])
        arrays[n] = v
    return {n: np.ascontiguousarray(v) for n, v in arrays.items()}


def make(arrays, new_core, upto=None):
    counts = ({}, {})
    for _ in range(2):
        nc = new_core()
        aps = {n: nc.dram_tensor("in_" + n, v.shape, mybir.dt.from_np(v.dtype), kind="ExternalInput").ap()
               for n, v in arrays.items()}
        out = nc.dram_tensor("out", (T, D), F32, kind="ExternalOutput").ap()
        counts = build(nc, aps, out, *counts, upto=upto)
    return nc


def kernel(**inputs):
    import concourse.bacc as bacc
    from concourse.bass_utils import run_bass_kernel_spmd
    arrays = lay_out(inputs)
    nc = make(arrays, lambda: bacc.Bacc("TRN2", target_bir_lowering=False, num_devices=1))
    r = run_bass_kernel_spmd(nc, [{"in_" + n: v for n, v in arrays.items()}], core_ids=[0])
    return r.results[0]["out"].reshape(1, T, D)
```
